# Optimizing a Trainium2 kernel written in Bass

```python
import math
import jax, jax.numpy as jnp
from jax import lax
import numpy as np
import jax
import jax.numpy as jnp

D_MODEL = 1024
BATCH = 1
SEQ = 256
DEPTH = 2

MOBA_HEAD_DIM = 128
MOBA_HEADS = D_MODEL // (2 * MOBA_HEAD_DIM)
MOBA_BLOCK = 256
MOBA_TOPK = 3
MOBA_QBLOCK = 32
GLA_DV = 128
GLA_HEADS = D_MODEL // (2 * GLA_DV)
GLA_DK = GLA_DV // 2
GLA_GATE_RANK = 16
GLA_GATE_NORM = 16.0
GLA_CHUNK = 64
GDN_DK = 128
GDN_DV = 128
GDN_HEADS = D_MODEL // GDN_DV
GDN_CONV = 4
GDN_CHUNK = 64
RPE_BUCKETS = 32
RPE_MAX_DIST = 2048
N_EXPERTS = 64
TOP_K = 6
N_GROUPS = 8
TOPK_GROUPS = 4
D_EXPERT = 256
D_SHARED = 256
ROUTED_SCALE = 2.5
MOE_BLOCK = 128
DEEPNORM_ALPHA = float((2 * DEPTH) ** 0.25)
DEEPNORM_BETA = float((8 * DEPTH) ** -0.25)
LN_EPS = 1e-5
NORM_EPS = 1e-6
N_EVEN = (DEPTH + 1) // 2
N_ODD = DEPTH // 2

MOBA_W = MOBA_HEADS * MOBA_HEAD_DIM
GLA_QK_W = GLA_HEADS * GLA_DK
GLA_V_W = GLA_HEADS * GLA_DV
EVEN_SPLITS = (MOBA_W, MOBA_W, MOBA_W, GLA_QK_W, GLA_QK_W, GLA_V_W, GLA_V_W, GLA_GATE_RANK)
EVEN_IN = sum(EVEN_SPLITS)
EVEN_MIX = MOBA_W + GLA_V_W
GDN_QK_W = GDN_HEADS * GDN_DK
GDN_V_W = GDN_HEADS * GDN_DV
GDN_QKV_W = 2 * GDN_QK_W + GDN_V_W
ODD_SPLITS = (GDN_QK_W, GDN_QK_W, GDN_V_W, GDN_V_W, GDN_HEADS, GDN_HEADS)
ODD_IN = sum(ODD_SPLITS)
ODD_MIX = GDN_V_W


F32 = jnp.float32

def _split(t, sizes):
    return jnp.split(t, np.cumsum(sizes)[:-1].tolist(), axis=-1)

def layer_norm(x, g, b):
    xf = x.astype(F32)
    mu = jnp.mean(xf, -1, keepdims=True)
    var = jnp.mean(jnp.square(xf - mu), -1, keepdims=True)
    return ((xf - mu) * lax.rsqrt(var + LN_EPS)).astype(x.dtype) * g + b

def l2norm(t):
    tf = t.astype(F32)
    return tf * lax.rsqrt(jnp.sum(tf * tf, -1, keepdims=True) + NORM_EPS)

def gated_rmsnorm(o, gate, w):
    of = o.astype(F32)
    of = of * lax.rsqrt(jnp.mean(of * of, -1, keepdims=True) + NORM_EPS)
    return of * w.astype(F32) * jax.nn.silu(gate.astype(F32))

def rpe_bucket(dist):
    exact = RPE_BUCKETS // 2
    d = jnp.maximum(dist, 0)
    logd = jnp.log(jnp.maximum(d, 1).astype(F32) / exact)
    large = exact + (logd / math.log(RPE_MAX_DIST / exact) * (RPE_BUCKETS - exact)).astype(jnp.int32)
    large = jnp.minimum(large, RPE_BUCKETS - 1)
    return jnp.where(d < exact, d, large)

def causal_dwconv(x, w):
    k = w.shape[0]
    return lax.conv_general_dilated(x, w[:, None, :], window_strides=(1,), padding=[(k - 1, 0)],
                                    dimension_numbers=('NWC', 'WIO', 'NWC'),
                                    feature_group_count=x.shape[-1])

def moba_attention(q, k, v, rpe_bias):
    B, S, H, Dh = q.shape
    nkb = -(-S // MOBA_BLOCK)
    nqb = S // MOBA_QBLOCK
    kk = min(MOBA_TOPK, nkb)
    pad = nkb * MOBA_BLOCK - S

    def blocks(t):
        t = jnp.pad(t, ((0, 0), (0, pad), (0, 0), (0, 0)))
        return t.reshape(B, nkb, MOBA_BLOCK, H, Dh).transpose(0, 3, 1, 2, 4)

    kb, vb = blocks(k), blocks(v)
    k_mean = jnp.mean(kb.astype(F32), axis=3)
    qb = q.reshape(B, nqb, MOBA_QBLOCK, H, Dh).transpose(1, 0, 3, 2, 4)
    rpe_hb = rpe_bias.T.astype(F32)
    scale = Dh ** -0.5
    b_idx = jnp.arange(B)[:, None, None, None]
    h_idx = jnp.arange(H)[None, :, None, None]
    offs = jnp.arange(MOBA_BLOCK)

    def one_block(args):
        qi, qblk = args
        q0 = qi * MOBA_QBLOCK
        qpos = q0 + jnp.arange(MOBA_QBLOCK)
        cur = q0 // MOBA_BLOCK
        gate = jnp.einsum('bhqd,bhnd->bhqn', qblk.astype(F32), k_mean)
        gate = jnp.where(jnp.arange(nkb) < cur, gate, -jnp.inf)
        _, sel = lax.top_k(gate, kk)
        valid = jnp.arange(kk) < cur
        k_sel = kb[b_idx, h_idx, sel]
        v_sel = vb[b_idx, h_idx, sel]
        kpos = sel[..., None] * MOBA_BLOCK + offs
        bias_sel = rpe_hb[h_idx[..., None], rpe_bucket(qpos[:, None, None] - kpos)]
        l_sel = jnp.einsum('bhqd,bhqrtd->bhqrt', qblk, k_sel).astype(F32) * scale + bias_sel
        l_sel = jnp.where(valid[:, None], l_sel, -jnp.inf)
        k_own = lax.dynamic_index_in_dim(kb, cur, axis=2, keepdims=False)
        v_own = lax.dynamic_index_in_dim(vb, cur, axis=2, keepdims=False)
        dist = qpos[:, None] - (cur * MOBA_BLOCK + offs)[None, :]
        l_own = jnp.einsum('bhqd,bhtd->bhqt', qblk, k_own).astype(F32) * scale + rpe_hb[:, rpe_bucket(dist)]
        l_own = jnp.where(dist >= 0, l_own, -jnp.inf)
        logits = jnp.concatenate([l_sel.reshape(B, H, MOBA_QBLOCK, kk * MOBA_BLOCK), l_own], axis=-1)
        p = jax.nn.softmax(logits, axis=-1).astype(v.dtype)
        p_sel = p[..., :kk * MOBA_BLOCK].reshape(B, H, MOBA_QBLOCK, kk, MOBA_BLOCK)
        p_own = p[..., kk * MOBA_BLOCK:]
        return (jnp.einsum('bhqrt,bhqrtd->bhqd', p_sel, v_sel)
                + jnp.einsum('bhqt,bhtd->bhqd', p_own, v_own))

    out = lax.map(one_block, (jnp.arange(nqb), qb))
    return out.transpose(1, 0, 3, 2, 4).reshape(B, S, H, Dh)

def gla_chunked(q, k, v, g):
    B, S, H, DK = q.shape
    DV = v.shape[-1]
    n = S // GLA_CHUNK

    def chunks(t):
        return t.astype(F32).reshape(B, n, GLA_CHUNK, H, t.shape[-1]).transpose(1, 0, 3, 2, 4)

    qc = chunks(q) * DK ** -0.5
    kc, vc, gc = chunks(k), chunks(v), chunks(g)
    b = jnp.cumsum(gc, axis=3)
    b_last = b[:, :, :, -1:, :]
    q_e = qc * jnp.exp(b)
    k_e = kc * jnp.exp(-b)
    k_end = kc * jnp.exp(b_last - b)
    causal = jnp.tril(jnp.ones((GLA_CHUNK, GLA_CHUNK), F32))
    o_intra = jnp.einsum('nbhij,nbhjv->nbhiv', jnp.einsum('nbhid,nbhjd->nbhij', q_e, k_e) * causal, vc)

    def step(state, xs):
        q_i, k_i, v_i, d_i = xs
        o_i = jnp.einsum('bhid,bhdv->bhiv', q_i, state)
        state = state * d_i[..., None] + jnp.einsum('bhjd,bhjv->bhdv', k_i, v_i)
        return state, o_i

    s0 = jnp.zeros((B, H, DK, DV), F32)
    _, o_inter = lax.scan(step, s0, (q_e, k_end, vc, jnp.exp(b_last[:, :, :, 0, :])))
    return (o_intra + o_inter).transpose(1, 0, 3, 2, 4).reshape(B, S, H, DV)

def gated_delta_chunked(q, k, v, g, beta):
    B, S, H, DK = q.shape
    DV = v.shape[-1]
    C = GDN_CHUNK
    n = S // C

    def chunks(t):
        return t.astype(F32).reshape(B, n, C, H, t.shape[-1]).transpose(1, 0, 3, 2, 4)

    qc = chunks(q) * DK ** -0.5
    kc, vc = chunks(k), chunks(v)
    gc = jnp.cumsum(chunks(g[..., None])[..., 0], axis=-1)
    bc = chunks(beta[..., None])
    incl = jnp.tril(jnp.ones((C, C), bool))
    strict = jnp.tril(jnp.ones((C, C), bool), -1)
    diff = gc[..., :, None] - gc[..., None, :]
    decay = jnp.where(incl, jnp.exp(jnp.where(incl, diff, 0.0)), 0.0)
    k_beta = kc * bc
    v_beta = vc * bc
    a = jnp.where(strict, jnp.einsum('nbhid,nbhjd->nbhij', k_beta, kc) * decay, 0.0)
    eye = jnp.eye(C, dtype=F32)
    t_mat = lax.linalg.triangular_solve(a + eye, jnp.broadcast_to(eye, a.shape), left_side=True,
                                        lower=True, unit_diagonal=True)
    w_val = t_mat @ v_beta
    k_cum = t_mat @ (k_beta * jnp.exp(gc)[..., None])
    attn = jnp.einsum('nbhid,nbhjd->nbhij', qc, kc) * decay
    q_g = qc * jnp.exp(gc)[..., None]
    g_last = gc[..., -1:]
    k_end = kc * jnp.exp(g_last - gc)[..., None]
    d_last = jnp.exp(g_last[..., 0])

    def step(state, xs):
        q_i, kc_i, w_i, at_i, ke_i, dl_i = xs
        v_new = w_i - jnp.einsum('bhcd,bhdv->bhcv', kc_i, state)
        o_i = jnp.einsum('bhcd,bhdv->bhcv', q_i, state) + jnp.einsum('bhij,bhjv->bhiv', at_i, v_new)
        state = state * dl_i[..., None, None] + jnp.einsum('bhcd,bhcv->bhdv', ke_i, v_new)
        return state, o_i

    s0 = jnp.zeros((B, H, DK, DV), F32)
    _, o = lax.scan(step, s0, (q_g, k_cum, w_val, attn, k_end, d_last))
    return o.transpose(1, 0, 3, 2, 4).reshape(B, S, H, DV)

def moba_gla_mixer(h, rpe_bias, w_in, gk_w2, gk_b, o_norm, w_out):
    B, S, _ = h.shape
    mq, mk, mv, gq, gk, gv, gg, glr = _split(h @ w_in, EVEN_SPLITS)
    o_a = moba_attention(mq.reshape(B, S, MOBA_HEADS, MOBA_HEAD_DIM),
                         mk.reshape(B, S, MOBA_HEADS, MOBA_HEAD_DIM),
                         mv.reshape(B, S, MOBA_HEADS, MOBA_HEAD_DIM), rpe_bias)
    log_gate = jax.nn.log_sigmoid((glr @ gk_w2 + gk_b).astype(F32)) / GLA_GATE_NORM
    o_b = gla_chunked(gq.reshape(B, S, GLA_HEADS, GLA_DK), gk.reshape(B, S, GLA_HEADS, GLA_DK),
                      gv.reshape(B, S, GLA_HEADS, GLA_DV), log_gate.reshape(B, S, GLA_HEADS, GLA_DK))
    o_b = gated_rmsnorm(o_b, gg.reshape(B, S, GLA_HEADS, GLA_DV), o_norm).astype(h.dtype)
    mixed = jnp.concatenate([o_a.reshape(B, S, MOBA_W), o_b.reshape(B, S, GLA_V_W)], axis=-1)
    return mixed @ w_out

def gated_deltanet_mixer(h, w_in, conv_w, a_log, dt_bias, o_norm, w_out):
    B, S, _ = h.shape
    proj = h @ w_in
    qkv = jax.nn.silu(causal_dwconv(proj[..., :GDN_QKV_W], conv_w))
    q, k, v = _split(qkv, (GDN_QK_W, GDN_QK_W, GDN_V_W))
    gate, b_raw, a_raw = _split(proj[..., GDN_QKV_W:], (GDN_V_W, GDN_HEADS, GDN_HEADS))
    q = l2norm(q.reshape(B, S, GDN_HEADS, GDN_DK))
    k = l2norm(k.reshape(B, S, GDN_HEADS, GDN_DK))
    beta = jax.nn.sigmoid(b_raw.astype(F32))
    g = -jnp.exp(a_log.astype(F32)) * jax.nn.softplus(a_raw.astype(F32) + dt_bias.astype(F32))
    o = gated_delta_chunked(q, k, v.reshape(B, S, GDN_HEADS, GDN_DV), g, beta)
    o = gated_rmsnorm(o, gate.reshape(B, S, GDN_HEADS, GDN_DV), o_norm).astype(h.dtype)
    return o.reshape(B, S, GDN_V_W) @ w_out

def routed_experts(xf, topi, topw, w_gate, w_up, w_down):
    T, D = xf.shape
    M = T * TOP_K
    eid = topi.reshape(M)
    tok = jnp.arange(M, dtype=jnp.int32) // TOP_K
    wts = topw.reshape(M)
    order = jnp.argsort(eid)
    eid_s, tok_s, w_s = eid[order], tok[order], wts[order]
    counts = jnp.bincount(eid, length=N_EXPERTS)
    padded = (counts + MOE_BLOCK - 1) // MOE_BLOCK * MOE_BLOCK
    pad_end = jnp.cumsum(padded)
    pad_start = pad_end - padded
    start = jnp.cumsum(counts) - counts
    dest = pad_start[eid_s] + jnp.arange(M) - start[eid_s]
    nblk = (M + N_EXPERTS * (MOE_BLOCK - 1) + MOE_BLOCK - 1) // MOE_BLOCK
    P = nblk * MOE_BLOCK
    row_tok = jnp.zeros((P,), jnp.int32).at[dest].set(tok_s)
    row_w = jnp.zeros((P,), F32).at[dest].set(w_s)
    blk_exp = jnp.minimum(jnp.searchsorted(pad_end, jnp.arange(nblk) * MOE_BLOCK, side='right'),
                          N_EXPERTS - 1)

    def step(acc, xs):
        e, rt, rw = xs
        xb = xf[rt]
        hb = jax.nn.silu(xb @ w_gate[e]) * (xb @ w_up[e])
        yb = (hb @ w_down[e]).astype(F32) * rw[:, None]
        return acc.at[rt].add(yb), None

    out, _ = lax.scan(step, jnp.zeros((T, D), F32),
                      (blk_exp, row_tok.reshape(nblk, MOE_BLOCK), row_w.reshape(nblk, MOE_BLOCK)))
    return out.astype(xf.dtype)

def moe_ffn(h, router_w, router_b, w_gate, w_up, w_down, sh_gate, sh_up, sh_down):
    B, S, D = h.shape
    xf = h.reshape(B * S, D)
    scores = jax.nn.sigmoid((xf @ router_w).astype(F32))
    sel_scores = scores + router_b.astype(F32)
    grp = sel_scores.reshape(-1, N_GROUPS, N_EXPERTS // N_GROUPS)
    grp_score = jnp.sum(lax.top_k(grp, 2)[0], axis=-1)
    _, top_g = lax.top_k(grp_score, TOPK_GROUPS)
    gmask = jnp.any(top_g[..., None] == jnp.arange(N_GROUPS), axis=1)
    emask = jnp.repeat(gmask, N_EXPERTS // N_GROUPS, axis=1)
    _, topi = lax.top_k(jnp.where(emask, sel_scores, -jnp.inf), TOP_K)
    topw = jnp.take_along_axis(scores, topi, axis=1)
    topw = topw / (jnp.sum(topw, -1, keepdims=True) + 1e-20) * ROUTED_SCALE
    routed = routed_experts(xf, topi, topw, w_gate, w_up, w_down)
    shared = (jax.nn.silu(xf @ sh_gate) * (xf @ sh_up)) @ sh_down
    return (routed + shared).reshape(B, S, D)

def first_inputs(seed: int = 0) -> dict:
    key = jax.random.key(seed)
    ks = iter(jax.random.split(key, 32))

    def nrm(shape, s):
        return jax.random.normal(next(ks), shape, F32) * s

    D = D_MODEL
    u_a = jax.random.uniform(next(ks), (N_ODD, GDN_HEADS), F32, 1.0, 16.0)
    u_dt = jax.random.uniform(next(ks), (N_ODD, GDN_HEADS), F32)
    dt = jnp.exp(u_dt * (math.log(0.1) - math.log(0.001)) + math.log(0.001))
    return {
        "x": nrm((BATCH, SEQ, D), 1.0),
        "c": nrm((BATCH, D), 1.0),
        "rpe_bias": nrm((RPE_BUCKETS, MOBA_HEADS), 0.5),
        "ada_w": nrm((DEPTH, D, 6 * D), 0.5 * D ** -0.5),
        "ada_b": nrm((DEPTH, 6 * D), 0.02),
        "ln_mix_g": 1.0 + nrm((DEPTH, D), 0.02),
        "ln_mix_b": nrm((DEPTH, D), 0.02),
        "ln_ffn_g": 1.0 + nrm((DEPTH, D), 0.02),
        "ln_ffn_b": nrm((DEPTH, D), 0.02),
        "ev_w_in": nrm((N_EVEN, D, EVEN_IN), D ** -0.5),
        "ev_gk_w2": nrm((N_EVEN, GLA_GATE_RANK, GLA_QK_W), GLA_GATE_RANK ** -0.5),
        "ev_gk_b": nrm((N_EVEN, GLA_QK_W), 0.1),
        "ev_norm": 1.0 + nrm((N_EVEN, GLA_DV), 0.02),
        "ev_w_out": nrm((N_EVEN, EVEN_MIX, D), EVEN_MIX ** -0.5 * DEEPNORM_BETA),
        "od_w_in": nrm((N_ODD, D, ODD_IN), D ** -0.5),
        "od_conv_w": nrm((N_ODD, GDN_CONV, GDN_QKV_W), GDN_CONV ** -0.5),
        "od_a_log": jnp.log(u_a),
        "od_dt_bias": dt + jnp.log(-jnp.expm1(-dt)),
        "od_norm": 1.0 + nrm((N_ODD, GDN_DV), 0.02),
        "od_w_out": nrm((N_ODD, ODD_MIX, D), ODD_MIX ** -0.5 * DEEPNORM_BETA),
        "moe_router_w": nrm((DEPTH, D, N_EXPERTS), D ** -0.5),
        "moe_router_b": nrm((DEPTH, N_EXPERTS), 0.01),
        "moe_w_gate": nrm((DEPTH, N_EXPERTS, D, D_EXPERT), D ** -0.5),
        "moe_w_up": nrm((DEPTH, N_EXPERTS, D, D_EXPERT), D ** -0.5),
        "moe_w_down": nrm((DEPTH, N_EXPERTS, D_EXPERT, D), D_EXPERT ** -0.5 * DEEPNORM_BETA),
        "sh_w_gate": nrm((DEPTH, D, D_SHARED), D ** -0.5),
        "sh_w_up": nrm((DEPTH, D, D_SHARED), D ** -0.5),
        "sh_w_down": nrm((DEPTH, D_SHARED, D), D_SHARED ** -0.5 * DEEPNORM_BETA),
    }

def first_block(x, c, rpe_bias, ada_w, ada_b, ln_mix_g, ln_mix_b, ln_ffn_g, ln_ffn_b,
              ev_w_in, ev_gk_w2, ev_gk_b, ev_norm, ev_w_out,
              od_w_in, od_conv_w, od_a_log, od_dt_bias, od_norm, od_w_out,
              moe_router_w, moe_router_b, moe_w_gate, moe_w_up, moe_w_down,
              sh_w_gate, sh_w_up, sh_w_down):
    c_act = jax.nn.silu(c)
    for layer in range(DEPTH):
        mod = c_act @ ada_w[layer] + ada_b[layer]
        sh1, sc1, g1, sh2, sc2, g2 = jnp.split(mod[:, None, :], 6, axis=-1)
        h = x * (1.0 + sc1) + sh1
        i = layer // 2
        if layer % 2 == 0:
            y = moba_gla_mixer(h, rpe_bias, ev_w_in[i], ev_gk_w2[i], ev_gk_b[i], ev_norm[i], ev_w_out[i])
        else:
            y = gated_deltanet_mixer(h, od_w_in[i], od_conv_w[i], od_a_log[i], od_dt_bias[i],
                                     od_norm[i], od_w_out[i])
        x = layer_norm(DEEPNORM_ALPHA * x + g1 * y, ln_mix_g[layer], ln_mix_b[layer])
        h = x * (1.0 + sc2) + sh2
        y = moe_ffn(h, moe_router_w[layer], moe_router_b[layer], moe_w_gate[layer], moe_w_up[layer],
                    moe_w_down[layer], sh_w_gate[layer], sh_w_up[layer], sh_w_down[layer])
        x = layer_norm(DEEPNORM_ALPHA * x + g2 * y, ln_ffn_g[layer], ln_ffn_b[layer])
    return x


GRID_W = 64
CTX_LEN = 256
EPS = 1e-6
POOL_GROUPS = 4
POOL_WINDOWS = (2, 4, 8, 16)
POOL_WIDTH = D_MODEL // 4
POOL_GROUP_DIM = POOL_WIDTH // POOL_GROUPS
HEAD_DIM = 128
N_Q_HEADS = (D_MODEL - POOL_WIDTH) // HEAD_DIM
N_KV_HEADS = 2
ATT_WIDTH = N_Q_HEADS * HEAD_DIM
KV_WIDTH = N_KV_HEADS * HEAD_DIM
Q_BLOCK = 128
ROPE_THETA = 10000.0
ROPE_FREQS = HEAD_DIM // 4
EVEN_SPLITS_2 = (POOL_WIDTH, 2 * POOL_WIDTH, 2 * POOL_WIDTH + ATT_WIDTH,
               2 * POOL_WIDTH + ATT_WIDTH + KV_WIDTH, 2 * POOL_WIDTH + ATT_WIDTH + 2 * KV_WIDTH)
EVEN_IN_2 = 2 * POOL_WIDTH + 2 * ATT_WIDTH + 2 * KV_WIDTH
EVEN_MIX_2 = POOL_WIDTH + ATT_WIDTH
HY_ORDER = 2
HY_WIDTH = 3 * D_MODEL // 4
HY_EMB = 33
HY_BANDS = (HY_EMB - 1) // 2
HY_HIDDEN = 64
HY_DECAY_TARGET = 1e-2
HY_FAST_DECAY = 0.3
HY_SLOW_DECAY = 1.5
FN_WIDTH = D_MODEL - HY_WIDTH
ODD_SPLITS_2 = ((HY_ORDER + 1) * HY_WIDTH, (HY_ORDER + 2) * HY_WIDTH,
              (HY_ORDER + 2) * HY_WIDTH + FN_WIDTH)
ODD_IN_2 = (HY_ORDER + 2) * HY_WIDTH + 2 * FN_WIDTH
ODD_MIX_2 = HY_WIDTH + FN_WIDTH
N_EVEN_2 = (DEPTH + 1) // 2
N_ODD_2 = DEPTH // 2


def rmsnorm(x, g):
    xf = x.astype(jnp.float32)
    y = xf * lax.rsqrt(jnp.mean(xf * xf, axis=-1, keepdims=True) + EPS)
    return y.astype(x.dtype) * g

def modulation(cond, w_mod, b_mod):
    m = jax.nn.silu(cond) @ w_mod + b_mod
    return jnp.split(m, 3, axis=-1)

def to_heads(t, n_heads):
    return t.reshape(t.shape[:2] + (n_heads, HEAD_DIM))

def axial_rope_tables(row_idx, col_idx):
    inv_freq = ROPE_THETA ** (-jnp.arange(ROPE_FREQS, dtype=jnp.float32) / ROPE_FREQS)
    ang = jnp.stack([row_idx[:, None] * inv_freq, col_idx[:, None] * inv_freq], axis=1)
    ang = ang[:, None, :, None, :]
    return jnp.cos(ang), jnp.sin(ang)

def apply_rope(x, cos, sin):
    xr = x.reshape(x.shape[:-1] + (2, 2, ROPE_FREQS)).astype(jnp.float32)
    rot = jnp.concatenate([-xr[..., 1:, :], xr[..., :1, :]], axis=-2)
    return (xr * cos + rot * sin).astype(x.dtype).reshape(x.shape)

def blocked_attention(q, k, v):
    b, lq, hq, dh = q.shape
    hkv = k.shape[2]
    grp = hq // hkv
    nb = lq // Q_BLOCK
    qb = q.reshape(b, nb, Q_BLOCK, hkv, grp, dh).transpose(1, 0, 2, 3, 4, 5)
    scale = dh ** -0.5

    def one_block(qblk):
        s = jnp.einsum('bqhgd,bkhd->bhgqk', qblk, k, preferred_element_type=jnp.float32) * scale
        p = jax.nn.softmax(s, axis=-1).astype(v.dtype)
        return jnp.einsum('bhgqk,bkhd->bqhgd', p, v)

    o = lax.map(one_block, qb)
    return o.transpose(1, 0, 2, 3, 4, 5).reshape(b, lq, hq * dh)

def pool_mixer(u, w_grp, scale):
    b, L, _ = u.shape
    ug = u.reshape(b, L, POOL_GROUPS, POOL_GROUP_DIM).astype(jnp.float32)
    cs = jnp.concatenate([jnp.zeros((b, 1, POOL_GROUPS, POOL_GROUP_DIM), jnp.float32),
                          jnp.cumsum(ug, axis=1)], axis=1)
    t = jnp.arange(L)
    outs = []
    for gi, w in enumerate(POOL_WINDOWS):
        lo = jnp.clip(t - w // 2, 0, L)
        hi = jnp.clip(t + w // 2, 0, L)
        csg = cs[:, :, gi]
        win_sum = jnp.take(csg, hi, axis=1) - jnp.take(csg, lo, axis=1)
        cnt = (hi - lo).astype(jnp.float32)[None, :, None]
        outs.append(win_sum / cnt - ug[:, :, gi])
    d = jnp.stack(outs, axis=2).astype(u.dtype)
    y = jnp.einsum('blgc,gcd->blgd', d, w_grp)
    return y.reshape(b, L, POOL_WIDTH) * scale

def even_mix(a_val, a_gate, q, b_gate, k_all, v_all, pool_w, pool_scale, w_out):
    ya = pool_mixer(a_val, pool_w, pool_scale)
    yb = blocked_attention(q, k_all, v_all)
    y = jnp.concatenate([ya * jax.nn.silu(a_gate), yb * jax.nn.silu(b_gate)], axis=-1)
    return y @ w_out

def short_conv3(u, w, b):
    up = jnp.pad(u, ((0, 0), (1, 1), (0, 0)))
    return up[:, :-2] * w[0] + up[:, 1:-1] * w[1] + up[:, 2:] * w[2] + b

def hyena_filters(L, w1, b1, w2, b2, w3, freq):
    f32 = jnp.float32
    t = jnp.linspace(0.0, 1.0, L, dtype=f32)[:, None]
    w = 2.0 * math.pi * jnp.arange(L, dtype=f32)[:, None] / L
    f = jnp.linspace(1e-4, HY_BANDS - 1, HY_BANDS, dtype=f32)[None, :]
    emb = jnp.concatenate([t, jnp.cos(f * w), -jnp.sin(f * w)], axis=-1)
    fr = freq.astype(f32)
    hdn = jnp.sin(fr * (emb @ w1.astype(f32) + b1.astype(f32)))
    hdn = jnp.sin(fr * (hdn @ w2.astype(f32) + b2.astype(f32)))
    h = (hdn @ w3.astype(f32)).reshape(L, HY_ORDER, 2, HY_WIDTH)
    max_decay = math.log(HY_DECAY_TARGET) / HY_FAST_DECAY
    min_decay = math.log(HY_DECAY_TARGET) / HY_SLOW_DECAY
    deltas = jnp.linspace(min_decay, max_decay, HY_WIDTH, dtype=f32)
    decay = jnp.exp(-t * jnp.abs(deltas))
    h = h * decay[:, None, None, :]
    h = h / (jnp.sum(jnp.abs(h), axis=(0, 2), keepdims=True) + EPS)
    zero = jnp.zeros((1, HY_ORDER, HY_WIDTH), f32)
    return jnp.concatenate([h[:, :, 0], zero, h[:0:-1, :, 1]], axis=0)

def fft_long_conv(z, kfull):
    L = z.shape[1]
    zf = jnp.fft.rfft(z, n=2 * L, axis=1)
    kf = jnp.fft.rfft(kfull, n=2 * L, axis=0)
    return jnp.fft.irfft(zf * kf[None], n=2 * L, axis=1)[:, :L]

def hyena_mixer(u, conv_w, conv_b, w1, b1, w2, b2, w3, freq, skip):
    L = u.shape[1]
    uc = short_conv3(u, conv_w, conv_b)
    v, x1, x2 = jnp.split(uc, HY_ORDER + 1, axis=-1)
    k = hyena_filters(L, w1, b1, w2, b2, w3, freq)
    z = v.astype(jnp.float32)
    for o, gate_o in enumerate((x1, x2)):
        z = gate_o.astype(jnp.float32) * (fft_long_conv(z, k[:, o]) + skip[o].astype(jnp.float32) * z)
    return z.astype(u.dtype)

def fourier_mixer(u, w):
    y = jnp.fft.fft2(u.astype(jnp.float32), axes=(1, 2), norm='ortho').real
    return y.astype(u.dtype) @ w

def odd_mix(h, w_in, w_out, fn_w, conv_w, conv_b, w1, b1, w2, b2, w3, freq, skip):
    hy_in, hy_gate, fn_in, fn_gate = jnp.split(h @ w_in, ODD_SPLITS_2, axis=-1)
    yc = hyena_mixer(hy_in, conv_w, conv_b, w1, b1, w2, b2, w3, freq, skip)
    yd = fourier_mixer(fn_in, fn_w)
    y = jnp.concatenate([yc * jax.nn.silu(hy_gate), yd * jax.nn.silu(fn_gate)], axis=-1)
    return y @ w_out

def second_inputs(seed: int = 0) -> dict:
    key = jax.random.key(seed)
    ks = jax.random.split(key, 26)

    def nrm(k, shape, s):
        return jax.random.normal(k, shape, jnp.float32) * s

    return {
        'x': nrm(ks[0], (BATCH, SEQ, D_MODEL), 1.0),
        'c': nrm(ks[1], (BATCH, D_MODEL), 1.0),
        'ctx': nrm(ks[2], (BATCH, CTX_LEN, D_MODEL), 1.0),
        'c_ctx': nrm(ks[3], (D_MODEL,), 1.0),
        'w_mod': nrm(ks[4], (DEPTH, D_MODEL, 3 * D_MODEL), 0.5 * D_MODEL ** -0.5),
        'b_mod': nrm(ks[5], (DEPTH, 3 * D_MODEL), 0.01),
        'norm_g': 1.0 + nrm(ks[6], (DEPTH, D_MODEL), 0.05),
        'ev_w_in': nrm(ks[7], (N_EVEN_2, D_MODEL, EVEN_IN_2), D_MODEL ** -0.5),
        'ev_w_out': nrm(ks[8], (N_EVEN_2, EVEN_MIX_2, D_MODEL), EVEN_MIX_2 ** -0.5),
        'pool_w': nrm(ks[9], (N_EVEN_2, POOL_GROUPS, POOL_GROUP_DIM, POOL_GROUP_DIM), POOL_GROUP_DIM ** -0.5),
        'pool_scale': 1.0 + nrm(ks[10], (N_EVEN_2, POOL_WIDTH), 0.1),
        'q_norm_g': 1.0 + nrm(ks[11], (N_EVEN_2, HEAD_DIM), 0.05),
        'k_norm_g': 1.0 + nrm(ks[12], (N_EVEN_2, HEAD_DIM), 0.05),
        'od_w_in': nrm(ks[13], (N_ODD_2, D_MODEL, ODD_IN_2), D_MODEL ** -0.5),
        'od_w_out': nrm(ks[14], (N_ODD_2, ODD_MIX_2, D_MODEL), ODD_MIX_2 ** -0.5),
        'hy_conv_w': nrm(ks[15], (N_ODD_2, 3, (HY_ORDER + 1) * HY_WIDTH), 3 ** -0.5),
        'hy_conv_b': nrm(ks[16], (N_ODD_2, (HY_ORDER + 1) * HY_WIDTH), 0.01),
        'hy_w1': nrm(ks[17], (N_ODD_2, HY_EMB, HY_HIDDEN), HY_EMB ** -0.5),
        'hy_b1': nrm(ks[18], (N_ODD_2, HY_HIDDEN), 0.1),
        'hy_w2': nrm(ks[19], (N_ODD_2, HY_HIDDEN, HY_HIDDEN), HY_HIDDEN ** -0.5),
        'hy_b2': nrm(ks[20], (N_ODD_2, HY_HIDDEN), 0.1),
        'hy_w3': nrm(ks[21], (N_ODD_2, HY_HIDDEN, HY_ORDER * 2 * HY_WIDTH), HY_HIDDEN ** -0.5),
        'hy_freq': 1.0 + nrm(ks[22], (N_ODD_2, HY_HIDDEN), 0.1),
        'hy_skip': nrm(ks[23], (N_ODD_2, HY_ORDER, HY_WIDTH), 1.0),
        'fn_w': nrm(ks[24], (N_ODD_2, FN_WIDTH, FN_WIDTH), FN_WIDTH ** -0.5),
        'final_g': 1.0 + nrm(ks[25], (D_MODEL,), 0.05),
    }

def second_block(x, c, ctx, c_ctx, w_mod, b_mod, norm_g, ev_w_in, ev_w_out, pool_w, pool_scale,
              q_norm_g, k_norm_g, od_w_in, od_w_out, hy_conv_w, hy_conv_b, hy_w1, hy_b1, hy_w2, hy_b2,
              hy_w3, hy_freq, hy_skip, fn_w, final_g):
    n_tok = x.shape[1]
    rows = n_tok // GRID_W
    row_idx = jnp.broadcast_to(jnp.arange(rows, dtype=jnp.float32)[:, None], (rows, GRID_W)).reshape(-1)
    col_idx = jnp.broadcast_to(jnp.arange(GRID_W, dtype=jnp.float32)[None, :], (rows, GRID_W)).reshape(-1)
    cos, sin = axial_rope_tables(row_idx, col_idx)

    for i in range(DEPTH):
        li = i // 2
        is_even = i % 2 == 0
        ctx_needed = any(j % 2 == 0 for j in range(i + 1, DEPTH))
        shift, scale, gate = modulation(c[:, None, :], w_mod[i], b_mod[i])
        h = rmsnorm(x, norm_g[i]) * (1 + scale) + shift
        if is_even or ctx_needed:
            cshift, cscale, cgate = modulation(c_ctx[None, None, :], w_mod[i], b_mod[i])
            hc = rmsnorm(ctx, norm_g[i]) * (1 + cscale) + cshift
        if is_even:
            w_in = ev_w_in[li]
            a_val, a_gate, q, k, v, b_gate = jnp.split(h @ w_in, EVEN_SPLITS_2, axis=-1)
            q = apply_rope(rmsnorm(to_heads(q, N_Q_HEADS), q_norm_g[li]), cos, sin)
            k = apply_rope(rmsnorm(to_heads(k, N_KV_HEADS), k_norm_g[li]), cos, sin)
            if ctx_needed:
                ca_val, ca_gate, cq, ck, cv, cb_gate = jnp.split(hc @ w_in, EVEN_SPLITS_2, axis=-1)
            else:
                ck, cv = jnp.split(hc @ w_in[:, EVEN_SPLITS_2[2]:EVEN_SPLITS_2[4]], 2, axis=-1)
            ck = rmsnorm(to_heads(ck, N_KV_HEADS), k_norm_g[li])
            cv = to_heads(cv, N_KV_HEADS)
            k_all = jnp.concatenate([ck, k], axis=1)
            v_all = jnp.concatenate([cv, to_heads(v, N_KV_HEADS)], axis=1)
            y = even_mix(a_val, a_gate, q, b_gate, k_all, v_all, pool_w[li], pool_scale[li], ev_w_out[li])
            if ctx_needed:
                cq = rmsnorm(to_heads(cq, N_Q_HEADS), q_norm_g[li])
                yc = even_mix(ca_val, ca_gate, cq, cb_gate, ck, cv, pool_w[li], pool_scale[li], ev_w_out[li])
                ctx = ctx + cgate * yc
            x = x + gate * y
        else:
            y = odd_mix(h, od_w_in[li], od_w_out[li], fn_w[li], hy_conv_w[li], hy_conv_b[li],
                        hy_w1[li], hy_b1[li], hy_w2[li], hy_b2[li], hy_w3[li], hy_freq[li], hy_skip[li])
            if ctx_needed:
                yc = odd_mix(hc, od_w_in[li], od_w_out[li], fn_w[li], hy_conv_w[li], hy_conv_b[li],
                             hy_w1[li], hy_b1[li], hy_w2[li], hy_b2[li], hy_w3[li], hy_freq[li], hy_skip[li])
                ctx = ctx + cgate * yc
            x = x + gate * y
    return rmsnorm(x, final_g)


def setup_inputs(seed=0):
    out = dict(first_inputs(seed))
    for name, value in second_inputs(seed + 1).items():
        if name != "x":
            out[name + "_2"] = value
    return out


def reference(
    x, c, rpe_bias, ada_w, ada_b, ln_mix_g, ln_mix_b, ln_ffn_g, ln_ffn_b, ev_w_in, ev_gk_w2,
    ev_gk_b, ev_norm, ev_w_out, od_w_in, od_conv_w, od_a_log, od_dt_bias, od_norm, od_w_out,
    moe_router_w, moe_router_b, moe_w_gate, moe_w_up, moe_w_down, sh_w_gate, sh_w_up, sh_w_down,
    c_2, ctx_2, c_ctx_2, w_mod_2, b_mod_2, norm_g_2, ev_w_in_2, ev_w_out_2, pool_w_2,
    pool_scale_2, q_norm_g_2, k_norm_g_2, od_w_in_2, od_w_out_2, hy_conv_w_2, hy_conv_b_2,
    hy_w1_2, hy_b1_2, hy_w2_2, hy_b2_2, hy_w3_2, hy_freq_2, hy_skip_2, fn_w_2, final_g_2,
):
    x = first_block(
        x, c, rpe_bias, ada_w, ada_b, ln_mix_g, ln_mix_b, ln_ffn_g, ln_ffn_b, ev_w_in, ev_gk_w2,
        ev_gk_b, ev_norm, ev_w_out, od_w_in, od_conv_w, od_a_log, od_dt_bias, od_norm, od_w_out,
        moe_router_w, moe_router_b, moe_w_gate, moe_w_up, moe_w_down, sh_w_gate, sh_w_up,
        sh_w_down,
    )
    return second_block(
        x, c_2, ctx_2, c_ctx_2, w_mod_2, b_mod_2, norm_g_2, ev_w_in_2, ev_w_out_2, pool_w_2,
        pool_scale_2, q_norm_g_2, k_norm_g_2, od_w_in_2, od_w_out_2, hy_conv_w_2, hy_conv_b_2,
        hy_w1_2, hy_b1_2, hy_w2_2, hy_b2_2, hy_w3_2, hy_freq_2, hy_skip_2, fn_w_2, final_g_2,
    )


_drawn_inputs = setup_inputs


def setup_inputs(seed=0):
    import zlib

    import numpy as np

    out = dict(_drawn_inputs(seed))
    spreads = {}
    factors = {'rpe_bias': 4.466,
     'ev_gk_w2': 4.68,
     'ev_gk_b': 8.0,
     'ev_norm': 8.0,
     'od_a_log': 3.877,
     'od_dt_bias': 3.18,
     'od_norm': 21.715,
     'ctx_2': 5.701,
     'b_mod_2': 5.454,
     'pool_scale_2': 5.573,
     'q_norm_g_2': 8.0,
     'k_norm_g_2': 8.0,
     'hy_conv_b_2': 8.0,
     'hy_b1_2': 8.0,
     'hy_b2_2': 5.433,
     'hy_freq_2': 8.0}
    for name, (base, spread) in spreads.items():
        noise = np.random.default_rng([zlib.crc32(name.encode()), seed]).standard_normal(out[name].shape)
        drawn = base * np.exp(spread * noise) if base else spread * noise
        out[name] = jnp.asarray(drawn.astype(out[name].dtype))
    for name, factor in factors.items():
        out[name] = (out[name] * factor).astype(out[name].dtype)
    return out
```

```python
import math
from contextlib import ExitStack

import numpy as np

import concourse.bass as bass
from concourse import mybir

F32 = mybir.dt.float32
ACT = mybir.ActivationFunctionType
ALU = mybir.AluOpType
AX = mybir.AxisListType

D = 1024
T = 256
NE = 64
ALPHA = float(4 ** 0.25)
STOP = None


def shape_constants():
    p = np.arange(128)
    blk = {}
    blk["ident"] = np.eye(128)
    blk["flip"] = np.eye(128)[::-1]
    blk["ones"] = np.ones((128, 128))
    same = (p[:, None] // 64) == (p[None, :] // 64)
    blk["incl"] = (same & (p[:, None] <= p[None, :])).astype(float)
    blk["after"] = (same & (p[:, None] > p[None, :])).astype(float)
    blk["same"] = same.astype(float)
    lv = []
    for b in (1, 2, 4, 8, 16, 32):
        pair = (p[:, None] // (2 * b)) == (p[None, :] // (2 * b))
        lv.append(pair & (p[:, None] % (2 * b) >= b) & (p[None, :] % (2 * b) < b))
    blk["level"] = np.stack(lv, 1).reshape(128, -1).astype(float)
    rot = np.zeros((128, 128))
    for a in range(2):
        for i in range(32):
            rot[a * 64 + 32 + i, a * 64 + i] = -1.0
            rot[a * 64 + i, a * 64 + 32 + i] = 1.0
    blk["rot"] = rot
    t = np.arange(T)
    inv = (np.float32(10000.0) ** (-np.arange(32, dtype=np.float32) / np.float32(32))).astype(np.float32)
    row = (t // 64).astype(np.float32)
    col = (t % 64).astype(np.float32)
    ang = np.stack([row[:, None] * inv, col[:, None] * inv], 1)
    ang = np.broadcast_to(ang[:, :, None, :], (T, 2, 2, 32)).reshape(T, 128).T.astype(np.float64)
    blk["cosr"] = np.cos(ang)
    blk["sinr"] = np.sin(ang)
    s = np.arange(256)
    w = (2 * s[None, :] + 1) * np.pi / 512 * s[:, None]
    for name, m in (("dc", np.cos(w)), ("ds", np.sin(w)), ("dct", np.cos(w).T / 256), ("dst", -np.sin(w).T / 256),
                    ("fc", np.cos(2 * np.pi * s[:, None] * s / 256)), ("fs", np.sin(2 * np.pi * s[:, None] * s / 256))):
        blk[name] = m.reshape(2, 128, 256).transpose(1, 0, 2).reshape(128, 512)
    ic = np.zeros((2, 128, 256))
    for g, wd in enumerate((2, 4, 8, 16)):
        cnt = np.clip(t + wd // 2, 0, T) - np.clip(t - wd // 2, 0, T)
        ic[g // 2, (g % 2) * 64:(g % 2) * 64 + 64] = 1.0 / cnt
    blk["icnt"] = ic.transpose(1, 0, 2).reshape(128, 512)
    hot = np.zeros((128, 512))
    for m in range(512):
        d = 255 - m
        if d < 0:
            hot[32, m] = 1.0
        else:
            if d < 16:
                bkt = d
            else:
                lg = np.float32(np.log(np.float32(d) / np.float32(16)))
                bkt = min(16 + int(np.float32(lg / np.float32(math.log(128.0)) * np.float32(16))), 31)
            hot[bkt, m] = 1.0
    blk["hot"] = hot
    lin = np.linspace(0.0, 1.0, T, dtype=np.float32)
    wv = (np.float32(2.0 * math.pi) * np.arange(T, dtype=np.float32)[:, None] / np.float32(T)).astype(np.float32)
    f = np.linspace(1e-4, 15, 16, dtype=np.float32)[None, :]
    fw = (f * wv).astype(np.float64)
    emb = np.concatenate([lin[:, None], np.cos(fw), -np.sin(fw)], -1)
    e = np.zeros((128, 256))
    e[:33] = emb.T
    blk["emb"] = e
    deltas = np.linspace(math.log(1e-2) / 1.5, math.log(1e-2) / 0.3, 768, dtype=np.float32)
    dec = np.exp((-lin[:, None] * np.abs(deltas)).astype(np.float64))
    blk["dec"] = dec.reshape(2, 128, 768).transpose(1, 0, 2).reshape(128, 1536)
    rs = np.ones((128, 512))
    rs[:, ::64] = 0.0
    blk["rset"] = rs
    eps = np.zeros((128, 4))
    eps[:, 0] = 1e-5
    eps[:, 1] = 1e-6
    eps[:, 2] = 1.0
    blk["eps"] = eps
    first = ("ident", "flip", "ones", "eps", "incl", "after", "same", "level", "hot", "rset")
    order = list(first) + [n for n in blk if n not in first]
    at, cols, lo = {}, 0, 0
    for n in order:
        at[n] = (cols, blk[n].shape[1])
        cols += blk[n].shape[1]
        if n == first[-1]:
            lo = cols
    return np.concatenate([blk[n] for n in order], 1).astype(np.float32), at, lo


class Queue:

    def __init__(self, sem):
        self.sem, self.n, self.ops, self.seen = sem, 0, [], {}

    def wait(self, *toks):
        for t in toks:
            if t is None:
                continue
            if isinstance(t, list):
                self.wait(*t)
                continue
            s, v = t
            if self.seen.get(s.name, 0) < v:
                self.seen[s.name] = v
                self.ops.append(lambda e, s=s, v=v: e.wait_ge(s, v))

    def do(self, fn, *toks, inc=True):
        self.wait(*toks)
        if not inc:
            self.ops.append(fn)
            return None
        self.n += 1
        self.ops.append(lambda e: fn(e).then_inc(self.sem, 1))
        return (self.sem, self.n)

    def last(self):
        return (self.sem, self.n)

    def emit(self, e):
        for op in self.ops:
            op(e)


class Ring:

    def __init__(self, ids):
        self.ids, self.at = list(ids), 0
        self.free = {i: [] for i in ids}

    def take(self):
        i = self.ids[self.at % len(self.ids)]
        self.at += 1
        return i, self.free[i]

    def rel(self, i, *toks):
        self.free[i] = list(toks)


def build(nc, A, out, at, lo):
    ctx = ExitStack()
    with ctx:
        def sb(name, shape, dt=F32):
            return ctx.enter_context(nc.sbuf_tensor(name, shape, dt))

        def sem(name):
            return ctx.enter_context(nc.semaphore(name))

        pe, act, dve, pool, sp = (Queue(sem("s_" + n)) for n in ("pe", "act", "dve", "pool", "sp"))
        dcount = {}

        def dma(q, dst, src, s, *toks):
            dcount[s.name] = dcount.get(s.name, 0) + 16
            q.wait(*toks)
            q.ops.append(lambda e: e.dma_start(dst, src).then_inc(s, 16))
            return (s, dcount[s.name])

        NS = 6
        wbuf = sb("wbuf", [128, NS, 2048])
        wsem = [sem(f"s_w{i}") for i in range(NS)]
        wr = Ring(range(NS))
        cst = sb("cst", [128, A["consts"].shape[1]])
        xT = sb("xT", [128, 8, T])
        hT = sb("hT", [128, 8, T])
        slab = sb("slab", [128, 9, 2048])
        ps = [ctx.enter_context(nc.psum_tensor(f"ps{i}", [128, 512], F32)) for i in range(8)]
        pr = Ring(range(8))

        def C(name):
            c0, n = at[name]
            return cst[:, c0:c0 + n]

        ident, flip, ones = C("ident"), C("flip"), C("ones")
        eps5, eps6 = C("eps")[:, 0:1], C("eps")[:, 1:2]
        one_c = C("eps")[:, 2:3]

        def S(i, *dims):
            v = slab[:, i, :]
            if len(dims) == 1:
                return v[:, 0:dims[0]]
            if len(dims) == 2:
                return v[:, 0:dims[0] * dims[1]].rearrange("p (a b) -> p a b", b=dims[1])
            return v[:, 0:dims[0] * dims[1] * dims[2]].rearrange("p (a b c) -> p a b c", b=dims[1], c=dims[2])

        def bc(v, n):
            return v.unsqueeze(1).broadcast_to([v.shape[0], n, v.shape[1]])

        def inner(v, n):
            return v.unsqueeze(2).broadcast_to([v.shape[0], v.shape[1], n])

        def mm(o, lhsT, rhs, start, stop, *toks, inc=False, skip=False):
            return pe.do(lambda e: e.matmul(o, lhsT, rhs, start=start, stop=stop, skip_group_check=skip),
                         *toks, inc=inc)

        def tr(o, i, *toks, inc=False):
            n = i.shape[0]
            return pe.do(lambda e: e.transpose(o, i, ident[0:n, 0:n]), *toks, inc=inc)

        def afn(o, i, fn, *toks, scale=1.0, bias=0.0, acc=None):
            return act.do(lambda e: e.activation(o, i, fn, bias=bias, scale=scale, accum_out=acc), *toks)

        def tt(q, o, a, b, op, *toks):
            return q.do(lambda e: e.tensor_tensor(o, a, b, op), *toks)

        def ts(q, o, a, s1, s2, op0, op1, *toks):
            if s2 is None:
                return q.do(lambda e: e.tensor_scalar(o, a, s1, None, op0), *toks)
            return q.do(lambda e: e.tensor_scalar(o, a, s1, s2, op0, op1), *toks)

        def stt(o, a, s, b, op0, op1, *toks):
            return dve.do(lambda e: e.scalar_tensor_tensor(o, a, s, b, op0, op1), *toks)

        def copy(o, i, *toks):
            return dve.do(lambda e: e.tensor_copy(o, i), *toks)

        def meet():
            all_ = [q.last() for q in (pe, act, dve, pool)]
            for q in (pe, act, dve, pool):
                q.wait(*all_)
            return all_

        class Unit:
            pass

        def unit(src, a, b):
            u = Unit()
            u.i, free = wr.take()
            u.v = wbuf[:, u.i, 0:a * b].rearrange("p (a b) -> p a b", b=b)
            u.tok = dma(sp, u.v, src, wsem[u.i], *free)
            return u

        def cols(w, c0, n):
            return unit(w.rearrange("(p k) n -> p k n", k=8)[:, :, c0:c0 + n], 8, n)

        def rows(w, k0):
            return unit(w.rearrange("(k p) n -> p k n", p=128)[:, k0:k0 + 2, :], 2, w.shape[1])

        def proj_f(w, c0, n, rhs, evac, *ready):
            u = cols(w, c0, n)
            b, free = pr.take()
            pe.wait(u.tok, free, *ready)
            for m in range((n + 127) // 128):
                mc = min(128, n - m * 128)
                for k in range(8):
                    t = mm(ps[b][0:mc, m * 256:(m + 1) * 256], u.v[:, k, m * 128:m * 128 + mc], rhs[:, k, :],
                           k == 0, k == 7, inc=(k == 7))
            wr.rel(u.i, t)
            pr.rel(b, evac(ps[b], t))

        def proj_t(w, c0, n, lhs, evac, *ready):
            u = cols(w, c0, n)
            b, free = pr.take()
            pe.wait(u.tok, free, *ready)
            for m in range(2):
                for k in range(8):
                    t = mm(ps[b][:, m * 256:m * 256 + n], lhs[:, k, m * 128:(m + 1) * 128], u.v[:, k, :],
                           k == 0, k == 7, inc=(k == 7))
            wr.rel(u.i, t)
            pr.rel(b, evac(ps[b], t))

        YB = (4, 5, 6, 7)

        def Y(j):
            return ps[YB[j // 2]][:, (j % 2) * 256:(j % 2) * 256 + 256]

        def down(u, rhs, first, last, *ready):
            pe.wait(u.tok, *ready)
            t = None
            for kk in range(2):
                for j in range(8):
                    fin = kk == 1 and j == 7
                    t = mm(Y(j), u.v[:, kk, j::8], rhs[kk], first and kk == 0 and j % 2 == 0,
                           last and kk == 1 and j % 2 == 1, inc=fin, skip=True)
            wr.rel(u.i, t)
            return t

        def take_y():
            toks = []
            for b in YB:
                toks += pr.free[b]
            pr.ids, pr.at = [0, 1, 2, 3], 0
            return toks

        def give_y(tok):
            for b in YB:
                pr.rel(b, tok)
            pr.ids, pr.at = list(range(8)), 0

        s_in = sem("s_in")
        s_c2 = sem("s_c2")
        s_sm = sem("s_sm")
        xin = slab[:, 0:1, :].rearrange("p o n -> p (o n)").rearrange("p (t n) -> p t n", t=2)
        dma(sp, xin, A["x"][0].rearrange("(t p) n -> p t n", p=128), s_in)
        cv = sb("cv", [128, 3, 8])
        dma(sp, cv[:, 0, :], A["c"][0].rearrange("(p k) -> p k", k=8), s_in)
        dma(sp, cv[:, 1, :], A["c_2"][0].rearrange("(p k) -> p k", k=8), s_in)
        dma(sp, cv[:, 2, :], A["c_ctx_2"].rearrange("(p k) -> p k", k=8), s_in)
        t_in = dma(sp, cst[:, 0:lo], A["consts"][:, 0:lo], s_in)
        t_c2 = dma(pool, cst[:, lo:], A["consts"][:, lo:], s_c2)

        nvec = 128
        vec = sb("vec", [128, 21, 8])
        small = {}

        def vload(i, src, n=1):
            if n == 1:
                return dma(pool, vec[:, i, :], src.rearrange("(p k) -> p k", k=8), s_sm)
            return dma(pool, vec[:, i:i + n, :], src.rearrange("s (p k) -> p s k", k=8), s_sm)

        for i, n in enumerate(("ln_mix_g", "ln_mix_b", "ln_ffn_g", "ln_ffn_b")):
            for l in range(2):
                vload(2 * i + l, A[n][l])
        vload(8, A["norm_g_2"][0])
        vload(9, A["norm_g_2"][1])
        vload(10, A["final_g_2"])
        modb = sb("modb", [128, 18, 8])
        for l in range(2):
            dma(pool, modb[:, 6 * l:6 * l + 6, :], A["ada_b"][l].rearrange("(s p k) -> p s k", s=6, k=8), s_sm)
            dma(pool, modb[:, 12 + 3 * l:15 + 3 * l, :],
                A["b_mod_2"][l].rearrange("(s p k) -> p s k", s=3, k=8), s_sm)
        misc = sb("misc", [128, 2048])
        stage = misc[:, 1600:1984].rearrange("p (a b) -> p a b", a=3)
        colv = sb("colv", [128, 3, 128])
        dma(pool, stage[0:96, 0, :], A["od_conv_w"][0].rearrange("k (j p) -> (k j) p", p=128), s_sm)
        row = [0]
        place = {}

        def srow(name, src):
            n = src.shape[0]
            place[name] = row[0]
            dma(pool, stage[row[0]:row[0] + n, 1, :], src, s_sm)
            row[0] += n

        srow("hcw", A["hy_conv_w_2"][0].rearrange("k (j p) -> (k j) p", p=128))
        srow("hcb", A["hy_conv_b_2"][0].rearrange("(j p) -> j p", p=128))
        srow("skip", A["hy_skip_2"][0].rearrange("o (j p) -> (o j) p", p=128))
        srow("psc", A["pool_scale_2"][0].rearrange("(j p) -> j p", p=128))
        srow("evn", A["ev_norm"])
        srow("odn", A["od_norm"])
        srow("qn", A["q_norm_g_2"])
        srow("kn", A["k_norm_g_2"])
        srow("gkb", A["ev_gk_b"][0].rearrange("(j p) -> j p", p=128))
        nrow = row[0]
        for i, n in enumerate(("hy_b1_2", "hy_b2_2", "hy_freq_2")):
            dma(pool, stage[i:i + 1, 2, 0:64], A[n], s_sm)
        rpe33 = sb("rpe33", [33, 4])
        t_rm = pool.do(lambda e: e.memset(rpe33[:, :], -1e30))
        dma(pool, rpe33[0:32, :], A["rpe_bias"], s_sm, t_rm)
        gkw2 = sb("gkw2", [16, 256])
        dma(pool, gkw2[:, :], A["ev_gk_w2"][0], s_sm)
        poolw = sb("poolw", [128, 2, 64])
        dma(pool, poolw[:, :, :], A["pool_w_2"][0].rearrange("(t g) c d -> (g c) t d", t=2), s_sm)
        hw12 = sb("hw12", [64, 2, 64])
        dma(pool, hw12[0:33, 0, :], A["hy_w1_2"][0], s_sm)
        dma(pool, hw12[:, 1, :], A["hy_w2_2"][0], s_sm)
        rtr = sb("rtr", [128, 2, 8, 64])
        for l in range(2):
            dma(pool, rtr[:, l, :, :], A["moe_router_w"][l].rearrange("(p k) n -> p k n", k=8), s_sm)
        rtb = sb("rtb", [128, 2, 64])
        for l in range(2):
            dma(pool, rtb[:, l, :], A["moe_router_b"][l:l + 1, :].broadcast_to([128, 64]), s_sm)
        adt = sb("adt", [128, 2, 8])
        dma(pool, adt[:, 0, :], A["od_a_log"].broadcast_to([128, 8]), s_sm)
        t_sm = dma(pool, adt[:, 1, :], A["od_dt_bias"].broadcast_to([128, 8]), s_sm)

        def vc(i, j):
            return vec[:, i, j:j + 1]

        def cv1(name, j=0):
            r = place[name] + j
            return colv[:, 1, r:r + 1]

        pe.wait(t_in, t_sm)
        b, free = pr.take()
        tr(ps[b][:, 0:96], stage[0:96, 0, :])
        tr(ps[b][:, 128:128 + nrow], stage[0:nrow, 1, :])
        t = tr(ps[b][0:64, 256:259], stage[0:3, 2, 0:64], inc=True)
        copy(colv[:, 0, 0:96], ps[b][:, 0:96], t)
        copy(colv[:, 1, 0:nrow], ps[b][:, 128:128 + nrow])
        t_cols = copy(colv[0:64, 2, 0:3], ps[b][0:64, 256:259])
        pr.rel(b, t_cols)

        def to_features(src, dst, tok):
            last = None
            for k2 in range(4):
                b, free = pr.take()
                pe.wait(free, tok)
                for kk in range(2):
                    for m in range(2):
                        t = tr(ps[b][:, kk * 256 + m * 128:kk * 256 + m * 128 + 128],
                               src[:, m, 2 * k2 + kk::8], inc=(kk == 1 and m == 1))
                o = dst[:, 2 * k2:2 * k2 + 2, :].rearrange("p a b -> p (a b)")
                last = copy(o, ps[b][:, :], t)
                pr.rel(b, last)
            return last

        t_x = to_features(xin, xT, t_in)

        ca = sb("ca", [128, 8, 3])
        t = afn(ca[:, :, :].rearrange("p k s -> p s k"), cv[:, :, :], ACT.Silu, t_in)
        t_ca = t
        mods = sb("mods", [128, 18, 8])
        modc = sb("modc", [128, 2, 8])

        def modulate(w, nsec, base, ctx_too=False):
            v0, nv = (0, 1) if base < 12 else ((1, 2) if ctx_too else (1, 1))
            b, free = pr.take()
            pe.wait(free, t_ca)
            wv = w.rearrange("(p k) n -> p k n", k=8)
            for s in range(nsec):
                for q in range(4):
                    u = unit(wv[:, 2 * q:2 * q + 2, s * 1024:(s + 1) * 1024], 2, 1024)
                    pe.wait(u.tok)
                    for kk in range(2):
                        for j in range(8):
                            k = 2 * q + kk
                            o = ps[b][:, (s * 8 + j) * nv:(s * 8 + j + 1) * nv]
                            fin = kk == 1 and j == 7
                            t = mm(o, u.v[:, kk, j::8], ca[:, k, v0:v0 + nv], s == 0 and k == 0 and j == 0,
                                   s == nsec - 1 and k == 7 and j == 7, inc=fin, skip=True)
                    wr.rel(u.i, t)
            pv = ps[b][:, 0:nsec * 8 * nv].rearrange("p (s j v) -> p s j v", s=nsec, v=nv)
            t1 = tt(dve, mods[:, base:base + nsec, :], pv[:, :, :, 0], modb[:, base:base + nsec, :], ALU.add,
                    t, t_sm)
            if ctx_too:
                t1 = tt(dve, modc[:, :, :], pv[:, 0:2, :, 1], modb[:, base:base + 2, :], ALU.add, t, t_sm)
                t2 = ts(dve, modc[:, 1, :], modc[:, 1, :], 1.0, None, ALU.add, None, t1)
            secs = (1, 4) if base < 12 else (1,)
            for s in secs:
                t2 = ts(dve, mods[:, base + s, :], mods[:, base + s, :], 1.0, None, ALU.add, None, dve.last())
            pr.rel(b, t2)
            return t2

        def mc(base, s, j):
            return mods[:, base + s, j:j + 1]

        def scale_shift(dst, src, g, bcol, *toks):
            for j in range(8):
                t = ts(dve, dst[:, j, :], src[:, j, :], g(j), bcol(j), ALU.mult, ALU.add, *toks)
            return t

        def col_sum(src, n, scale_tok, *toks):
            b, free = pr.take()
            pe.wait(free, *toks)
            for k in range(n):
                t = mm(ps[b][:, 0:256], ones, src[:, k, :], k == 0, k == n - 1, inc=(k == n - 1))
            return b, t

        rs_t = sb("rs_t", [128, 2, 512])
        eps_a = {1e-5: eps5, 1e-6: eps6}

        def rsqrt(o, tmp, src, scale, eps, *toks):
            t = afn(tmp, src, ACT.Ln, *toks, scale=scale, bias=eps_a[eps])
            return afn(o, tmp, ACT.Exp, t, scale=-0.5)

        def norm_to(dst, src, sq, eps, tok, mean=True):
            rs = rs_t[:, 0, 0:256]
            if mean:
                b, t = col_sum(src, 8, None, tok)
                t = ts(dve, rs_t[:, 1, 256:512], ps[b][:, 0:256], 1.0 / D, None, ALU.mult, None, t)
                pr.rel(b, t)
                tok = tt(dve, src, src, bc(rs_t[:, 1, 256:512], 8), ALU.subtract, t)
            t = afn(sq, src, ACT.Square, tok)
            b, t = col_sum(sq, 8, None, t)
            t = rsqrt(rs, rs_t[:, 1, 0:256], ps[b][:, 0:256], 1.0 / D, eps, t)
            pr.rel(b, t)
            return tt(dve, dst, src, bc(rs, 8), ALU.mult, t, tok)

        def residual(base, gsec, t_y, vi, l, hbase, hsec):
            u, sq = S(8, 8, 256), S(7, 8, 256)
            meet()
            t = ts(dve, u, xT[:, :, :], ALPHA, None, ALU.mult, None)
            for j in range(8):
                t = stt(u[:, j, :], Y(j), mc(base, gsec, j), u[:, j, :], ALU.mult, ALU.add, t_y, t)
            give_y(t)
            t = norm_to(u, u, sq, 1e-5, t)
            t = scale_shift(xT, u, lambda j: vc(vi + l, j), lambda j: vc(vi + 2 + l, j), t)
            if hbase is not None:
                t = scale_shift(hT, xT, lambda j: mc(hbase, hsec + 1, j), lambda j: mc(hbase, hsec, j), t)
            return t

        def out_proj(w, src, *ready):
            toks = take_y()
            for q in range(4):
                u = rows(w, 2 * q)
                t = down(u, [src[:, 2 * q, :], src[:, 2 * q + 1, :]], q == 0, q == 3, toks, *ready)
            return t

        rtS = sb("rtS", [128, 2, 66])
        rtG = sb("rtG", [128, 2, 12])
        rt8 = sb("rt8", [128, 2, 8, 8])
        rtm = S(2, 768).rearrange("p (a m e) -> p a m e", a=6, m=2)
        wT = sb("wT", [64, 256])
        hid = S(0, 8, 256).rearrange("p (h m) n -> p h m n", m=2)
        hsg = S(1, 2, 256)
        t_sent = pool.do(lambda e: e.memset(rtS[:, :, :], -2e38))
        t_sent = pool.do(lambda e: e.memset(rtG[:, :, :], -2e38), t_sent)

        def route(l, t_h):
            b, free = pr.take()
            pe.wait(free, t_h, t_sm)
            for m in range(2):
                for k in range(8):
                    t = mm(ps[b][:, m * 64:m * 64 + 64], hT[:, k, m * 128:(m + 1) * 128], rtr[:, l, k, :],
                           k == 0, k == 7, inc=(k == 7))
            lg = ps[b][:, 0:128].rearrange("p (m e) -> p m e", m=2)
            sc, sel, gm, wk = rtm[:, 0, :, :], rtm[:, 1, :, :], rtm[:, 2, :, 0:8], rtm[:, 3, :, :]
            t = afn(sc, lg, ACT.Exp, t, scale=-1.0)
            pr.rel(b, t)
            t = ts(dve, sc, sc, 1.0, None, ALU.add, None, t)
            t = dve.do(lambda e: e.reciprocal(sc, sc), t)
            t = tt(dve, sel, sc, bc(rtb[:, l, :], 2), ALU.add, t)
            for m in range(2):
                for g in range(8):
                    t1 = dve.do(lambda e, m=m, g=g: e.max(rt8[:, m, g, :], sel[:, m, g * 8:g * 8 + 8]), t)
            gs = rtG[:, :, 0:8]
            t = tt(dve, gs, rt8[:, :, :, 0], rt8[:, :, :, 1], ALU.add, t1, t_sent)
            for m in range(2):
                t1 = dve.do(lambda e, m=m: e.max(rt8[:, m, 0, :], gs[:, m, :]), t)
            t1 = dve.do(lambda e: e.memset(rt8[:, :, 0, 4:8], -2e38), t1)
            for m in range(2):
                t2 = dve.do(lambda e, m=m: e.match_replace(rtm[:, 4, m, 0:12], rt8[:, m, 0, :], rtG[:, m, :],
                                                           -3e38), t1)
            t = tt(dve, gm, rtm[:, 4, :, 0:8], gs, ALU.not_equal, t2)
            neg = rtm[:, 4, :, 16:24]
            t = ts(dve, neg, gm, 1e30, -1e30, ALU.mult, ALU.add, t)
            s4 = rtS[:, :, 0:64]
            for m in range(2):
                t1 = tt(dve, s4[:, m, :].rearrange("p (g e) -> p g e", e=8),
                        sel[:, m, :].rearrange("p (g e) -> p g e", e=8), inner(gm[:, m, :], 8), ALU.mult, t, t_sent)
            for m in range(2):
                t2 = tt(dve, s4[:, m, :].rearrange("p (g e) -> p g e", e=8),
                        s4[:, m, :].rearrange("p (g e) -> p g e", e=8), inner(neg[:, m, :], 8), ALU.add, t1)
            for m in range(2):
                t = dve.do(lambda e, m=m: e.max(rt8[:, m, 0, :], s4[:, m, :]), t2)
            t = dve.do(lambda e: e.memset(rt8[:, :, 0, 6:8], -2e38), t)
            wk66 = rtm[:, 3:6, :, :].rearrange("p a m e -> p (a m e)")
            for m in range(2):
                t1 = dve.do(lambda e, m=m: e.match_replace(wk66[:, 80 * m:80 * m + 66], rt8[:, m, 0, :],
                                                           rtS[:, m, :], -3e38), t)
            for m in range(2):
                t2 = tt(dve, sel[:, m, :], wk66[:, 80 * m:80 * m + 64], s4[:, m, :], ALU.not_equal, t1)
            t = tt(dve, sel, sel, sc, ALU.mult, t2)
            t = dve.do(lambda e: e.tensor_reduce(rt8[:, :, 1, 0:1], sel, AX.X, ALU.add), t)
            t = ts(dve, rt8[:, :, 1, 0:1], rt8[:, :, 1, 0:1], 1e-20, None, ALU.add, None, t)
            t = dve.do(lambda e: e.reciprocal(rt8[:, :, 1, 1:2], rt8[:, :, 1, 0:1]), t)
            for m in range(2):
                t1 = ts(dve, sel[:, m, :], sel[:, m, :], rt8[:, m, 1, 1:2], 2.5, ALU.mult, ALU.mult, t)
            b, free = pr.take()
            pe.wait(free, t1)
            for m in range(2):
                t = tr(ps[b][0:64, m * 128:(m + 1) * 128], sel[:, m, :], inc=(m == 1))
            t = copy(wT[:, :], ps[b][0:64, 0:256], t)
            pr.rel(b, t)
            return t

        def moe(l, t_h):
            meet()
            t_w = route(l, t_h)
            toks = take_y()
            gu = Ring((0, 1, 2))
            for i in (0, 1, 2):
                gu.free[i] = pr.free[i]
            wb = Ring((3,))
            wb.free[3] = pr.free[3]
            ws = Ring((0, 1))
            wsb = S(1, 8, 256)[:, 4:6, :]
            hr = Ring(range(4))
            sg = Ring(range(2))
            pend = []

            def finish(first, last):
                ud, h, t1 = pend.pop(0)
                t = down(ud, [hid[:, h, 0, :], hid[:, h, 1, :]], first, last, t1, toks if first else None)
                hr.rel(h, t)
                return t

            n = 0
            for e in range(-1, NE):
                if e < 0:
                    ug, uu = cols(A["sh_w_gate"][l], 0, 256), cols(A["sh_w_up"][l], 0, 256)
                    ud = rows(A["sh_w_down"][l], 0)
                else:
                    ug, uu = cols(A["moe_w_gate"][l, e], 0, 256), cols(A["moe_w_up"][l, e], 0, 256)
                    ud = rows(A["moe_w_down"][l, e], 0)
                    wi, free = wb.take()
                    t_b = mm(ps[3][:, 0:256], ident[0:64, e:e + 1].broadcast_to([64, 128]), wT[:, :], True, True,
                             free, t_w, inc=True)
                    wi, free = ws.take()
                    wv = wsb[:, wi, :]
                    t_b = afn(wv, ps[3][:, 0:256], ACT.Copy, t_b, free)
                    wb.rel(3, t_b)
                h, hfree = hr.take()
                for m in range(2):
                    b, free = gu.take()
                    pe.wait(ug.tok, uu.tok, free, t_h)
                    for half, u in ((0, ug), (1, uu)):
                        for k in range(8):
                            t = mm(ps[b][:, half * 256:half * 256 + 256], u.v[:, k, m * 128:m * 128 + 128],
                                   hT[:, k, :], k == 0, k == 7, inc=(k == 7))
                        if m == 1:
                            wr.rel(u.i, t)
                    s, sfree = sg.take()
                    t1 = afn(hsg[:, s, :], ps[b][:, 0:256], ACT.Silu, t, sfree)
                    if e < 0:
                        t2 = tt(dve, hid[:, h, m, :], ps[b][:, 256:512], hsg[:, s, :], ALU.mult, t1, hfree)
                        gu.rel(b, t2)
                        sg.rel(s, t2)
                    else:
                        t2 = tt(dve, hsg[:, s, :], ps[b][:, 256:512], hsg[:, s, :], ALU.mult, t1)
                        gu.rel(b, t2)
                        t2 = tt(dve, hid[:, h, m, :], wv, hsg[:, s, :], ALU.mult, t2, t_b, hfree)
                        sg.rel(s, t2)
                if e >= 0:
                    ws.rel(wi, t2)
                if pend:
                    finish(n == 0, False)
                    n += 1
                pend.append((ud, h, t2))
            t = finish(False, True)
            for i in (0, 1, 2):
                pr.free[i] = gu.free[i]
            pr.free[3] = wb.free[3]
            return t

        scr = nc.dram_tensor("scr_tab", [4, 512], F32, kind="Internal")
        s_tab = sem("s_tab")
        stat = sb("stat", [128, 4, 16])

        def softmax_T(score_b, n, col, t_s, dst):
            pass

        def even_mixer(t_h):
            w = A["ev_w_in"][0]
            qk = S(0, 8, 256)
            vt = S(1, 2, 512)
            gv = S(1, 4, 512)[:, 2:4, :]
            gqk = S(2, 8, 256)
            gg = S(3, 8, 256)
            glr = gqk[:, 4, :]
            gT = S(3, 8, 256)[:, 4:6, :]
            mix = S(4, 8, 256)
            P = S(5, 8, 256)
            PT = S(6, 8, 256)

            def to(dst, scale=1.0, a=True, n=512):
                def ev(p, t):
                    if a:
                        return afn(dst, p[:, 0:n], ACT.Copy, t, scale=scale)
                    return ts(dve, dst, p[:, 0:n], scale, None, ALU.mult, None, t)
                return ev

            def flat(v):
                return v.rearrange("p a b -> p (a b)")

            b, free = pr.take()
            t = mm(ps[b][0:4, :], rpe33[:, :], C("hot")[0:33, :], True, True, free, t_sm, t_in, inc=True)
            t = copy(rs_t[0:4, 0, :], ps[b][0:4, :], t)
            pr.rel(b, t)
            t = dma(pool, scr.ap(), rs_t[0:4, 0, :], s_tab, t)
            hank = S(7, 2, 4, 256)
            for qt in range(2):
                src = bass.AP(scr, 128 * (1 - qt), [[1, 128], [512, 4], [1, 256]])
                t_hk = dma(pool, hank[:, qt, :, :], src, s_tab, t)

            for i in range(2):
                proj_f(w, 256 * i, 256, hT, to(flat(qk[:, 2 * i:2 * i + 2, :]), 128 ** -0.5, i % 2 == 0), t_h)
            for i in range(2):
                proj_f(w, 512 + 256 * i, 256, hT, to(flat(qk[:, 4 + 2 * i:6 + 2 * i, :]), 1.0, i % 2 == 0), t_h)

            def to_t(dst, i):
                def ev(p, t):
                    return copy(dst[:, :, 256 * i:256 * i + 256], p[:, :].rearrange("p (m n) -> p m n", m=2), t)
                return ev

            for i in range(2):
                proj_t(w, 1024 + 256 * i, 256, hT, to_t(vt, i), t_h)
            proj_f(w, 1536, 256, hT, to(flat(gqk[:, 0:2, :]), 0.125), t_h)
            proj_f(w, 1792, 256, hT, to(flat(gqk[:, 2:4, :]), 1.0, False), t_h)
            for i in range(2):
                proj_t(w, 2048 + 256 * i, 256, hT, to_t(gv, i), t_h)
            for i in range(2):
                proj_f(w, 2560 + 256 * i, 256, hT, to(flat(gg[:, 2 * i:2 * i + 2, :]), 1.0, i % 2 == 0), t_h)
            proj_f(w, 3072, 16, hT, lambda p, t: copy(glr[0:16, :], p[0:16, 0:256], t), t_h)
            meet()

            for q in range(8):
                h, qt = q // 2, q % 2
                b, free = pr.take()
                mm(ps[b][:, 0:256], qk[:, h, qt * 128:qt * 128 + 128], qk[:, 4 + h, :], True, False, free)
                t = mm(ps[b][:, 0:256], flip, hank[:, qt, h, :], False, True, t_hk, inc=True)
                t = dve.do(lambda e, b=b, q=q: e.tensor_reduce(stat[:, 0, q:q + 1], ps[b][:, 0:256], AX.X,
                                                               ALU.max, negate=True), t)
                t = afn(P[:, q, :], ps[b][:, 0:256], ACT.Exp, t, bias=stat[:, 0, q:q + 1],
                        acc=stat[:, 1, q:q + 1])
                pr.rel(b, t)
                t = dve.do(lambda e, q=q: e.reciprocal(stat[:, 2, q:q + 1], stat[:, 1, q:q + 1]), t)
                ts(dve, P[:, q, :], P[:, q, :], stat[:, 2, q:q + 1], None, ALU.mult, None, t)
            for h in range(4):
                b, free = pr.take()
                pe.wait(free, dve.last())
                for kt in range(2):
                    for qt in range(2):
                        t = tr(ps[b][:, kt * 256 + qt * 128:kt * 256 + qt * 128 + 128],
                               P[:, 2 * h + qt, kt * 128:kt * 128 + 128], inc=(kt == 1 and qt == 1))
                t = copy(flat(PT[:, 2 * h:2 * h + 2, :]), ps[b][:, :], t)
                pr.rel(b, t)
            for h in range(4):
                b, free = pr.take()
                pe.wait(free, dve.last())
                for kt in range(2):
                    t = mm(ps[b][:, 0:256], vt[:, kt, h * 128:h * 128 + 128], PT[:, 2 * h + kt, :], kt == 0,
                           kt == 1, inc=(kt == 1))
                t = afn(mix[:, h, :], ps[b][:, 0:256], ACT.Copy, t)
                pr.rel(b, t)

            b, free = pr.take()
            for j in range(2):
                t = mm(ps[b][:, j * 256:j * 256 + 256], gkw2[:, j * 128:j * 128 + 128], glr[0:16, :], True, True,
                       free, inc=(j == 1))
            z, ez = S(8, 8, 256)[:, 0:2, :], S(8, 8, 256)[:, 2:4, :]
            bb, e2 = S(8, 8, 256)[:, 4:6, :], S(8, 8, 256)[:, 6:8, :]
            for j in range(2):
                t1 = ts(dve, z[:, j, :], ps[b][:, j * 256:j * 256 + 256], cv1("gkb", j), None, ALU.add, None, t,
                        t_cols)
            pr.rel(b, t1)
            t = afn(ez, z, ACT.Abs, t1)
            t = afn(ez, ez, ACT.Exp, t, scale=-1.0)
            t = afn(ez, ez, ACT.Ln, t, bias=one_c)
            t = ts(dve, z, z, 0.0, None, ALU.min, None, t)
            t = tt(dve, z, z, ez, ALU.subtract, t)
            t = ts(dve, z, z, 1.0 / 16, None, ALU.mult, None, t)
            fz, fb = flat(z), flat(bb)
            t = dve.do(lambda e: e.tensor_tensor_scan(fb, C("rset"), fz, 0.0, ALU.mult, ALU.add), t)
            b4 = bb.rearrange("p j (c i) -> p (j c) i", i=64)
            e4 = e2.rearrange("p j (c i) -> p (j c) i", i=64)
            t_e = tt(dve, e4, b4[:, :, 63:64].broadcast_to([128, 8, 64]), b4, ALU.subtract, t)
            dl = stat[:, 3, 0:8]
            t = afn(dl, b4[:, :, 63], ACT.Exp, t_e)
            t = afn(z, bb, ACT.Exp, t, t_e)
            t = afn(ez, bb, ACT.Exp, t, scale=-1.0)
            t = afn(e2, e2, ACT.Exp, t, t_e)
            qe, ke, kn = S(7, 8, 256)[:, 0:2, :], S(7, 8, 256)[:, 2:4, :], S(7, 8, 256)[:, 4:6, :]
            knt = S(7, 8, 256)[:, 6:8, :]
            meet()
            tt(dve, qe, gqk[:, 0:2, :], z, ALU.mult)
            tt(dve, ke, gqk[:, 2:4, :], ez, ALU.mult)
            t = tt(dve, kn, gqk[:, 2:4, :], e2, ALU.mult)
            b, free = pr.take()
            pe.wait(free, t)
            for m in range(2):
                for j in range(2):
                    t = tr(ps[b][:, m * 256 + j * 128:m * 256 + j * 128 + 128], kn[:, j, m * 128:m * 128 + 128],
                           inc=(m == 1 and j == 1))
            t = copy(flat(knt), ps[b][:, :], t)
            pr.rel(b, t)
            aT = S(6, 8, 128)
            for m in range(2):
                b, free = pr.take()
                pe.wait(free, dve.last())
                for h in (0, 2, 1, 3):
                    po, j = (h % 2) * 64, h // 2
                    t = mm(ps[b][:, h * 128:h * 128 + 128], ke[po:po + 64, j, m * 128:m * 128 + 128],
                           qe[po:po + 64, j, m * 128:m * 128 + 128], True, True, t if h == 1 else None,
                           inc=(h >= 2))
                meet()
                t = tt(dve, aT[:, 4 * m:4 * m + 4, :], ps[b][:, :].rearrange("p (h i) -> p h i", h=4),
                       bc(C("incl"), 4), ALU.mult, t)
                pr.rel(b, t)
            st = S(5, 8, 128)[:, 0:2, :]
            oT = S(5, 8, 256)[:, 4:8, :]
            meet()
            for c in range(4):
                m, off = c // 2, (c % 2) * 64
                b, free = pr.take()
                pe.wait(free, dve.last())
                for h in range(4):
                    po, j = (h % 2) * 64, h // 2
                    t = mm(ps[b][:, h * 64:h * 64 + 64], gv[off:off + 64, m, h * 128:h * 128 + 128],
                           aT[off:off + 64, 4 * m + h, off:off + 64], h == 0, c == 0, inc=(h == 3), skip=True)
                if c:
                    for h in (0, 2, 1, 3):
                        po, j = (h % 2) * 64, h // 2
                        t = mm(ps[b][:, h * 64:h * 64 + 64], st[po:po + 64, j, :],
                               qe[po:po + 64, j, c * 64:c * 64 + 64], False, True, t if h < 2 else None,
                               inc=(h >= 2), skip=True)
                t_o = afn(oT[:, :, c * 64:c * 64 + 64], ps[b][:, 0:256].rearrange("p (h i) -> p h i", h=4),
                          ACT.Copy, t)
                pr.rel(b, t_o)
                if c < 3:
                    b, free = pr.take()
                    pe.wait(free)
                    for h in range(4):
                        po, j = (h % 2) * 64, h // 2
                        t = mm(ps[b][po:po + 64, j * 128:j * 128 + 128],
                               knt[off:off + 64, m, h * 64:h * 64 + 64], gv[off:off + 64, m, h * 128:h * 128 + 128],
                               True, True, inc=True)
                    for j in range(2):
                        u = ps[b][:, j * 128:j * 128 + 128]
                        if c == 0:
                            t1 = copy(st[:, j, :], u, t)
                        else:
                            t1 = stt(st[:, j, :], st[:, j, :], dl[:, j * 4 + c:j * 4 + c + 1], u, ALU.mult,
                                     ALU.add, t)
                    pr.rel(b, t1)
            t = gated_norm(oT, gg, mix[:, 4:8, :], 4, cv1("evn"), t_o)
            meet()
            return out_proj(A["ev_w_out"][0], mix, t)

        def gated_norm(oT, gate, dst, n, wcol, tok):
            sq = S(8, 8, 256)
            t_s = afn(gate[:, 0:n, :], gate[:, 0:n, :], ACT.Silu, tok)
            t = afn(sq[:, 0:n, :], oT, ACT.Square, tok, t_s)
            for i in range(n // 2):
                b, free = pr.take()
                t1 = mm(ps[b][:, :], ones, sq[:, 2 * i:2 * i + 2, :], True, True, free, t, inc=True)
                r = sq[:, 2 * i:2 * i + 2, :].rearrange("p a b -> p (a b)")
                t2 = rsqrt(r, rs_t[:, i % 2, :], ps[b][:, :], 1.0 / 128, 1e-6, t1, dve.last())
                pr.rel(b, t2)
            t = stt(dst, oT, wcol, sq[:, 0:n, :], ALU.mult, ALU.mult, t2, t_cols)
            return tt(dve, dst, dst, gate[:, 0:n, :], ALU.mult, t, t_s)

        raw = misc[:, 0:3 * 518].rearrange("p (r m n) -> p r m n", r=3, m=2)
        gds = sb("gds", [128, 16, 16])
        t_raw = pool.do(lambda e: e.memset(raw[:, :, :, 0:3], 0.0))

        def delta_mixer(t_h):
            w = A["od_w_in"][0]
            qT, kT, vT, gate = S(0, 8, 256), S(1, 8, 256), S(2, 8, 256), S(3, 8, 256)
            rr = Ring(range(3))

            def flat(v):
                return v.rearrange("p a b -> p (a b)")

            ba = gds[:, 0:4, :].rearrange("p a b -> p (a b)")[:, 0:32].rearrange("p (m n) -> p m n", m=2)
            proj_t(w, 4096, 16, hT, lambda p, t: copy(ba, p[:, :].rearrange("p (m n) -> p m n", m=2)[:, :, 0:16], t),
                   t_h)
            be = gds[:, 4, :].rearrange("p (m n) -> p m n", m=2)
            gg = gds[:, 5, :].rearrange("p (m n) -> p m n", m=2)
            tz = gds[:, 6, :].rearrange("p (m n) -> p m n", m=2)
            ea = gds[:, 7, 0:8]
            t = afn(be, ba[:, :, 0:8], ACT.Exp, dve.last(), scale=-1.0)
            t = ts(dve, be, be, 1.0, None, ALU.add, None, t)
            t = dve.do(lambda e: e.reciprocal(be, be), t)
            t = tt(dve, gg, ba[:, :, 8:16], bc(adt[:, 1, :], 2), ALU.add, t)
            t = afn(tz, gg, ACT.Abs, t)
            t = afn(tz, tz, ACT.Exp, t, scale=-1.0)
            s1 = gds[:, 12, :].rearrange("p (m n) -> p m n", m=2)
            s2 = gds[:, 13, :].rearrange("p (m n) -> p m n", m=2)
            qq = gds[:, 14, :].rearrange("p (m n) -> p m n", m=2)
            t = ts(dve, s1, tz, 2.0, None, ALU.add, None, t)
            t = dve.do(lambda e: e.reciprocal(s1, s1), t)
            t = tt(dve, s1, s1, tz, ALU.mult, t)
            t = tt(dve, s2, s1, s1, ALU.mult, t)
            t = ts(dve, qq, s2, 1.0 / 15, None, ALU.mult, None, t)
            for n in (13, 11, 9, 7, 5, 3):
                t = stt(qq, qq, 1.0 / n, s2, ALU.add, ALU.mult, t)
            t = stt(qq, qq, 1.0, s1, ALU.add, ALU.mult, t)
            t = ts(dve, tz, qq, 2.0, None, ALU.mult, None, t)
            t = afn(ea, adt[:, 0, :], ACT.Exp, t)
            t = ts(dve, gg, gg, 0.0, None, ALU.max, None, t)
            t = tt(dve, gg, gg, tz, ALU.add, t)
            t = tt(dve, gg, gg, bc(ea, 2), ALU.mult, t)
            t_g = ts(dve, gg, gg, -1.0, None, ALU.mult, None, t)
            b, free = pr.take()
            pe.wait(free, t_g)
            for m in range(2):
                mm(ps[b][:, m * 8:m * 8 + 8], C("incl"), gg[:, m, :], True, True)
                mm(ps[b][:, 16 + m * 8:24 + m * 8], C("same"), gg[:, m, :], True, True)
            t = None
            for c in (0, 2, 1, 3):
                po = (c % 2) * 64
                t = mm(ps[b][:, 32 + c * 8:40 + c * 8], ones[po:po + 64, :], gg[po:po + 64, c // 2, :], True, True,
                       t if c == 1 else None, inc=(c >= 2))
            egc = gds[:, 8, :]
            een = gds[:, 9, :]
            DL = gds[:, 10:12, :].rearrange("p a b -> p (a b)")
            t1 = copy(egc, ps[b][:, 0:16], t)
            t1 = tt(dve, een, ps[b][:, 16:32], egc, ALU.subtract, t1)
            t1 = afn(egc, egc, ACT.Exp, t1)
            t1 = afn(een, een, ACT.Exp, t1)
            t1 = afn(DL, ps[b][:, 32:64], ACT.Exp, t1)
            pr.rel(b, t1)

            def conv(dst, j0):
                def ev(p, t):
                    r, free = rr.take()
                    t = afn(raw[:, r, :, 3:259], p[:, :].rearrange("p (m n) -> p m n", m=2), ACT.Copy, t, t_raw,
                            free)
                    tl = t
                    for m in range(2):
                        x = raw[:, r, m, :]
                        j = j0 + m
                        o = dst[:, m, :]
                        t1 = ts(dve, o, x[:, 0:256], colv[:, 0, j:j + 1], None, ALU.mult, None, t, t_cols)
                        for k in range(1, 4):
                            t1 = stt(o, x[:, k:k + 256], colv[:, 0, k * 24 + j:k * 24 + j + 1], o, ALU.mult,
                                     ALU.add, t1)
                    rr.rel(r, t1)
                    afn(dst, dst, ACT.Silu, t1)
                    return tl
                return ev

            for s, dst in ((0, qT), (1, kT), (2, vT)):
                for i in range(4):
                    proj_f(w, s * 1024 + 256 * i, 256, hT, conv(dst[:, 2 * i:2 * i + 2, :], s * 8 + 2 * i), t_h)
            for i in range(4):
                g = gate[:, 2 * i:2 * i + 2, :]
                proj_f(w, 3072 + 256 * i, 256, hT,
                       lambda p, t, g=g: afn(g, p[:, :].rearrange("p (m n) -> p m n", m=2), ACT.Copy, t), t_h)
            meet()
            sq, rn = S(4, 8, 256), S(5, 8, 256)
            for x, scale in ((qT, 128 ** -0.5), (kT, 1.0)):
                t = afn(sq, x, ACT.Square, dve.last(), pe.last())
                for i in range(4):
                    b, free = pr.take()
                    t1 = mm(ps[b][:, :], ones, sq[:, 2 * i:2 * i + 2, :], True, True, free, t, inc=True)
                    t2 = rsqrt(flat(rn[:, 2 * i:2 * i + 2, :]), rs_t[:, i % 2, :], ps[b][:, :], 1.0, 1e-6, t1,
                               dve.last())
                    pr.rel(b, t2)
                t = stt(x, x, scale, rn, ALU.mult, ALU.mult, t2)
            meet()
            kg, ke, vt = S(4, 16, 128), S(5, 16, 128), S(6, 16, 128)
            for i in range(4):
                b, free = pr.take()
                pe.wait(free)
                for j in range(4):
                    h, m = 2 * i + j // 2, j % 2
                    t = tr(ps[b][:, j * 128:j * 128 + 128], kT[:, h, m * 128:m * 128 + 128], inc=(j == 3))
                t = afn(flat(ke[:, 4 * i:4 * i + 4, :]), ps[b][:, :], ACT.Copy, t)
                pr.rel(b, t)
                for j in range(4):
                    h, m = 2 * i + j // 2, j % 2
                    g = 4 * i + j
                    t1 = ts(dve, kg[:, g, :], ke[:, g, :], egc[:, m * 8 + h:m * 8 + h + 1], None, ALU.mult, None,
                            t)
                    ts(dve, ke[:, g, :], ke[:, g, :], een[:, m * 8 + h:m * 8 + h + 1], None, ALU.mult, None, t1)
                b, free = pr.take()
                pe.wait(free)
                for j in range(4):
                    h, m = 2 * i + j // 2, j % 2
                    t = tr(ps[b][:, j * 128:j * 128 + 128], vT[:, h, m * 128:m * 128 + 128], inc=(j == 3))
                t = afn(flat(vt[:, 4 * i:4 * i + 4, :]), ps[b][:, :], ACT.Copy, t)
                pr.rel(b, t)
            meet()
            GM, DT = S(8, 4, 4, 128), S(2, 16, 128)
            for i in range(4):
                for j in range(4):
                    h, m = 2 * i + j // 2, j % 2
                    t = ts(dve, GM[:, i, j, :], C("after"), gg[:, m, h:h + 1], None, ALU.mult, None)
                b, free = pr.take()
                pe.wait(free, t)
                for j in range(4):
                    t = mm(ps[b][:, j * 128:j * 128 + 128], GM[:, i, j, :], C("incl"), True, True, inc=(j == 3))
                d4 = DT[:, 4 * i:4 * i + 4, :]
                t = afn(flat(d4), ps[b][:, :], ACT.Exp, t)
                pr.rel(b, t)
                tt(dve, d4, d4, bc(C("incl"), 4), ALU.mult, t)
            AT, QK = S(7, 16, 128), S(8, 16, 128)
            meet()
            for i in range(4):
                b, free = pr.take()
                b2, free2 = pr.take()
                pe.wait(free, free2)
                for j in range(4):
                    h, m = 2 * i + j // 2, j % 2
                    x = kT[:, h, m * 128:m * 128 + 128]
                    mm(ps[b][:, j * 128:j * 128 + 128], x, x, True, True)
                    t = mm(ps[b2][:, j * 128:j * 128 + 128], x, qT[:, h, m * 128:m * 128 + 128], True, True,
                           inc=(j == 3))
                for j in range(4):
                    h, m = 2 * i + j // 2, j % 2
                    g = 4 * i + j
                    t1 = stt(AT[:, g, :], ps[b][:, j * 128:j * 128 + 128], be[:, m, h:h + 1], DT[:, g, :],
                             ALU.mult, ALU.mult, t)
                t2 = tt(dve, flat(QK[:, 4 * i:4 * i + 4, :]), ps[b2][:, :], flat(DT[:, 4 * i:4 * i + 4, :]),
                        ALU.mult, t)
                pr.rel(b, t1)
                pr.rel(b2, t2)
            meet()
            for i in range(4):
                b, free = pr.take()
                pe.wait(free)
                for j in range(4):
                    h, m = 2 * i + j // 2, j % 2
                    t = mm(ps[b][:, j * 128:j * 128 + 128], gg[:, m, h:h + 1].broadcast_to([128, 128]), C("incl"),
                           True, True, inc=(j == 3))
                r = rs_t[:, i % 2, :]
                t = afn(r, ps[b][:, :], ACT.Exp, t, dve.last())
                pr.rel(b, t)
                x = flat(qT[:, 2 * i:2 * i + 2, :])
                t = tt(dve, x, x, r, ALU.mult, t)
            TM, TTm, PM = S(1, 16, 128), S(2, 16, 128), wP
            meet()
            for lv in range(6):
                M = C("level")[:, lv * 128:(lv + 1) * 128]
                tp = []
                for i in range(4):
                    b, free = pr.take()
                    pe.wait(free)
                    for j in range(4):
                        g = 4 * i + j
                        t = mm(ps[b][:, j * 128:j * 128 + 128], AT[:, g, :], ident if lv == 0 else TM[:, g, :],
                               True, True, inc=(j == 3))
                    t = tt(dve, PM[:, 4 * i:4 * i + 4, :], ps[b][:, :].rearrange("p (a b) -> p a b", a=4),
                           bc(M, 4), ALU.mult, t)
                    pr.rel(b, t)
                    tp.append(t)
                for i in range(4):
                    b, free = pr.take()
                    b2, free2 = pr.take()
                    pe.wait(free, free2, tp[i])
                    for j in range(4):
                        g = 4 * i + j
                        mm(ps[b][:, j * 128:j * 128 + 128], ident if lv == 0 else TTm[:, g, :], PM[:, g, :], True,
                           True)
                        t = mm(ps[b2][:, j * 128:j * 128 + 128], PM[:, g, :], ident if lv == 0 else TTm[:, g, :],
                               True, True, inc=(j == 3))
                    for bb, X in ((b, TM), (b2, TTm)):
                        o = X[:, 4 * i:4 * i + 4, :]
                        old = bc(ident, 4) if lv == 0 else o
                        t1 = tt(dve, o, old, ps[bb][:, :].rearrange("p (a b) -> p a b", a=4), ALU.subtract, t)
                        pr.rel(bb, t1)
                pe.wait(dve.last())
            KC = S(7, 16, 128)
            meet()
            for i in range(4):
                b, free = pr.take()
                pe.wait(free)
                for j in range(4):
                    g = 4 * i + j
                    t = mm(ps[b][:, j * 128:j * 128 + 128], kg[:, g, :], TTm[:, g, :], True, True, inc=(j == 3))
                t = afn(flat(KC[:, 4 * i:4 * i + 4, :]), ps[b][:, :], ACT.Copy, t, scale=-1.0)
                pr.rel(b, t)
            meet()
            st = S(1, 8, 128)
            vn = S(4, 8, 128)
            oT = PM.rearrange("p a b -> p (a b)").rearrange("p (a b) -> p a b", b=256)
            for c in range(4):
                m, off = c // 2, (c % 2) * 64
                vb = []
                for i in range(2):
                    b, free = pr.take()
                    pe.wait(free, dve.last())
                    for j in range(4):
                        h = 4 * i + j
                        o = ps[b][off:off + 64, j * 128:j * 128 + 128]
                        t = mm(o, TTm[:, 2 * h + m, off:off + 64], vt[:, 2 * h + m, :], True, c == 0, inc=True)
                        if c:
                            t = mm(o, KC[:, 2 * h + m, off:off + 64], st[:, h, :], False, True, inc=True)
                    t = tt(dve, vn[off:off + 64, 4 * i:4 * i + 4, :],
                           ps[b][off:off + 64, :].rearrange("p (a b) -> p a b", a=4),
                           inner(be[off:off + 64, m, 4 * i:4 * i + 4], 128), ALU.mult, t)
                    pr.rel(b, t)
                    vb.append(t)
                b, free = pr.take()
                pe.wait(free, vb)
                for h in range(8):
                    o = ps[b][:, h * 64:h * 64 + 64]
                    t = mm(o, vn[off:off + 64, h, :], QK[off:off + 64, 2 * h + m, off:off + 64], True, c == 0,
                           inc=True)
                    if c:
                        t = mm(o, st[:, h, :], qT[:, h, c * 64:c * 64 + 64], False, True, inc=True)
                t_o = afn(oT[:, :, c * 64:c * 64 + 64], ps[b][:, :].rearrange("p (h i) -> p h i", h=8), ACT.Copy, t)
                pr.rel(b, t_o)
                if c < 3:
                    for i in range(2):
                        b, free = pr.take()
                        pe.wait(free)
                        for j in range(4):
                            h = 4 * i + j
                            t = mm(ps[b][:, j * 128:j * 128 + 128], ke[off:off + 64, 2 * h + m, :],
                                   vn[off:off + 64, h, :], True, True, inc=(j == 3))
                        for j in range(4):
                            h = 4 * i + j
                            u = ps[b][:, j * 128:j * 128 + 128]
                            if c == 0:
                                t1 = copy(st[:, h, :], u, t)
                            else:
                                t1 = stt(st[:, h, :], st[:, h, :], DL[:, c * 8 + h:c * 8 + h + 1], u, ALU.mult,
                                         ALU.add, t)
                        pr.rel(b, t1)
            mix = S(0, 8, 256)
            meet()
            t = gated_norm(oT, gate, mix, 8, cv1("odn"), t_o)
            meet()
            return out_proj(A["od_w_out"][0], mix, t)

        wP = sb("wP", [128, 16, 128])
        kc_x = sb("kc_x", [128, 2, 512])

        def rms_mod(src, base, gi, tok, dst, mcols=None):
            u, sq = S(8, 8, 256), S(7, 8, 256)
            t = afn(sq, src, ACT.Square, tok)
            b, t = col_sum(sq, 8, None, t)
            t = rsqrt(rs_t[:, 0, 0:256], rs_t[:, 1, 0:256], ps[b][:, 0:256], 1.0 / D, 1e-6, t)
            pr.rel(b, t)
            t = tt(dve, u, src, bc(rs_t[:, 0, 0:256], 8), ALU.mult, t, tok)
            for j in range(8):
                if mcols is None:
                    sc, sh = mc(base, 1, j), mc(base, 0, j)
                else:
                    sc, sh = mcols[:, 1, j:j + 1], mcols[:, 0, j:j + 1]
                t1 = ts(dve, u[:, j, :], u[:, j, :], vc(gi, j), sc, ALU.mult, ALU.mult, t, t_sm)
                t2 = ts(dve, dst[:, j, :], u[:, j, :], sh, None, ALU.add, None, t1)
            return t2

        s_cx = sem("s_cx")

        def attn_layer(t_x):
            w = A["ev_w_in_2"][0]
            free = meet()
            cin = S(6, 2, 1024)
            t = dma(pool, cin, A["ctx_2"][0].rearrange("(t p) n -> p t n", p=128), s_cx, *free)
            cT, hc = S(5, 8, 256), S(4, 8, 256)
            t = to_features(cin, cT, t)
            t_c = rms_mod(cT, 12, 8, t, hc, modc)
            meet()
            t_h = rms_mod(xT[:, :, :], 12, 8, t_x, hT)
            meet()

            def flat(v):
                return v.rearrange("p a b -> p (a b)")

            q = S(0, 8, 256)
            kk = S(1, 8, 256)
            v = S(2, 4, 256)
            av, ag = S(2, 8, 256)[:, 4:6, :], S(2, 8, 256)[:, 6:8, :]
            bg = S(3, 8, 256)

            def to(dst):
                return lambda p, t: afn(flat(dst), p[:, :], ACT.Copy, t)

            proj_f(w, 0, 256, hT, to(av), t_h)
            proj_f(w, 256, 256, hT, to(ag), t_h)
            for i in range(3):
                proj_f(w, 512 + 256 * i, 256, hT, to(q[:, 2 * i:2 * i + 2, :]), t_h)
            for c0, dst in ((1280, kk), (1536, None)):
                u = cols(w, c0, 256)
                for src, o in ((hc, 0), (hT, 1)):
                    b, free = pr.take()
                    pe.wait(u.tok, free, t_h, t_c)
                    for m in range(2):
                        for k in range(8):
                            a1 = u.v[:, k, m * 128:m * 128 + 128] if dst is not None else \
                                src[:, k, m * 128:m * 128 + 128]
                            a2 = src[:, k, :] if dst is not None else u.v[:, k, :]
                            t = mm(ps[b][:, m * 256:m * 256 + 256], a1, a2, k == 0, k == 7, inc=(k == 7))
                    if dst is not None:
                        t1 = copy(flat(kk[:, 2 * o:2 * o + 2, :]), ps[b][:, :], t)
                    else:
                        t1 = copy(flat(v[:, 2 * o:2 * o + 2, :]), ps[b][:, :], t)
                    pr.rel(b, t1)
                wr.rel(u.i, t)
            for i in range(3):
                proj_f(w, 1792 + 256 * i, 256, hT, to(bg[:, 2 * i:2 * i + 2, :]), t_h)
            meet()
            sq = S(7, 8, 256)
            rn = S(6, 8, 256)
            for x, n, nm in ((q, 6, "qn"), (kk, 4, "kn")):
                t = afn(sq[:, 0:n, :], x[:, 0:n, :], ACT.Square, dve.last(), pe.last())
                for i in range(n // 2):
                    b, free = pr.take()
                    t1 = mm(ps[b][:, :], ones, sq[:, 2 * i:2 * i + 2, :], True, True, free, t, inc=True)
                    t2 = rsqrt(flat(rn[:, 2 * i:2 * i + 2, :]), rs_t[:, i % 2, :], ps[b][:, :], 1.0 / 128, 1e-6,
                               t1, dve.last())
                    pr.rel(b, t2)
                t = stt(x[:, 0:n, :], x[:, 0:n, :], cv1(nm), rn[:, 0:n, :], ALU.mult, ALU.mult, t2)
            meet()
            for x, j in [(q, j) for j in range(6)] + [(kk, 2), (kk, 3)]:
                b, free = pr.take()
                t = mm(ps[b][:, 0:256], C("rot"), x[:, j, :], True, True, free, t_c2, inc=True)
                t = tt(dve, ps[b][:, 256:512], ps[b][:, 0:256], C("sinr"), ALU.mult, t)
                t1 = tt(dve, x[:, j, :], x[:, j, :], C("cosr"), ALU.mult, t)
                t = tt(dve, x[:, j, :], x[:, j, :], ps[b][:, 256:512], ALU.add, t1)
                pr.rel(b, t)
            t = None
            kr = wP[:, 0:8, :].rearrange("p a b -> p (a b)").rearrange("p (g n) -> p g n", g=2)
            for g in range(2):
                copy(kr[:, g, 0:256], kk[:, g, :], dve.last())
                t = copy(kr[:, g, 256:512], kk[:, 2 + g, :])
            mix = S(7, 8, 256)
            meet()
            P = S(4, 4, 512)
            PT = S(5, 2, 4, 256)
            scale = 128 ** -0.5
            for hp in range(3):
                for i in range(4):
                    h, qt = 2 * hp + i // 2, i % 2
                    b, free = pr.take()
                    t = mm(ps[b][:, :], q[:, h, qt * 128:qt * 128 + 128], kr[:, h // 3, :], True, True, free,
                           inc=True)
                    t = dve.do(lambda e, b=b, i=i: e.tensor_reduce(stat[:, 0, i:i + 1], ps[b][:, :], AX.X,
                                                                   ALU.max), t)
                    t = ts(dve, stat[:, 0, i:i + 1], stat[:, 0, i:i + 1], -scale, None, ALU.mult, None, t)
                    t = afn(P[:, i, :], ps[b][:, :], ACT.Exp, t, pe.last(), bias=stat[:, 0, i:i + 1], scale=scale,
                            acc=stat[:, 1, i:i + 1])
                    pr.rel(b, t)
                    t = dve.do(lambda e, i=i: e.reciprocal(stat[:, 2, i:i + 1], stat[:, 1, i:i + 1]), t)
                    tp = ts(dve, P[:, i, :], P[:, i, :], stat[:, 2, i:i + 1], None, ALU.mult, None, t)
                for i in range(2):
                    for k2 in range(2):
                        b, free = pr.take()
                        pe.wait(free, tp)
                        for kt in range(2):
                            for qt in range(2):
                                t = tr(ps[b][:, kt * 256 + qt * 128:kt * 256 + qt * 128 + 128],
                                       P[:, 2 * i + qt, (2 * k2 + kt) * 128:(2 * k2 + kt) * 128 + 128],
                                       inc=(kt == 1 and qt == 1))
                        t = copy(flat(PT[:, i, 2 * k2:2 * k2 + 2, :]), ps[b][:, :], t)
                        pr.rel(b, t)
                for i in range(2):
                    h = 2 * hp + i
                    b, free = pr.take()
                    pe.wait(free, dve.last())
                    for kt in range(4):
                        t = mm(ps[b][:, 0:256], v[:, kt, (h // 3) * 128:(h // 3) * 128 + 128], PT[:, i, kt, :],
                               kt == 0, kt == 3, inc=(kt == 3))
                    t = afn(mix[:, 2 + h, :], ps[b][:, 0:256], ACT.Copy, t)
                    pr.rel(b, t)
            meet()
            cs = S(6, 2, 272)
            dd = S(5, 2, 256)
            t = dve.do(lambda e: e.memset(cs[:, :, 0:9], 0.0))
            for j in range(2):
                t = dve.do(lambda e, j=j: e.tensor_tensor_scan(cs[:, j, 9:265], ones[:, 0:1].broadcast_to([128, 256]),
                                                               av[:, j, :], 0.0, ALU.mult, ALU.add), t)
            for j in range(2):
                t = copy(cs[:, j, 265:272], cs[:, j, 264:265].broadcast_to([128, 7]), t)
            for g, wd in enumerate((2, 4, 8, 16)):
                j, po, hw = g // 2, (g % 2) * 64, wd // 2
                t1 = tt(dve, dd[po:po + 64, j, :], cs[po:po + 64, j, 8 + hw:264 + hw],
                        cs[po:po + 64, j, 8 - hw:264 - hw], ALU.subtract, t)
            t1 = tt(dve, flat(dd), flat(dd), C("icnt"), ALU.mult, t1)
            t1 = tt(dve, dd, dd, av, ALU.subtract, t1)
            b, free = pr.take()
            pe.wait(free, t1)
            t = None
            for g in (0, 2, 1, 3):
                j, po = g // 2, (g % 2) * 64
                t = mm(ps[b][po:po + 64, j * 256:j * 256 + 256], poolw[po:po + 64, j, :], dd[po:po + 64, j, :],
                       True, True, t if g == 1 else None, inc=(g >= 2))
            for j in range(2):
                t1 = ts(dve, mix[:, j, :], ps[b][:, j * 256:j * 256 + 256], cv1("psc", j), None, ALU.mult, None, t)
            pr.rel(b, t1)
            t = afn(ag, ag, ACT.Silu)
            t = afn(bg[:, 0:6, :], bg[:, 0:6, :], ACT.Silu)
            t = tt(dve, mix[:, 0:2, :], mix[:, 0:2, :], ag, ALU.mult, t, t1)
            t = tt(dve, mix[:, 2:8, :], mix[:, 2:8, :], bg[:, 0:6, :], ALU.mult, t)
            meet()
            t_y = out_proj(A["ev_w_out_2"][0], mix, t)
            for j in range(8):
                t = stt(xT[:, j, :], Y(j), mc(12, 2, j), xT[:, j, :], ALU.mult, ALU.add, t_y)
            give_y(t)
            return t

        raw3 = misc[:, 0:2 * 516].rearrange("p (r m n) -> p r m n", r=2, m=2)
        s_w3 = sem("s_hw3")
        hd = misc[0:64, 0:1536].rearrange("p (a n) -> p a n", a=6)
        nrm = sb("nrm", [128, 2, 12])

        def sin_layer(dst, src, bi, tok):
            x, k = hd[:, 4, :], hd[:, 5, :]
            fr = colv[0:64, 2, 2:3]
            t = ts(dve, x, src, colv[0:64, 2, bi:bi + 1], fr, ALU.add, ALU.mult, tok, t_cols)
            big = 12582912.0
            t = ts(dve, k, x, 1.0 / (2 * math.pi), big, ALU.mult, ALU.add, t)
            t = ts(dve, k, k, big, None, ALU.subtract, None, t)
            c1 = 6.28125
            c2 = float(np.float32(2 * math.pi - c1))
            t = stt(x, k, -c1, x, ALU.mult, ALU.add, t)
            t = stt(x, k, -c2, x, ALU.mult, ALU.add, t)
            pi = 3.1415925
            t = ts(dve, x, x, pi, -pi, ALU.min, ALU.max, t)
            return afn(dst, x, ACT.Sin, t)

        def hyena_layer(t_x):
            w = A["od_w_in_2"][0]
            fr = meet()
            w3 = wP[0:64, :, :].rearrange("p a b -> p (a b)")
            w3b = kc_x[0:64, :, :].rearrange("p a b -> p (a b)")
            dma(pool, w3, A["hy_w3_2"][0][:, 0:2048], s_w3, *fr)
            t_w3 = dma(pool, w3b, A["hy_w3_2"][0][:, 2048:3072], s_w3, *fr)
            t_h = rms_mod(xT[:, :, :], 15, 9, t_x, hT)
            meet()

            def flat(v):
                return v.rearrange("p a b -> p (a b)")

            b, free = pr.take()
            t = mm(ps[b][0:64, 0:256], hw12[0:33, 0, :], C("emb")[0:33, :], True, True, free, t_c2, inc=True)
            t = sin_layer(hd[:, 0, :], ps[b][0:64, 0:256], 0, t)
            pr.rel(b, t)
            b, free = pr.take()
            t = mm(ps[b][0:64, 0:256], hw12[:, 1, :], hd[:, 0, :], True, True, free, t, inc=True)
            t = sin_layer(hd[:, 1, :], ps[b][0:64, 0:256], 1, t)
            pr.rel(b, t)
            hs, hdif = [S(0, 1536), S(1, 1536)], [S(2, 1536), S(3, 1536)]
            fa, fb = S(7, 1536), S(8, 1536)
            dec = C("dec")
            nb, nfree = pr.take()
            first = True
            pe.wait(nfree, t, t_w3)
            onec = one_c
            for m in range(2):
                meet()
                for o in range(2):
                    for dr in range(2):
                        dst = (fa if dr == 0 else fb)[:, o * 768:o * 768 + 768]
                        for hf in range(2):
                            c0 = o * 1536 + dr * 768 + hf * 384
                            b, free = pr.take()
                            if b == nb:
                                pr.rel(b, *free)
                                b, free = pr.take()
                            pe.wait(free)
                            lhs = hd[:, 1, m * 128:m * 128 + 128]
                            parts = [(c0, c0 + 384)] if c0 + 384 <= 2048 or c0 >= 2048 else \
                                [(c0, 2048), (2048, c0 + 384)]
                            for (a0, a1) in parts:
                                rhs = w3[:, a0:a1] if a1 <= 2048 else w3b[:, a0 - 2048:a1 - 2048]
                                t = mm(ps[b][:, a0 - c0:a1 - c0], lhs, rhs, True, True, inc=True)
                            t = tt(dve, dst[:, hf * 384:hf * 384 + 384], ps[b][:, 0:384],
                                   dec[:, m * 768 + hf * 384:m * 768 + hf * 384 + 384], ALU.mult, t, t_c2)
                            pr.rel(b, t)
                ab = S(6, 1536)
                for f, x in enumerate((fa, fb)):
                    t = afn(ab, x, ACT.Abs, dve.last(), pe.last())
                    pe.wait(t)
                    for g in range(12):
                        lst = m == 1 and f == 1 and g == 11
                        t = mm(ps[nb][:, g:g + 1], ab[:, g * 128:g * 128 + 128], onec, first and g == 0, lst,
                               inc=(g == 11), skip=True)
                    first = False
                if m == 0:
                    t = dve.do(lambda e: e.memset(fb[0:1, :], 0.0), t)
                t = tt(dve, hs[m], fa, fb, ALU.add, t)
                t = tt(dve, hdif[m], fa, fb, ALU.subtract, t)
            t = ts(dve, nrm[:, 0, :], ps[nb][:, 0:12], 1e-6, None, ALU.add, None, pe.last())
            t = dve.do(lambda e: e.reciprocal(nrm[:, 1, :], nrm[:, 0, :]), t)
            pr.rel(nb, t)
            meet()
            KR = [S(4, 1536), S(5, 1536)]
            KI = [S(6, 1536), S(7, 1536)]
            DC = C("dc").rearrange("p (a b) -> p a b", a=2)
            DS = C("ds").rearrange("p (a b) -> p a b", a=2)
            for f in range(2):
                for mat, src, dst, sc in ((DC, hs, KR, 1.0), (DS, hdif, KI, -1.0)):
                    for c in range(3):
                        b, free = pr.take()
                        pe.wait(free)
                        for m in range(2):
                            t = mm(ps[b][:, :], mat[:, m, f * 128:f * 128 + 128], src[m][:, c * 512:c * 512 + 512],
                                   m == 0, m == 1, inc=(m == 1))
                        t = afn(dst[f][:, c * 512:c * 512 + 512], ps[b][:, :], ACT.Copy, t, scale=sc)
                        pr.rel(b, t)
            meet()
            t_r3 = pool.do(lambda e: e.memset(misc[:, 0:1032], 0.0))
            z = S(0, 8, 256)
            x1, x2 = S(1, 8, 256), S(2, 8, 256)
            gt = S(3, 8, 256)
            r3 = Ring(range(2))

            def conv3(dst, j0):
                def ev(p, t):
                    r, free = r3.take()
                    t = afn(raw3[:, r, :, 1:257], p[:, :].rearrange("p (m n) -> p m n", m=2), ACT.Copy, t, t_r3,
                            free)
                    for m in range(2):
                        x = raw3[:, r, m, :]
                        j = j0 + m
                        t1 = ts(dve, dst[:, m, :], x[:, 0:256], cv1("hcw", j), cv1("hcb", j), ALU.mult, ALU.add,
                                t)
                        for k in (1, 2):
                            t1 = stt(dst[:, m, :], x[:, k:k + 256], cv1("hcw", k * 18 + j), dst[:, m, :],
                                     ALU.mult, ALU.add, t1)
                    r3.rel(r, t1)
                    return t
                return ev

            for s, dst in ((0, z), (1, x1), (2, x2)):
                for i in range(3):
                    proj_f(w, s * 768 + 256 * i, 256, hT, conv3(dst[:, 2 * i:2 * i + 2, :], s * 6 + 2 * i), t_h)
            for i in range(3):
                g = gt[:, 2 * i:2 * i + 2, :]
                proj_f(w, 2304 + 256 * i, 256, hT,
                       lambda p, t, g=g: afn(g, p[:, :].rearrange("p (m n) -> p m n", m=2), ACT.Silu, t), t_h)
            fin = z[:, 6:8, :]
            proj_f(w, 3072, 256, hT, lambda p, t: copy(flat(fin), p[:, :], t), t_h)
            g = gt[:, 6:8, :]
            proj_f(w, 3328, 256, hT, lambda p, t: afn(flat(g), p[:, :], ACT.Silu, t), t_h)
            meet()
            CT = C("dct").rearrange("p (a b) -> p a b", a=2)
            ST = C("dst").rearrange("p (a b) -> p a b", a=2)
            zt = wP[:, 0:12, :].rearrange("p a b -> p (a b)").rearrange("p (m n) -> p m n", m=2)
            ZR, ZI = S(8, 2048)[:, 0:768], S(8, 2048)[:, 768:1536]
            tmp = kc_x[:, :, :].rearrange("p a b -> p (a b)")[:, 0:768]
            YR = [hT[:, :, :].rearrange("p a b -> p (a b)")[:, 0:768],
                  hT[:, :, :].rearrange("p a b -> p (a b)")[:, 768:1536]]
            YI = [yib[:, 0, :], yib[:, 1, :]]
            for o in range(2):
                for j in range(6):
                    b, free = pr.take()
                    pe.wait(free)
                    for m in range(2):
                        t = tr(ps[b][:, m * 128:m * 128 + 128], z[:, j, m * 128:m * 128 + 128], inc=(m == 1))
                    t = copy(zt[:, :, j * 128:j * 128 + 128], ps[b][:, 0:256].rearrange("p (m n) -> p m n", m=2), t)
                    pr.rel(b, t)
                meet()
                for f in range(2):
                    for mat, dst, sc in ((DC, ZR, 1.0), (DS, ZI, -1.0)):
                        for c in range(2):
                            b, free = pr.take()
                            pe.wait(free)
                            for m in range(2):
                                t = mm(ps[b][:, 0:384], mat[:, m, f * 128:f * 128 + 128],
                                       zt[:, m, c * 384:c * 384 + 384], m == 0, m == 1, inc=(m == 1))
                            t = afn(dst[:, c * 384:c * 384 + 384], ps[b][:, 0:384], ACT.Copy, t, dve.last(),
                                    scale=sc)
                            pr.rel(b, t)
                    kr, ki = KR[f][:, o * 768:o * 768 + 768], KI[f][:, o * 768:o * 768 + 768]
                    t = tt(dve, YR[f], ZR, kr, ALU.mult, t)
                    t = tt(dve, tmp, ZI, ki, ALU.mult, t)
                    t = tt(dve, YR[f], YR[f], tmp, ALU.subtract, t)
                    t = tt(dve, YI[f], ZR, ki, ALU.mult, t)
                    t = tt(dve, tmp, ZI, kr, ALU.mult, t)
                    t = tt(dve, YI[f], YI[f], tmp, ALU.add, t)
                meet()
                gx = x1 if o == 0 else x2
                for j in range(6):
                    b, free = pr.take()
                    pe.wait(free)
                    for f in range(2):
                        mm(ps[b][:, 0:256], YR[f][:, j * 128:j * 128 + 128], CT[:, f, :], f == 0, False)
                        t = mm(ps[b][:, 0:256], YI[f][:, j * 128:j * 128 + 128], ST[:, f, :], False, f == 1,
                               inc=(f == 1))
                    r = rs_t[:, j % 2, 0:256]
                    t = afn(r, ps[b][:, 0:256], ACT.Copy, t, dve.last(), scale=nrm[:, 1, o * 6 + j:o * 6 + j + 1])
                    pr.rel(b, t)
                    t = stt(z[:, j, :], z[:, j, :], cv1("skip", o * 6 + j), r, ALU.mult, ALU.add, t)
                    t = tt(dve, z[:, j, :], z[:, j, :], gx[:, j, :], ALU.mult, t)
                meet()
            FC = C("fc").rearrange("p (a b) -> p a b", a=2)
            FS = C("fs").rearrange("p (a b) -> p a b", a=2)
            PQ = S(1, 8, 256)
            for m in range(2):
                for q, mat in ((0, FC), (1, FS)):
                    b, free = pr.take()
                    pe.wait(free)
                    for c in range(2):
                        t = mm(ps[b][:, 0:256], fin[:, c, m * 128:m * 128 + 128], mat[:, c, :], c == 0, c == 1,
                               inc=(c == 1))
                    t = afn(PQ[:, 2 * q + m, :], ps[b][:, 0:256], ACT.Copy, t, scale=1.0 if q == 0 else -1.0)
                    pr.rel(b, t)
            yt = S(2, 8, 256)
            pe.wait(t)
            for j in range(2):
                b, free = pr.take()
                pe.wait(free)
                n = 0
                for q, mat in ((0, FC), (1, FS)):
                    for m in range(2):
                        t = mm(ps[b][:, 0:256], PQ[:, 2 * q + m, j * 128:j * 128 + 128], mat[:, m, :], n == 0,
                               n == 3, inc=(n == 3))
                        n += 1
                t = afn(yt[:, j, :], ps[b][:, 0:256], ACT.Copy, t, scale=1.0 / 256)
                pr.rel(b, t)
            u = unit(A["fn_w_2"][0].rearrange("(k p) n -> p k n", p=128), 2, 256)
            for j in range(2):
                b, free = pr.take()
                pe.wait(free, u.tok, act.last())
                for c in range(2):
                    t = mm(ps[b][:, 0:256], u.v[:, c, j * 128:j * 128 + 128], yt[:, c, :], c == 0, c == 1,
                           inc=(c == 1))
                t1 = tt(dve, z[:, 6 + j, :], ps[b][:, 0:256], gt[:, 6 + j, :], ALU.mult, t)
                pr.rel(b, t1)
            wr.rel(u.i, t)
            t = tt(dve, z[:, 0:6, :], z[:, 0:6, :], gt[:, 0:6, :], ALU.mult, t1)
            meet()
            t_y = out_proj(A["od_w_out_2"][0], z, t)
            for j in range(8):
                t = stt(xT[:, j, :], Y(j), mc(15, 2, j), xT[:, j, :], ALU.mult, ALU.add, t_y)
            give_y(t)
            return t

        yib = misc[:, 0:1536].rearrange("p (a n) -> p a n", a=2)

        def whole():
            t_m = modulate(A["ada_w"][0], 6, 0)
            t_h = scale_shift(hT, xT, lambda j: mc(0, 1, j), lambda j: mc(0, 0, j), t_m, t_x)
            if STOP == "h0":
                return t_h
            t_y = even_mixer(t_h)
            modulate(A["ada_w"][1], 6, 6) if False else None
            t_h = residual(0, 2, t_y, 0, 0, 0, 3)
            if STOP == "x1":
                return t_h
            t_y = moe(0, t_h)
            t_m = None
            t_h = residual(0, 5, t_y, 4, 0, None, 0)
            t_m = modulate(A["ada_w"][1], 6, 6)
            t_h = scale_shift(hT, xT, lambda j: mc(6, 1, j), lambda j: mc(6, 0, j), t_m, t_h)
            if STOP == "x2":
                return t_h
            t_y = delta_mixer(t_h)
            t_h = residual(6, 2, t_y, 0, 1, 6, 3)
            if STOP == "x3":
                return t_h
            t_y = moe(1, t_h)
            t_xx = residual(6, 5, t_y, 4, 1, None, 0)
            if STOP == "x4":
                return t_xx
            modulate(A["w_mod_2"][0], 3, 12, True)
            t_xx = attn_layer(t_xx)
            if STOP == "x5":
                return t_xx
            modulate(A["w_mod_2"][1], 3, 15)
            return hyena_layer(t_xx)

        t_end = whole()
        meet()
        u, sq = S(8, 8, 256), S(7, 8, 256)
        if STOP is None:
            t = afn(sq, xT[:, :, :], ACT.Square, t_end)
            b, t = col_sum(sq, 8, None, t)
            t = rsqrt(rs_t[:, 0, 0:256], rs_t[:, 1, 0:256], ps[b][:, 0:256], 1.0 / D, 1e-6, t)
            pr.rel(b, t)
            t = tt(dve, u, xT[:, :, :], bc(rs_t[:, 0, 0:256], 8), ALU.mult, t)
            for j in range(8):
                t1 = ts(dve, u[:, j, :], u[:, j, :], vc(10, j), None, ALU.mult, None, t, t_sm)
            t = t1
        else:
            t = copy(u, xT[:, :, :], t_end)
        xo = S(6, 2, 1024)
        for m in range(2):
            for k2 in range(2):
                b, free = pr.take()
                pe.wait(free, t)
                for kk in range(4):
                    tp = tr(ps[b][:, kk * 128:kk * 128 + 128], u[:, 4 * k2 + kk, m * 128:m * 128 + 128],
                            inc=(kk == 3))
                o = xo[:, m, :].rearrange("p (f k) -> p k f", k=8)[:, 4 * k2:4 * k2 + 4, :]
                t1 = copy(o, ps[b][:, :].rearrange("p (k f) -> p k f", k=4), tp)
                pr.rel(b, t1)
        s_out = sem("s_out")
        t = dma(sp, out[0].rearrange("(t p) n -> p t n", p=128), xo, s_out, t1)
        sp.wait(t)

        block = ctx.enter_context(nc.Block())

        @block.sync
        def _(e):
            sp.emit(e)

        @block.gpsimd
        def _(e):
            pool.emit(e)

        @block.scalar
        def _(e):
            act.emit(e)

        @block.vector
        def _(e):
            dve.emit(e)

        @block.tensor
        def _(e):
            pe.emit(e)


def kernel(**inputs):
    import numpy as _np
    import concourse.bacc as _bacc
    from concourse import mybir as _mybir
    from concourse.bass_utils import run_bass_kernel_spmd as _run

    nc = _bacc.Bacc("TRN2", target_bir_lowering=False, num_devices=1)
    consts, at, lo = shape_constants()
    arrays, args = {}, {}
    for name, a in list(inputs.items()) + [("consts", consts)]:
        a = _np.ascontiguousarray(a)
        arrays[f"in_{name}"] = a
        args[name] = nc.dram_tensor(f"in_{name}", a.shape, _mybir.dt.from_np(a.dtype), kind="ExternalInput").ap()
    o = nc.dram_tensor("out_0", (1, 256, 1024), _mybir.dt.float32, kind="ExternalOutput").ap()
    build(nc, args, o, at, lo)
    r = _run(nc, [arrays], core_ids=[0])
    return r.results[0]["out_0"]
```

```python
import math
from contextlib import ExitStack

import numpy as np

import concourse.bass as bass
from concourse import mybir

F32 = mybir.dt.float32
ACT = mybir.ActivationFunctionType
ALU = mybir.AluOpType
AX = mybir.AxisListType

D = 1024
T = 256
NE = 64
ALPHA = float(4 ** 0.25)
STOP = None
CAP = 64
R0, R1 = 3, 2


def shape_constants():
    p = np.arange(128)
    blk = {}
    blk["ident"] = np.eye(128)
    blk["flip"] = np.eye(128)[::-1]
    blk["ones"] = np.ones((128, 128))
    same = (p[:, None] // 64) == (p[None, :] // 64)
    blk["incl"] = (same & (p[:, None] <= p[None, :])).astype(float)
    blk["after"] = (same & (p[:, None] > p[None, :])).astype(float)
    blk["same"] = same.astype(float)
    blk["before"] = (p[:, None] < p[None, :]).astype(float)
    blk["pick"] = (p[:, None] % 32 == np.arange(2)[None, :]).astype(float)
    blk["iota"] = np.broadcast_to(np.arange(64), (128, 64))
    lv = []
    for b in (1, 2, 4, 8, 16, 32):
        pair = (p[:, None] // (2 * b)) == (p[None, :] // (2 * b))
        lv.append(pair & (p[:, None] % (2 * b) >= b) & (p[None, :] % (2 * b) < b))
    blk["level"] = np.stack(lv, 1).reshape(128, -1).astype(float)
    rot = np.zeros((128, 128))
    for a in range(2):
        for i in range(32):
            rot[a * 64 + 32 + i, a * 64 + i] = -1.0
            rot[a * 64 + i, a * 64 + 32 + i] = 1.0
    blk["rot"] = rot
    t = np.arange(T)
    inv = (np.float32(10000.0) ** (-np.arange(32, dtype=np.float32) / np.float32(32))).astype(np.float32)
    row = (t // 64).astype(np.float32)
    col = (t % 64).astype(np.float32)
    ang = np.stack([row[:, None] * inv, col[:, None] * inv], 1)
    ang = np.broadcast_to(ang[:, :, None, :], (T, 2, 2, 32)).reshape(T, 128).T.astype(np.float64)
    blk["cosr"] = np.cos(ang)
    blk["sinr"] = np.sin(ang)
    s = np.arange(256)
    w = (2 * s[None, :] + 1) * np.pi / 512 * s[:, None]
    for name, m in (("dc", np.cos(w)), ("ds", np.sin(w)), ("dct", np.cos(w).T / 256), ("dst", -np.sin(w).T / 256),
                    ("fc", np.cos(2 * np.pi * s[:, None] * s / 256)), ("fs", np.sin(2 * np.pi * s[:, None] * s / 256))):
        blk[name] = m.reshape(2, 128, 256).transpose(1, 0, 2).reshape(128, 512)
    ic = np.zeros((2, 128, 256))
    for g, wd in enumerate((2, 4, 8, 16)):
        cnt = np.clip(t + wd // 2, 0, T) - np.clip(t - wd // 2, 0, T)
        ic[g // 2, (g % 2) * 64:(g % 2) * 64 + 64] = 1.0 / cnt
    blk["icnt"] = ic.transpose(1, 0, 2).reshape(128, 512)
    hot = np.zeros((128, 512))
    for m in range(512):
        d = 255 - m
        if d < 0:
            hot[32, m] = 1.0
        else:
            if d < 16:
                bkt = d
            else:
                lg = np.float32(np.log(np.float32(d) / np.float32(16)))
                bkt = min(16 + int(np.float32(lg / np.float32(math.log(128.0)) * np.float32(16))), 31)
            hot[bkt, m] = 1.0
    blk["hot"] = hot
    lin = np.linspace(0.0, 1.0, T, dtype=np.float32)
    wv = (np.float32(2.0 * math.pi) * np.arange(T, dtype=np.float32)[:, None] / np.float32(T)).astype(np.float32)
    f = np.linspace(1e-4, 15, 16, dtype=np.float32)[None, :]
    fw = (f * wv).astype(np.float64)
    emb = np.concatenate([lin[:, None], np.cos(fw), -np.sin(fw)], -1)
    e = np.zeros((128, 256))
    e[:33] = emb.T
    blk["emb"] = e
    deltas = np.linspace(math.log(1e-2) / 1.5, math.log(1e-2) / 0.3, 768, dtype=np.float32)
    dec = np.exp((-lin[:, None] * np.abs(deltas)).astype(np.float64))
    blk["dec"] = dec.reshape(2, 128, 768).transpose(1, 0, 2).reshape(128, 1536)
    rs = np.ones((128, 512))
    rs[:, ::64] = 0.0
    blk["rset"] = rs
    eps = np.zeros((128, 4))
    eps[:, 0] = 1e-5
    eps[:, 1] = 1e-6
    eps[:, 2] = 1.0
    blk["eps"] = eps
    first = ("ident", "flip", "ones", "eps", "incl", "after", "same", "before", "iota", "pick", "level", "hot", "rset")
    order = list(first) + [n for n in blk if n not in first]
    at, cols, lo = {}, 0, 0
    for n in order:
        at[n] = (cols, blk[n].shape[1])
        cols += blk[n].shape[1]
        if n == first[-1]:
            lo = cols
    return np.concatenate([blk[n] for n in order], 1).astype(np.float32), at, lo


class Queue:

    def __init__(self, sem):
        self.sem, self.n, self.ops, self.seen = sem, 0, [], {}

    def wait(self, *toks):
        for t in toks:
            if t is None:
                continue
            if isinstance(t, list):
                self.wait(*t)
                continue
            s, v = t
            if self.seen.get(s.name, 0) < v:
                self.seen[s.name] = v
                self.ops.append(lambda e, s=s, v=v: e.wait_ge(s, v))

    def do(self, fn, *toks, inc=True):
        self.wait(*toks)
        if not inc:
            self.ops.append(fn)
            return None
        self.n += 1
        self.ops.append(lambda e, s=self.sem: fn(e).then_inc(s, 1))
        return (self.sem, self.n)

    def last(self):
        return (self.sem, self.n)

    def enter(self, sem):
        self.kept = (self.sem, self.n, self.ops, dict(self.seen))
        self.sem, self.n, self.ops = sem, 0, []

    def leave(self, flag):
        body = self.ops
        self.sem, self.n, self.ops, self.seen = self.kept
        self.ops.append((flag, body))

    def emit(self, e):
        for n, op in enumerate(self.ops):
            if isinstance(op, tuple):
                flag, body = op
                reg = e.alloc_register(f"flag{n}_{self.sem.name}")
                e.reg_load(reg, flag)
                with e.If_ne(reg, 0):
                    for o in body:
                        o(e)
            else:
                op(e)


class Ring:

    def __init__(self, ids):
        self.ids, self.at = list(ids), 0
        self.free = {i: [] for i in ids}

    def take(self):
        i = self.ids[self.at % len(self.ids)]
        self.at += 1
        return i, self.free[i]

    def rel(self, i, *toks):
        self.free[i] = list(toks)


def build(nc, A, out, at, lo):
    ctx = ExitStack()
    with ctx:
        def sb(name, shape, dt=F32):
            return ctx.enter_context(nc.sbuf_tensor(name, shape, dt))

        def sem(name):
            return ctx.enter_context(nc.semaphore(name))

        pe, act, dve, pool, sp = (Queue(sem("s_" + n)) for n in ("pe", "act", "dve", "pool", "sp"))
        dcount = {}

        def dma(q, dst, src, s, *toks):
            dcount[s.name] = dcount.get(s.name, 0) + 16
            q.wait(*toks)
            q.ops.append(lambda e: e.dma_start(dst, src).then_inc(s, 16))
            return (s, dcount[s.name])

        NS = 6
        wbuf = sb("wbuf", [128, NS, 2048])
        wsem = [sem(f"s_w{i}") for i in range(NS + 3)]
        wr = Ring(range(NS))
        wsec = []
        cst = sb("cst", [128, A["consts"].shape[1]])
        xT = sb("xT", [128, 8, T])
        hT = sb("hT", [128, 8, T])
        slab = sb("slab", [128, 9, 2048])
        ps = [ctx.enter_context(nc.psum_tensor(f"ps{i}", [128, 512], F32)) for i in range(8)]
        pr = Ring(range(8))

        def C(name):
            c0, n = at[name]
            return cst[:, c0:c0 + n]

        ident, flip, ones = C("ident"), C("flip"), C("ones")
        eps5, eps6 = C("eps")[:, 0:1], C("eps")[:, 1:2]
        one_c = C("eps")[:, 2:3]

        def S(i, *dims):
            v = slab[:, i, :]
            if len(dims) == 1:
                return v[:, 0:dims[0]]
            if len(dims) == 2:
                return v[:, 0:dims[0] * dims[1]].rearrange("p (a b) -> p a b", b=dims[1])
            return v[:, 0:dims[0] * dims[1] * dims[2]].rearrange("p (a b c) -> p a b c", b=dims[1], c=dims[2])

        def bc(v, n):
            return v.unsqueeze(1).broadcast_to([v.shape[0], n, v.shape[1]])

        def inner(v, n):
            return v.unsqueeze(2).broadcast_to([v.shape[0], v.shape[1], n])

        def mm(o, lhsT, rhs, start, stop, *toks, inc=False, skip=False):
            return pe.do(lambda e: e.matmul(o, lhsT, rhs, start=start, stop=stop, skip_group_check=skip),
                         *toks, inc=inc)

        def tr(o, i, *toks, inc=False):
            n = i.shape[0]
            return pe.do(lambda e: e.transpose(o, i, ident[0:n, 0:n]), *toks, inc=inc)

        def afn(o, i, fn, *toks, scale=1.0, bias=0.0, acc=None):
            return act.do(lambda e: e.activation(o, i, fn, bias=bias, scale=scale, accum_out=acc), *toks)

        def tt(q, o, a, b, op, *toks):
            return q.do(lambda e: e.tensor_tensor(o, a, b, op), *toks)

        def ts(q, o, a, s1, s2, op0, op1, *toks):
            if s2 is None:
                return q.do(lambda e: e.tensor_scalar(o, a, s1, None, op0), *toks)
            return q.do(lambda e: e.tensor_scalar(o, a, s1, s2, op0, op1), *toks)

        def stt(o, a, s, b, op0, op1, *toks):
            return dve.do(lambda e: e.scalar_tensor_tensor(o, a, s, b, op0, op1), *toks)

        def copy(o, i, *toks):
            return dve.do(lambda e: e.tensor_copy(o, i), *toks)

        fill_rate = [0]

        def meet():
            all_ = [q.last() for q in (pe, act, dve, pool)]
            fill(fill_rate[0])
            for q in (pe, act, dve, pool):
                q.wait(*all_)
            return all_

        class Unit:
            pass

        def unit(src, a, b):
            u = Unit()
            u.i, free = wr.take()
            u.v = wplace(u.i)[:, 0:a * b].rearrange("p (a b) -> p a b", b=b)
            u.tok = dma(sp, u.v, src, (wsec[-1] if wsec else wsem)[u.i], *free)
            return u

        def wplace(i):
            return wbuf[:, i, :] if i < NS else (slab[:, 7, :], slab[:, 8, :],
                                                 wP[:, :, :].rearrange("p a b -> p (a b)"))[i - NS]

        def pair_unit(g, u_, k0):
            u = Unit()
            u.i, free = wr.take()
            u.v = wplace(u.i).rearrange("p (k n) -> p k n", n=512)
            for half, w in ((0, g), (1, u_)):
                u.tok = dma(sp, u.v[:, :, half * 256:half * 256 + 256],
                            w.rearrange("(p k) n -> p k n", k=8)[:, k0:k0 + 4, :], wsem[u.i], *free)
            return u

        def cols(w, c0, n):
            return unit(w.rearrange("(p k) n -> p k n", k=8)[:, :, c0:c0 + n], 8, n)

        def rows(w, k0):
            return unit(w.rearrange("(k p) n -> p k n", p=128)[:, k0:k0 + 2, :], 2, w.shape[1])

        def proj_f(w, c0, n, rhs, evac, *ready):
            u = cols(w, c0, n)
            b, free = pr.take()
            pe.wait(u.tok, free, *ready)
            for m in range((n + 127) // 128):
                mc = min(128, n - m * 128)
                for k in range(8):
                    t = mm(ps[b][0:mc, m * 256:(m + 1) * 256], u.v[:, k, m * 128:m * 128 + mc], rhs[:, k, :],
                           k == 0, k == 7, inc=(k == 7))
            wr.rel(u.i, t)
            pr.rel(b, evac(ps[b], t))

        def proj_t(w, c0, n, lhs, evac, *ready):
            u = cols(w, c0, n)
            b, free = pr.take()
            pe.wait(u.tok, free, *ready)
            for m in range(2):
                for k in range(8):
                    t = mm(ps[b][:, m * 256:m * 256 + n], lhs[:, k, m * 128:(m + 1) * 128], u.v[:, k, :],
                           k == 0, k == 7, inc=(k == 7))
            wr.rel(u.i, t)
            pr.rel(b, evac(ps[b], t))

        YB = (4, 5, 6, 7)

        def Y(j):
            return ps[YB[j // 2]][:, (j % 2) * 256:(j % 2) * 256 + 256]

        def down(u, rhs, first, last, *ready):
            pe.wait(u.tok, *ready)
            t = None
            for kk in range(2):
                for j in range(8):
                    fin = kk == 1 and j == 7
                    t = mm(Y(j), u.v[:, kk, j::8], rhs[kk], first and kk == 0 and j % 2 == 0,
                           last and kk == 1 and j % 2 == 1, inc=fin, skip=True)
            wr.rel(u.i, t)
            return t

        def take_y():
            toks = []
            for b in YB:
                toks += pr.free[b]
            pr.ids, pr.at = [0, 1, 2, 3], 0
            return toks

        def give_y(tok):
            for b in YB:
                pr.rel(b, tok)
            pr.ids, pr.at = list(range(8)), 0

        s_in = sem("s_in")
        s_c2 = sem("s_c2")
        s_sm = sem("s_sm")
        xin = slab[:, 0:1, :].rearrange("p o n -> p (o n)").rearrange("p (t n) -> p t n", t=2)
        dma(sp, xin, A["x"][0].rearrange("(t p) n -> p t n", p=128), s_in)
        cv = sb("cv", [128, 3, 8])
        dma(sp, cv[:, 0, :], A["c"][0].rearrange("(p k) -> p k", k=8), s_in)
        dma(sp, cv[:, 1, :], A["c_2"][0].rearrange("(p k) -> p k", k=8), s_in)
        dma(sp, cv[:, 2, :], A["c_ctx_2"].rearrange("(p k) -> p k", k=8), s_in)
        t_in = dma(sp, cst[:, 0:lo], A["consts"][:, 0:lo], s_in)
        t_c2 = dma(pool, cst[:, lo:], A["consts"][:, lo:], s_c2)

        nvec = 128
        vec = sb("vec", [128, 21, 8])
        small = {}

        def vload(i, src, n=1):
            if n == 1:
                return dma(pool, vec[:, i, :], src.rearrange("(p k) -> p k", k=8), s_sm)
            return dma(pool, vec[:, i:i + n, :], src.rearrange("s (p k) -> p s k", k=8), s_sm)

        for i, n in enumerate(("ln_mix_g", "ln_mix_b", "ln_ffn_g", "ln_ffn_b")):
            for l in range(2):
                vload(2 * i + l, A[n][l])
        vload(8, A["norm_g_2"][0])
        vload(9, A["norm_g_2"][1])
        vload(10, A["final_g_2"])
        modb = sb("modb", [128, 18, 8])
        for l in range(2):
            dma(pool, modb[:, 6 * l:6 * l + 6, :], A["ada_b"][l].rearrange("(s p k) -> p s k", s=6, k=8), s_sm)
            dma(pool, modb[:, 12 + 3 * l:15 + 3 * l, :],
                A["b_mod_2"][l].rearrange("(s p k) -> p s k", s=3, k=8), s_sm)
        misc = sb("misc", [128, 2048])
        stage = misc[:, 1600:1984].rearrange("p (a b) -> p a b", a=3)
        colv = sb("colv", [128, 3, 128])
        dma(pool, stage[0:96, 0, :], A["od_conv_w"][0].rearrange("k (j p) -> (k j) p", p=128), s_sm)
        row = [0]
        place = {}

        def srow(name, src):
            n = src.shape[0]
            place[name] = row[0]
            dma(pool, stage[row[0]:row[0] + n, 1, :], src, s_sm)
            row[0] += n

        srow("hcw", A["hy_conv_w_2"][0].rearrange("k (j p) -> (k j) p", p=128))
        srow("hcb", A["hy_conv_b_2"][0].rearrange("(j p) -> j p", p=128))
        srow("skip", A["hy_skip_2"][0].rearrange("o (j p) -> (o j) p", p=128))
        srow("psc", A["pool_scale_2"][0].rearrange("(j p) -> j p", p=128))
        srow("evn", A["ev_norm"])
        srow("odn", A["od_norm"])
        srow("qn", A["q_norm_g_2"])
        srow("kn", A["k_norm_g_2"])
        srow("gkb", A["ev_gk_b"][0].rearrange("(j p) -> j p", p=128))
        nrow = row[0]
        for i, n in enumerate(("hy_b1_2", "hy_b2_2", "hy_freq_2")):
            dma(pool, stage[i:i + 1, 2, 0:64], A[n], s_sm)
        rpe33 = sb("rpe33", [33, 4])
        t_rm = pool.do(lambda e: e.memset(rpe33[:, :], -1e30))
        dma(pool, rpe33[0:32, :], A["rpe_bias"], s_sm, t_rm)
        gkw2 = sb("gkw2", [16, 256])
        dma(pool, gkw2[:, :], A["ev_gk_w2"][0], s_sm)
        poolw = sb("poolw", [128, 2, 64])
        dma(pool, poolw[:, :, :], A["pool_w_2"][0].rearrange("(t g) c d -> (g c) t d", t=2), s_sm)
        hw12 = sb("hw12", [64, 2, 64])
        dma(pool, hw12[0:33, 0, :], A["hy_w1_2"][0], s_sm)
        dma(pool, hw12[:, 1, :], A["hy_w2_2"][0], s_sm)
        rtb = sb("rtb", [128, 2, 64])
        for l in range(2):
            dma(pool, rtb[:, l, :], A["moe_router_b"][l:l + 1, :].broadcast_to([128, 64]), s_sm)
        adt = sb("adt", [128, 2, 8])
        dma(pool, adt[:, 0, :], A["od_a_log"].broadcast_to([128, 8]), s_sm)
        t_sm = dma(pool, adt[:, 1, :], A["od_dt_bias"].broadcast_to([128, 8]), s_sm)

        def vc(i, j):
            return vec[:, i, j:j + 1]

        def cv1(name, j=0):
            r = place[name] + j
            return colv[:, 1, r:r + 1]

        pe.wait(t_in, t_sm)
        b, free = pr.take()
        tr(ps[b][:, 0:96], stage[0:96, 0, :])
        tr(ps[b][:, 128:128 + nrow], stage[0:nrow, 1, :])
        t = tr(ps[b][0:64, 256:259], stage[0:3, 2, 0:64], inc=True)
        copy(colv[:, 0, 0:96], ps[b][:, 0:96], t)
        copy(colv[:, 1, 0:nrow], ps[b][:, 128:128 + nrow])
        t_cols = copy(colv[0:64, 2, 0:3], ps[b][0:64, 256:259])
        pr.rel(b, t_cols)

        def to_features(src, dst, tok):
            last = None
            for k2 in range(4):
                b, free = pr.take()
                pe.wait(free, tok)
                for kk in range(2):
                    for m in range(2):
                        t = tr(ps[b][:, kk * 256 + m * 128:kk * 256 + m * 128 + 128],
                               src[:, m, 2 * k2 + kk::8], inc=(kk == 1 and m == 1))
                o = dst[:, 2 * k2:2 * k2 + 2, :].rearrange("p a b -> p (a b)")
                last = copy(o, ps[b][:, :], t)
                pr.rel(b, last)
            return last

        t_x = to_features(xin, xT, t_in)

        cz = sb("cz", [128, 2, 8, 32])
        t_z = pool.do(lambda e: e.memset(cz[:, :, :, :], 0.0))
        afn(cz[:, 0, :, 0:1], cv[:, 0, :].unsqueeze(2), ACT.Silu, t_in, t_z)
        t_ca = afn(cz[:, 1, :, 0:2].rearrange("p k s -> p s k"), cv[:, 1:3, :], ACT.Silu)
        mods = sb("mods", [128, 18, 8])
        modc = sb("modc", [128, 2, 8])
        kc_x = sb("kc_x", [128, 2, 512])
        mrow = Ring((0, 1))
        tasks = []
        later = []
        m_done = {}

        def half_section(w, s, half, base, ctx_too=False):
            def first():
                wv = w.rearrange("(p k) n -> p k n", k=8)
                us = [unit(wv[:, 4 * q:4 * q + 4, s * 1024 + half * 512:s * 1024 + half * 512 + 512], 4, 512)
                      for q in range(2)]
                b, free = pr.take()
                pe.wait(free, t_ca)
                for q in range(2):
                    pe.wait(us[q].tok)
                    for i in range(4):
                        t = mm(ps[b][32 * i:32 * i + 32, :], cz[:, 0 if base < 12 else 1, 4 * q + i, :],
                               us[q].v[:, i, :], q == 0, q == 1, inc=(i == 3), skip=True)
                    wr.rel(us[q].i, t)
                i, rfree = mrow.take()
                t = afn(kc_x[:, i, :], ps[b][:, :], ACT.Copy, t, rfree)
                pr.rel(b, t)
                return i, t

            def second(i, t):
                b, free = pr.take()
                pe.wait(free, t)
                lo_ = 64 * half
                for k in range(8):
                    t = mm(ps[b][lo_:lo_ + 64, 2 * k:2 * k + 2], kc_x[:, i, k::8], C("pick"), True, True,
                           inc=(k == 7), skip=True)
                mrow.rel(i, t)
                pv = ps[b][lo_:lo_ + 64, 0:16].rearrange("p (j v) -> p j v", v=2)
                one = 1.0 if s in (1, 4) and (base < 12 or s == 1) else 0.0
                t1 = stt(mods[lo_:lo_ + 64, base + s, :], pv[:, :, 0], one, modb[lo_:lo_ + 64, base + s, :],
                         ALU.add, ALU.add, t, t_sm)
                if ctx_too:
                    t1 = stt(modc[lo_:lo_ + 64, s, :], pv[:, :, 1], one, modb[lo_:lo_ + 64, base + s, :],
                             ALU.add, ALU.add, t)
                pr.rel(b, t1)
                m_done[base] = t1
            return first, second

        for l in range(2):
            for s_ in range(6):
                for hf in range(2):
                    tasks.append(half_section(A["ada_w"][l], s_, hf, 6 * l))
        for l in range(2):
            for s_ in range(3):
                for hf in range(2):
                    tasks.append(half_section(A["w_mod_2"][l], s_, hf, 12 + 3 * l, l == 0 and s_ < 2))
        t_left = [len(tasks)]

        def fill(n):
            for _ in range(n):
                if tasks:
                    f, g = tasks.pop(0)
                    later.append((g, f()))
                if len(later) > 1 or (later and not tasks):
                    g, x = later.pop(0)
                    g(*x)

        def fill_to(n):
            while len(tasks) > n:
                fill(1)
            while later:
                g, x = later.pop(0)
                g(*x)
            return dve.last()

        def mc(base, s, j):
            return mods[:, base + s, j:j + 1]

        def scale_shift(dst, src, g, bcol, *toks):
            for j in range(8):
                t = ts(dve, dst[:, j, :], src[:, j, :], g(j), bcol(j), ALU.mult, ALU.add, *toks)
            return t

        def col_sum(src, n, scale_tok, *toks):
            b, free = pr.take()
            pe.wait(free, *toks)
            for k in range(n):
                t = mm(ps[b][:, 0:256], ones, src[:, k, :], k == 0, k == n - 1, inc=(k == n - 1))
            return b, t

        rs_t = sb("rs_t", [128, 2, 512])
        eps_a = {1e-5: eps5, 1e-6: eps6}

        def rsqrt(o, tmp, src, scale, eps, *toks):
            t = afn(tmp, src, ACT.Ln, *toks, scale=scale, bias=eps_a[eps])
            return afn(o, tmp, ACT.Exp, t, scale=-0.5)

        def norm_to(dst, src, sq, eps, tok, mean=True):
            rs = rs_t[:, 0, 0:256]
            if mean:
                b, t = col_sum(src, 8, None, tok)
                t = ts(dve, rs_t[:, 1, 256:512], ps[b][:, 0:256], 1.0 / D, None, ALU.mult, None, t)
                pr.rel(b, t)
                tok = tt(dve, src, src, bc(rs_t[:, 1, 256:512], 8), ALU.subtract, t)
            t = afn(sq, src, ACT.Square, tok)
            b, t = col_sum(sq, 8, None, t)
            t = rsqrt(rs, rs_t[:, 1, 0:256], ps[b][:, 0:256], 1.0 / D, eps, t)
            pr.rel(b, t)
            return tt(dve, dst, src, bc(rs, 8), ALU.mult, t, tok)

        def residual(base, gsec, t_y, vi, l, hbase, hsec):
            u, sq = S(8, 8, 256), S(7, 8, 256)
            meet()
            t = ts(dve, u, xT[:, :, :], ALPHA, None, ALU.mult, None)
            for j in range(8):
                t = stt(u[:, j, :], Y(j), mc(base, gsec, j), u[:, j, :], ALU.mult, ALU.add, t_y, t)
            give_y(t)
            t = norm_to(u, u, sq, 1e-5, t)
            t = scale_shift(xT, u, lambda j: vc(vi + l, j), lambda j: vc(vi + 2 + l, j), t)
            if hbase is not None:
                t = scale_shift(hT, xT, lambda j: mc(hbase, hsec + 1, j), lambda j: mc(hbase, hsec, j), t)
            return t

        def out_proj(w, src, *ready):
            toks = take_y()
            for q in range(4):
                u = rows(w, 2 * q)
                t = down(u, [src[:, 2 * q, :], src[:, 2 * q + 1, :]], q == 0, q == 3, toks, *ready)
            return t

        rtS = sb("rtS", [128, 2, 66])
        rtG = sb("rtG", [128, 2, 12])
        rt8 = sb("rt8", [128, 2, 8, 8])
        rtm = S(6, 768).rearrange("p (a m e) -> p a m e", a=6, m=2)
        wT = rs_t[0:64, 0, 0:256]
        wov = rtm[:, 5, :, :]
        hid = S(0, 8, 256).rearrange("p (h m) n -> p h m n", m=2)
        hsg = S(1, 2, 256)
        flags = sb("flags", [1, 2], mybir.dt.int32)
        t_sent = pool.do(lambda e: e.memset(rtS[:, :, :], -2e38))
        t_sent = pool.do(lambda e: e.memset(rtG[:, :, :], -2e38), t_sent)

        def route(l, t_h):
            b, free = pr.take()
            u = cols(A["moe_router_w"][l], 0, 64)
            pe.wait(free, t_h, u.tok)
            for m in range(2):
                for k in range(8):
                    t = mm(ps[b][:, m * 64:m * 64 + 64], hT[:, k, m * 128:(m + 1) * 128], u.v[:, k, :],
                           k == 0, k == 7, inc=(k == 7))
            wr.rel(u.i, t)
            lg = ps[b][:, 0:128].rearrange("p (m e) -> p m e", m=2)
            sc, sel, gm, wk = rtm[:, 0, :, :], rtm[:, 1, :, :], rtm[:, 2, :, 0:8], rtm[:, 3, :, :]
            t = afn(sc, lg, ACT.Exp, t, scale=-1.0)
            pr.rel(b, t)
            t = ts(dve, sc, sc, 1.0, None, ALU.add, None, t)
            t = dve.do(lambda e: e.reciprocal(sc, sc), t)
            t = tt(dve, sel, sc, bc(rtb[:, l, :], 2), ALU.add, t)
            for m in range(2):
                for g in range(8):
                    t1 = dve.do(lambda e, m=m, g=g: e.max(rt8[:, m, g, :], sel[:, m, g * 8:g * 8 + 8]), t)
            gs = rtG[:, :, 0:8]
            t = tt(dve, gs, rt8[:, :, :, 0], rt8[:, :, :, 1], ALU.add, t1, t_sent)
            for m in range(2):
                t1 = dve.do(lambda e, m=m: e.max(rt8[:, m, 0, :], gs[:, m, :]), t)
            t1 = dve.do(lambda e: e.memset(rt8[:, :, 0, 4:8], -2e38), t1)
            for m in range(2):
                t2 = dve.do(lambda e, m=m: e.match_replace(rtm[:, 4, m, 0:12], rt8[:, m, 0, :], rtG[:, m, :],
                                                           -3e38), t1)
            t = tt(dve, gm, rtm[:, 4, :, 0:8], gs, ALU.not_equal, t2)
            neg = rtm[:, 4, :, 16:24]
            t = ts(dve, neg, gm, 1e30, -1e30, ALU.mult, ALU.add, t)
            s4 = rtS[:, :, 0:64]
            for m in range(2):
                t1 = tt(dve, s4[:, m, :].rearrange("p (g e) -> p g e", e=8),
                        sel[:, m, :].rearrange("p (g e) -> p g e", e=8), inner(gm[:, m, :], 8), ALU.mult, t, t_sent)
            for m in range(2):
                t2 = tt(dve, s4[:, m, :].rearrange("p (g e) -> p g e", e=8),
                        s4[:, m, :].rearrange("p (g e) -> p g e", e=8), inner(neg[:, m, :], 8), ALU.add, t1)
            for m in range(2):
                t = dve.do(lambda e, m=m: e.max(rt8[:, m, 0, :], s4[:, m, :]), t2)
            t = dve.do(lambda e: e.memset(rt8[:, :, 0, 6:8], -2e38), t)
            wk66 = rtm[:, 3:6, :, :].rearrange("p a m e -> p (a m e)")
            for m in range(2):
                t1 = dve.do(lambda e, m=m: e.match_replace(wk66[:, 80 * m:80 * m + 66], rt8[:, m, 0, :],
                                                           rtS[:, m, :], -3e38), t)
            msk = S(6, 2048)[:, 1792:1920].rearrange("p (m e) -> p m e", m=2)
            rk = S(6, 2048)[:, 1920:2048].rearrange("p (m e) -> p m e", m=2)
            for m in range(2):
                t2 = tt(dve, msk[:, m, :], wk66[:, 80 * m:80 * m + 64], s4[:, m, :], ALU.not_equal, t1)
            t_m = t2
            t = tt(dve, sel, msk, sc, ALU.mult, t2)
            t = dve.do(lambda e: e.tensor_reduce(rt8[:, :, 1, 0:1], sel, AX.X, ALU.add), t)
            t = ts(dve, rt8[:, :, 1, 0:1], rt8[:, :, 1, 0:1], 1e-20, None, ALU.add, None, t)
            t = dve.do(lambda e: e.reciprocal(rt8[:, :, 1, 1:2], rt8[:, :, 1, 0:1]), t)
            for m in range(2):
                t1 = ts(dve, sel[:, m, :], sel[:, m, :], rt8[:, m, 1, 1:2], 2.5, ALU.mult, ALU.mult, t)
            t_w = t1
            b, free = pr.take()
            pe.wait(free, t_m)
            mm(ps[b][:, 0:64], C("before"), msk[:, 0, :], True, True)
            mm(ps[b][:, 64:128], ones, msk[:, 0, :], True, False)
            t = mm(ps[b][:, 64:128], C("before"), msk[:, 1, :], False, True, inc=True)
            t = tt(dve, rk, ps[b][:, 0:128].rearrange("p (m e) -> p m e", m=2), msk, ALU.mult, t)
            pr.rel(b, t)
            t_r = stt(rk, msk, -1.0, rk, ALU.add, ALU.add, t)
            t = dve.do(lambda e: e.tensor_reduce(rt8[:, 0, 2, 0:1], rk, AX.XY, ALU.max), t_r)
            b, free = pr.take()
            t = tr(ps[b][0:1, 0:128], rt8[:, 0, 2, 0:1], free, t, inc=True)
            t = dve.do(lambda e: e.tensor_reduce(rt8[0:1, 0, 2, 1:2], ps[b][0:1, 0:128], AX.X, ALU.max), t)
            pr.rel(b, t)
            t_f = ts(dve, flags[0:1, l:l + 1], rt8[0:1, 0, 2, 1:2], CAP - 0.5, None, ALU.is_ge, None, t)
            t = ts(dve, wov, rk, CAP - 0.5, None, ALU.is_ge, None, t_r)
            tt(dve, wov, wov, sel, ALU.mult, t, t_w)
            return sel, rk, t_w, t_r, t_f

        s_sec = [[sem(f"s_sec{l}{n}") for n in range(4)] for l in range(2)]
        w_sec = [[sem(f"s_sw{l}{n}") for n in range(NS)] for l in range(2)]

        def moe_rest(l):
            toks = [q.last() for q in (pe, act, dve, pool)]
            flag = flags[0:1, l:l + 1]
            kept = (dict(pr.free), list(pr.ids), pr.at, dict(wr.free), list(wr.ids), wr.at)
            for q, x in zip((pe, act, dve, sp), s_sec[l]):
                q.enter(x)
                q.wait(toks)
            wsec.append(w_sec[l])
            wr.ids, wr.at = list(range(NS)), 0
            for i in range(NS):
                wr.free[i] = []
            for i in range(4):
                pr.free[i] = []
            b = 0
            for m in range(2):
                t = tr(ps[b][0:64, m * 128:(m + 1) * 128], wov[:, m, :], inc=(m == 1))
            t_w = copy(wT[:, :], ps[b][0:64, 0:256], t)
            pr.rel(b, t_w)
            gu = Ring((0, 1, 2))
            gu.free[0] = [t_w]
            ws = Ring((0, 1))
            wsb = S(1, 8, 256)[:, 4:6, :]
            hr = Ring(range(4))
            sg = Ring(range(2))
            fr3 = []
            pend = None
            for e in range(NE + 1):
                if e < NE:
                    ug, uu = cols(A["moe_w_gate"][l, e], 0, 256), cols(A["moe_w_up"][l, e], 0, 256)
                    ud = rows(A["moe_w_down"][l, e], 0)
                    t_b = mm(ps[3][:, 0:256], ident[0:64, e:e + 1].broadcast_to([64, 128]), wT[:, :], True, True,
                             fr3, t_w, inc=True)
                    wi, free = ws.take()
                    wv = wsb[:, wi, :]
                    t_b = afn(wv, ps[3][:, 0:256], ACT.Copy, t_b, free)
                    fr3 = [t_b]
                    h, hfree = hr.take()
                    for m in range(2):
                        b, free = gu.take()
                        pe.wait(ug.tok, uu.tok, free)
                        for half, u in ((0, ug), (1, uu)):
                            for k in range(8):
                                t = mm(ps[b][:, half * 256:half * 256 + 256], u.v[:, k, m * 128:m * 128 + 128],
                                       hT[:, k, :], k == 0, k == 7, inc=(k == 7))
                            if m == 1:
                                wr.rel(u.i, t)
                        s, sfree = sg.take()
                        t1 = afn(hsg[:, s, :], ps[b][:, 0:256], ACT.Silu, t, sfree)
                        t2 = tt(dve, hsg[:, s, :], ps[b][:, 256:512], hsg[:, s, :], ALU.mult, t1)
                        gu.rel(b, t2)
                        t2 = tt(dve, hid[:, h, m, :], wv, hsg[:, s, :], ALU.mult, t2, t_b, hfree)
                        sg.rel(s, t2)
                    ws.rel(wi, t2)
                if pend is not None:
                    pd, ph, pt = pend
                    t = down(pd, [hid[:, ph, 0, :], hid[:, ph, 1, :]], False, False, pt)
                    hr.rel(ph, t)
                pend = (ud, h, t2)
            ends = [q.last() for q in (pe, act, dve)]
            for q in (pe, act, dve, sp):
                q.wait(ends)
            wsec.pop()
            for q in (pe, act, dve, sp):
                q.leave(flag)
            pr.free, pr.ids, pr.at, wr.free, wr.ids, wr.at = kept

        def moe(l, t_h):
            start = meet()
            sel, rk, t_w, t_r, t_f = route(l, t_h)
            sp.wait(t_f)
            htok = S(0, 2, 1024)
            for m in range(2):
                for k2 in range(2):
                    b, free = pr.take()
                    pe.wait(free)
                    for k in range(4):
                        t = tr(ps[b][:, k * 128:k * 128 + 128], hT[:, 4 * k2 + k, m * 128:m * 128 + 128],
                               inc=(k == 3))
                    t_ht = afn(htok[:, m, k2 * 512:k2 * 512 + 512], ps[b][:, :], ACT.Copy, t)
                    pr.rel(b, t_ht)
            ylast = take_y()
            ug, uu = cols(A["sh_w_gate"][l], 0, 256), cols(A["sh_w_up"][l], 0, 256)
            us = rows(A["sh_w_down"][l], 0)
            sh = S(6, 2048)[:, 768:1792].rearrange("p (a n) -> p a n", a=4)
            for m in range(2):
                b, free = pr.take()
                pe.wait(ug.tok, uu.tok, free)
                for half, u in ((0, ug), (1, uu)):
                    for k in range(8):
                        t = mm(ps[b][:, half * 256:half * 256 + 256], u.v[:, k, m * 128:m * 128 + 128],
                               hT[:, k, :], k == 0, k == 7, inc=(k == 7))
                    if m == 1:
                        wr.rel(u.i, t)
                t1 = afn(sh[:, m, :], ps[b][:, 0:256], ACT.Silu, t)
                t_s = tt(dve, sh[:, 2 + m, :], ps[b][:, 256:512], sh[:, m, :], ALU.mult, t1)
                pr.rel(b, t_s)
            t = down(us, [sh[:, 2, :], sh[:, 3, :]], True, False, t_s, ylast)
            wr.ids, wr.at = [wr.ids[(wr.at + i) % NS] for i in range(NS)] + [NS, NS + 1, NS + 2], 0
            wr.at = 0
            for i in range(3):
                wr.rel(NS + i, *start)

            xg = [S(1, 8, 256), S(2, 8, 256)]
            pm = S(3, 4, 512)
            P = [pm[:, i, :].rearrange("p (m n) -> p m n", m=2) for i in range(2)]
            PW = [pm[:, 2 + i, :].rearrange("p (m n) -> p m n", m=2) for i in range(2)]
            ys = S(4, 2, 1024)
            tp = S(5, 4, 512)[:, 0:2, :]
            hh = S(5, 8, 256)[:, 4:6, :]
            sg = S(5, 8, 256)[:, 6:8, :]
            iota = C("iota")
            NG, NP = NE // 4, NE // 2
            t_P, t_PW, t_X = {}, {}, {}
            r_P, r_PW = {}, {}
            t_T, t_S, t_A = {}, {}, {}

            def places(g):
                i = g % 2
                dve.wait(r_P.get(g - 2), r_PW.get(g - 2), t_w, t_r)
                for m in range(2):
                    for j in range(4):
                        e = 4 * g + j
                        t_P[g] = ts(dve, P[i][:, m, j * 64:j * 64 + 64], iota, rk[:, m, e:e + 1],
                                    None, ALU.is_equal, None)
                for m in range(2):
                    for j in range(4):
                        e = 4 * g + j
                        t_PW[g] = ts(dve, PW[i][:, m, j * 64:j * 64 + 64], iota, rk[:, m, e:e + 1],
                                     sel[:, m, e:e + 1], ALU.is_equal, ALU.mult)
                if CAP < 64:
                    v = P[i].rearrange("p m (j c) -> p (m j) c", c=64)[:, :, CAP:64]
                    w = PW[i].rearrange("p m (j c) -> p (m j) c", c=64)[:, :, CAP:64]
                    t_P[g] = dve.do(lambda e, v=v: e.memset(v, 0.0), t_P[g])
                    t_PW[g] = dve.do(lambda e, w=w: e.memset(w, 0.0), t_PW[g])

            def gather(g, half):
                i = g % 2
                pe.wait(t_P[g], t_ht)
                for k2 in range(2):
                    b, free = pr.take()
                    pe.wait(free)
                    for kk in range(2):
                        k = 4 * half + 2 * k2 + kk
                        for m in range(2):
                            t = mm(ps[b][:, kk * 256:kk * 256 + 256], htok[:, m, k * 128:k * 128 + 128],
                                   P[i][:, m, :], m == 0, m == 1, inc=(kk == 1 and m == 1))
                    k = 4 * half + 2 * k2
                    o = xg[i][:, k:k + 2, :].rearrange("p a b -> p (a b)")
                    t1 = copy(o, ps[b][:, :], t, t_A.get(2 * g - 3))
                    pr.rel(b, t1)
                t_X[(g, half)] = t1
                if half == 1:
                    r_P[g] = t

            def scatter(q):
                pe.wait(t_S[q])
                for j in range(8):
                    t = mm(Y(j), ys[:, q % 2, j::8], tp[:, q % 2, 256:512], False, q == NP - 1 and j % 2 == 1,
                           inc=(j == 7), skip=True)
                return t

            places(0)
            gather(0, 0)
            gather(0, 1)
            done = {}
            for q in range(NP):
                g, o = q // 2, (q % 2) * 128
                if q % 2 == 0 and g + 1 < NG:
                    places(g + 1)
                es = (2 * q, 2 * q + 1)
                us = {}
                for k0 in (0, 4):
                    for e in es:
                        us[(e, k0)] = pair_unit(A["moe_w_gate"][l, e], A["moe_w_up"][l, e], k0)
                ud = [rows(A["moe_w_down"][l, e], 0) for e in es]
                b, free = pr.take()
                pe.wait(free, t_X[(g, 0)], t_X[(g, 1)])
                for k in range(8):
                    k0 = k // 4 * 4
                    for i, e in enumerate(es):
                        u = us[(e, k0)]
                        if k == k0:
                            pe.wait(u.tok)
                        fin = k % 4 == 3
                        t = mm(ps[b][64 * i:64 * i + 64, :], xg[g % 2][:, k, o + 64 * i:o + 64 * i + 64],
                               u.v[:, k - k0, :], k == 0, k == 7, inc=fin, skip=True)
                        if fin:
                            wr.rel(u.i, t)
                t_A[q] = t
                t1 = afn(sg[:, q % 2, :], ps[b][:, 0:256], ACT.Silu, t)
                t1 = tt(dve, hh[:, q % 2, :], ps[b][:, 256:512], sg[:, q % 2, :], ALU.mult, t1)
                pr.rel(b, t1)
                if q:
                    done[q - 1] = scatter(q - 1)
                b, free = pr.take()
                pe.wait(free, t1, t_PW[g])
                for i in range(2):
                    tr(ps[b][:, i * 128:i * 128 + 128], hh[:, q % 2, i * 128:i * 128 + 128])
                for m in range(2):
                    t = tr(ps[b][:, 256 + m * 128:384 + m * 128], PW[g % 2][:, m, o:o + 128], inc=(m == 1))
                if q % 2 == 1:
                    r_PW[g] = t
                t_t = copy(tp[:, q % 2, :], ps[b][:, :], t, done.get(q - 2))
                pr.rel(b, t_t)
                if g + 1 < NG:
                    gather(g + 1, q % 2)
                for half in range(2):
                    b, free = pr.take()
                    pe.wait(free, t_t)
                    for kk in range(2):
                        for i in range(2):
                            pe.wait(ud[i].tok)
                            fin = kk == 1
                            t = mm(ps[b][64 * i:64 * i + 64, :],
                                   tp[:, q % 2, kk * 128 + 64 * i:kk * 128 + 64 * i + 64],
                                   ud[i].v[:, kk, half * 512:half * 512 + 512], kk == 0, kk == 1, inc=fin,
                                   skip=True)
                            if fin and half == 1:
                                wr.rel(ud[i].i, t)
                    t_S[q] = afn(ys[:, q % 2, half * 512:half * 512 + 512], ps[b][:, :], ACT.Copy, t,
                                 done.get(q - 2))
                    pr.rel(b, t_S[q])
            t = scatter(NP - 1)
            wr.ids, wr.at = list(range(NS)), 0
            moe_rest(l)
            return t

        scr = nc.dram_tensor("scr_tab", [4, 512], F32, kind="Internal")
        s_tab = sem("s_tab")
        stat = sb("stat", [128, 4, 16])

        def softmax_T(score_b, n, col, t_s, dst):
            pass

        def even_mixer(t_h):
            w = A["ev_w_in"][0]
            qk = S(0, 8, 256)
            vt = S(1, 2, 512)
            gv = S(1, 4, 512)[:, 2:4, :]
            gqk = S(2, 8, 256)
            gg = S(3, 8, 256)
            glr = gqk[:, 4, :]
            gT = S(3, 8, 256)[:, 4:6, :]
            mix = S(4, 8, 256)
            P = S(5, 8, 256)
            PT = S(6, 8, 256)

            def to(dst, scale=1.0, a=True, n=512):
                def ev(p, t):
                    if a:
                        return afn(dst, p[:, 0:n], ACT.Copy, t, scale=scale)
                    return ts(dve, dst, p[:, 0:n], scale, None, ALU.mult, None, t)
                return ev

            def flat(v):
                return v.rearrange("p a b -> p (a b)")

            b, free = pr.take()
            t = mm(ps[b][0:4, :], rpe33[:, :], C("hot")[0:33, :], True, True, free, t_sm, t_in, inc=True)
            t = copy(rs_t[0:4, 0, :], ps[b][0:4, :], t)
            pr.rel(b, t)
            t = dma(pool, scr.ap(), rs_t[0:4, 0, :], s_tab, t)
            hank = S(7, 2, 4, 256)
            for qt in range(2):
                src = bass.AP(scr, 128 * (1 - qt), [[1, 128], [512, 4], [1, 256]])
                t_hk = dma(pool, hank[:, qt, :, :], src, s_tab, t)

            for i in range(2):
                proj_f(w, 256 * i, 256, hT, to(flat(qk[:, 2 * i:2 * i + 2, :]), 128 ** -0.5, i % 2 == 0), t_h)
            for i in range(2):
                proj_f(w, 512 + 256 * i, 256, hT, to(flat(qk[:, 4 + 2 * i:6 + 2 * i, :]), 1.0, i % 2 == 0), t_h)

            def to_t(dst, i):
                def ev(p, t):
                    return copy(dst[:, :, 256 * i:256 * i + 256], p[:, :].rearrange("p (m n) -> p m n", m=2), t)
                return ev

            for i in range(2):
                proj_t(w, 1024 + 256 * i, 256, hT, to_t(vt, i), t_h)
            proj_f(w, 1536, 256, hT, to(flat(gqk[:, 0:2, :]), 0.125), t_h)
            proj_f(w, 1792, 256, hT, to(flat(gqk[:, 2:4, :]), 1.0, False), t_h)
            for i in range(2):
                proj_t(w, 2048 + 256 * i, 256, hT, to_t(gv, i), t_h)
            for i in range(2):
                proj_f(w, 2560 + 256 * i, 256, hT, to(flat(gg[:, 2 * i:2 * i + 2, :]), 1.0, i % 2 == 0), t_h)
            proj_f(w, 3072, 16, hT, lambda p, t: copy(glr[0:16, :], p[0:16, 0:256], t), t_h)
            meet()

            for q in range(8):
                h, qt = q // 2, q % 2
                b, free = pr.take()
                mm(ps[b][:, 0:256], qk[:, h, qt * 128:qt * 128 + 128], qk[:, 4 + h, :], True, False, free)
                t = mm(ps[b][:, 0:256], flip, hank[:, qt, h, :], False, True, t_hk, inc=True)
                t = dve.do(lambda e, b=b, q=q: e.tensor_reduce(stat[:, 0, q:q + 1], ps[b][:, 0:256], AX.X,
                                                               ALU.max, negate=True), t)
                t = afn(P[:, q, :], ps[b][:, 0:256], ACT.Exp, t, bias=stat[:, 0, q:q + 1],
                        acc=stat[:, 1, q:q + 1])
                pr.rel(b, t)
                t = dve.do(lambda e, q=q: e.reciprocal(stat[:, 2, q:q + 1], stat[:, 1, q:q + 1]), t)
                ts(dve, P[:, q, :], P[:, q, :], stat[:, 2, q:q + 1], None, ALU.mult, None, t)
            for h in range(4):
                b, free = pr.take()
                pe.wait(free, dve.last())
                for kt in range(2):
                    for qt in range(2):
                        t = tr(ps[b][:, kt * 256 + qt * 128:kt * 256 + qt * 128 + 128],
                               P[:, 2 * h + qt, kt * 128:kt * 128 + 128], inc=(kt == 1 and qt == 1))
                t = copy(flat(PT[:, 2 * h:2 * h + 2, :]), ps[b][:, :], t)
                pr.rel(b, t)
            for h in range(4):
                b, free = pr.take()
                pe.wait(free, dve.last())
                for kt in range(2):
                    t = mm(ps[b][:, 0:256], vt[:, kt, h * 128:h * 128 + 128], PT[:, 2 * h + kt, :], kt == 0,
                           kt == 1, inc=(kt == 1))
                t = afn(mix[:, h, :], ps[b][:, 0:256], ACT.Copy, t)
                pr.rel(b, t)

            b, free = pr.take()
            for j in range(2):
                t = mm(ps[b][:, j * 256:j * 256 + 256], gkw2[:, j * 128:j * 128 + 128], glr[0:16, :], True, True,
                       free, inc=(j == 1))
            z, ez = S(8, 8, 256)[:, 0:2, :], S(8, 8, 256)[:, 2:4, :]
            bb, e2 = S(8, 8, 256)[:, 4:6, :], S(8, 8, 256)[:, 6:8, :]
            for j in range(2):
                t1 = ts(dve, z[:, j, :], ps[b][:, j * 256:j * 256 + 256], cv1("gkb", j), None, ALU.add, None, t,
                        t_cols)
            pr.rel(b, t1)
            t = afn(ez, z, ACT.Abs, t1)
            t = afn(ez, ez, ACT.Exp, t, scale=-1.0)
            t = afn(ez, ez, ACT.Ln, t, bias=one_c)
            t = ts(dve, z, z, 0.0, None, ALU.min, None, t)
            t = tt(dve, z, z, ez, ALU.subtract, t)
            t = ts(dve, z, z, 1.0 / 16, None, ALU.mult, None, t)
            fz, fb = flat(z), flat(bb)
            t = dve.do(lambda e: e.tensor_tensor_scan(fb, C("rset"), fz, 0.0, ALU.mult, ALU.add), t)
            b4 = bb.rearrange("p j (c i) -> p (j c) i", i=64)
            e4 = e2.rearrange("p j (c i) -> p (j c) i", i=64)
            t_e = tt(dve, e4, b4[:, :, 63:64].broadcast_to([128, 8, 64]), b4, ALU.subtract, t)
            dl = stat[:, 3, 0:8]
            t = afn(dl, b4[:, :, 63], ACT.Exp, t_e)
            t = afn(z, bb, ACT.Exp, t, t_e)
            t = afn(ez, bb, ACT.Exp, t, scale=-1.0)
            t = afn(e2, e2, ACT.Exp, t, t_e)
            qe, ke, kn = S(7, 8, 256)[:, 0:2, :], S(7, 8, 256)[:, 2:4, :], S(7, 8, 256)[:, 4:6, :]
            knt = S(7, 8, 256)[:, 6:8, :]
            meet()
            tt(dve, qe, gqk[:, 0:2, :], z, ALU.mult)
            tt(dve, ke, gqk[:, 2:4, :], ez, ALU.mult)
            t = tt(dve, kn, gqk[:, 2:4, :], e2, ALU.mult)
            b, free = pr.take()
            pe.wait(free, t)
            for m in range(2):
                for j in range(2):
                    t = tr(ps[b][:, m * 256 + j * 128:m * 256 + j * 128 + 128], kn[:, j, m * 128:m * 128 + 128],
                           inc=(m == 1 and j == 1))
            t = copy(flat(knt), ps[b][:, :], t)
            pr.rel(b, t)
            aT = S(6, 8, 128)
            for m in range(2):
                b, free = pr.take()
                pe.wait(free, dve.last())
                for h in (0, 2, 1, 3):
                    po, j = (h % 2) * 64, h // 2
                    t = mm(ps[b][:, h * 128:h * 128 + 128], ke[po:po + 64, j, m * 128:m * 128 + 128],
                           qe[po:po + 64, j, m * 128:m * 128 + 128], True, True, t if h == 1 else None,
                           inc=(h >= 2))
                meet()
                t = tt(dve, aT[:, 4 * m:4 * m + 4, :], ps[b][:, :].rearrange("p (h i) -> p h i", h=4),
                       bc(C("incl"), 4), ALU.mult, t)
                pr.rel(b, t)
            st = S(5, 8, 128)[:, 0:2, :]
            oT = S(5, 8, 256)[:, 4:8, :]
            meet()
            for c in range(4):
                m, off = c // 2, (c % 2) * 64
                b, free = pr.take()
                pe.wait(free, dve.last())
                for h in range(4):
                    po, j = (h % 2) * 64, h // 2
                    t = mm(ps[b][:, h * 64:h * 64 + 64], gv[off:off + 64, m, h * 128:h * 128 + 128],
                           aT[off:off + 64, 4 * m + h, off:off + 64], h == 0, c == 0, inc=(h == 3), skip=True)
                if c:
                    for h in (0, 2, 1, 3):
                        po, j = (h % 2) * 64, h // 2
                        t = mm(ps[b][:, h * 64:h * 64 + 64], st[po:po + 64, j, :],
                               qe[po:po + 64, j, c * 64:c * 64 + 64], False, True, t if h < 2 else None,
                               inc=(h >= 2), skip=True)
                t_o = afn(oT[:, :, c * 64:c * 64 + 64], ps[b][:, 0:256].rearrange("p (h i) -> p h i", h=4),
                          ACT.Copy, t)
                pr.rel(b, t_o)
                if c < 3:
                    b, free = pr.take()
                    pe.wait(free)
                    for h in range(4):
                        po, j = (h % 2) * 64, h // 2
                        t = mm(ps[b][po:po + 64, j * 128:j * 128 + 128],
                               knt[off:off + 64, m, h * 64:h * 64 + 64], gv[off:off + 64, m, h * 128:h * 128 + 128],
                               True, True, inc=True)
                    for j in range(2):
                        u = ps[b][:, j * 128:j * 128 + 128]
                        if c == 0:
                            t1 = copy(st[:, j, :], u, t)
                        else:
                            t1 = stt(st[:, j, :], st[:, j, :], dl[:, j * 4 + c:j * 4 + c + 1], u, ALU.mult,
                                     ALU.add, t)
                    pr.rel(b, t1)
            t = gated_norm(oT, gg, mix[:, 4:8, :], 4, cv1("evn"), t_o)
            meet()
            return out_proj(A["ev_w_out"][0], mix, t)

        def gated_norm(oT, gate, dst, n, wcol, tok):
            sq = S(8, 8, 256)
            t_s = afn(gate[:, 0:n, :], gate[:, 0:n, :], ACT.Silu, tok)
            t = afn(sq[:, 0:n, :], oT, ACT.Square, tok, t_s)
            for i in range(n // 2):
                b, free = pr.take()
                t1 = mm(ps[b][:, :], ones, sq[:, 2 * i:2 * i + 2, :], True, True, free, t, inc=True)
                r = sq[:, 2 * i:2 * i + 2, :].rearrange("p a b -> p (a b)")
                t2 = rsqrt(r, rs_t[:, i % 2, :], ps[b][:, :], 1.0 / 128, 1e-6, t1, dve.last())
                pr.rel(b, t2)
            t = stt(dst, oT, wcol, sq[:, 0:n, :], ALU.mult, ALU.mult, t2, t_cols)
            return tt(dve, dst, dst, gate[:, 0:n, :], ALU.mult, t, t_s)

        raw = misc[:, 0:3 * 518].rearrange("p (r m n) -> p r m n", r=3, m=2)
        gds = sb("gds", [128, 16, 16])
        t_raw = pool.do(lambda e: e.memset(raw[:, :, :, 0:3], 0.0))

        def delta_mixer(t_h):
            w = A["od_w_in"][0]
            qT, kT, vT, gate = S(0, 8, 256), S(1, 8, 256), S(2, 8, 256), S(3, 8, 256)
            rr = Ring(range(3))

            def flat(v):
                return v.rearrange("p a b -> p (a b)")

            ba = gds[:, 0:4, :].rearrange("p a b -> p (a b)")[:, 0:32].rearrange("p (m n) -> p m n", m=2)
            proj_t(w, 4096, 16, hT, lambda p, t: copy(ba, p[:, :].rearrange("p (m n) -> p m n", m=2)[:, :, 0:16], t),
                   t_h)
            be = gds[:, 4, :].rearrange("p (m n) -> p m n", m=2)
            gg = gds[:, 5, :].rearrange("p (m n) -> p m n", m=2)
            tz = gds[:, 6, :].rearrange("p (m n) -> p m n", m=2)
            ea = gds[:, 7, 0:8]
            t = afn(be, ba[:, :, 0:8], ACT.Exp, dve.last(), scale=-1.0)
            t = ts(dve, be, be, 1.0, None, ALU.add, None, t)
            t = dve.do(lambda e: e.reciprocal(be, be), t)
            t = tt(dve, gg, ba[:, :, 8:16], bc(adt[:, 1, :], 2), ALU.add, t)
            t = afn(tz, gg, ACT.Abs, t)
            t = afn(tz, tz, ACT.Exp, t, scale=-1.0)
            s1 = gds[:, 12, :].rearrange("p (m n) -> p m n", m=2)
            s2 = gds[:, 13, :].rearrange("p (m n) -> p m n", m=2)
            qq = gds[:, 14, :].rearrange("p (m n) -> p m n", m=2)
            t = ts(dve, s1, tz, 2.0, None, ALU.add, None, t)
            t = dve.do(lambda e: e.reciprocal(s1, s1), t)
            t = tt(dve, s1, s1, tz, ALU.mult, t)
            t = tt(dve, s2, s1, s1, ALU.mult, t)
            t = ts(dve, qq, s2, 1.0 / 15, None, ALU.mult, None, t)
            for n in (13, 11, 9, 7, 5, 3):
                t = stt(qq, qq, 1.0 / n, s2, ALU.add, ALU.mult, t)
            t = stt(qq, qq, 1.0, s1, ALU.add, ALU.mult, t)
            t = ts(dve, tz, qq, 2.0, None, ALU.mult, None, t)
            t = afn(ea, adt[:, 0, :], ACT.Exp, t)
            t = ts(dve, gg, gg, 0.0, None, ALU.max, None, t)
            t = tt(dve, gg, gg, tz, ALU.add, t)
            t = tt(dve, gg, gg, bc(ea, 2), ALU.mult, t)
            t_g = ts(dve, gg, gg, -1.0, None, ALU.mult, None, t)
            b, free = pr.take()
            pe.wait(free, t_g)
            for m in range(2):
                mm(ps[b][:, m * 8:m * 8 + 8], C("incl"), gg[:, m, :], True, True)
                mm(ps[b][:, 16 + m * 8:24 + m * 8], C("same"), gg[:, m, :], True, True)
            t = None
            for c in (0, 2, 1, 3):
                po = (c % 2) * 64
                t = mm(ps[b][:, 32 + c * 8:40 + c * 8], ones[po:po + 64, :], gg[po:po + 64, c // 2, :], True, True,
                       t if c == 1 else None, inc=(c >= 2))
            egc = gds[:, 8, :]
            een = gds[:, 9, :]
            DL = gds[:, 10:12, :].rearrange("p a b -> p (a b)")
            t1 = copy(egc, ps[b][:, 0:16], t)
            t1 = tt(dve, een, ps[b][:, 16:32], egc, ALU.subtract, t1)
            t1 = afn(egc, egc, ACT.Exp, t1)
            t1 = afn(een, een, ACT.Exp, t1)
            t1 = afn(DL, ps[b][:, 32:64], ACT.Exp, t1)
            pr.rel(b, t1)

            def conv(dst, j0):
                def ev(p, t):
                    r, free = rr.take()
                    t = afn(raw[:, r, :, 3:259], p[:, :].rearrange("p (m n) -> p m n", m=2), ACT.Copy, t, t_raw,
                            free)
                    tl = t
                    for m in range(2):
                        x = raw[:, r, m, :]
                        j = j0 + m
                        o = dst[:, m, :]
                        t1 = ts(dve, o, x[:, 0:256], colv[:, 0, j:j + 1], None, ALU.mult, None, t, t_cols)
                        for k in range(1, 4):
                            t1 = stt(o, x[:, k:k + 256], colv[:, 0, k * 24 + j:k * 24 + j + 1], o, ALU.mult,
                                     ALU.add, t1)
                    rr.rel(r, t1)
                    afn(dst, dst, ACT.Silu, t1)
                    return tl
                return ev

            for s, dst in ((0, qT), (1, kT), (2, vT)):
                for i in range(4):
                    proj_f(w, s * 1024 + 256 * i, 256, hT, conv(dst[:, 2 * i:2 * i + 2, :], s * 8 + 2 * i), t_h)
            for i in range(4):
                g = gate[:, 2 * i:2 * i + 2, :]
                proj_f(w, 3072 + 256 * i, 256, hT,
                       lambda p, t, g=g: afn(g, p[:, :].rearrange("p (m n) -> p m n", m=2), ACT.Copy, t), t_h)
            meet()
            sq, rn = S(4, 8, 256), S(5, 8, 256)
            for x, scale in ((qT, 128 ** -0.5), (kT, 1.0)):
                t = afn(sq, x, ACT.Square, dve.last(), pe.last())
                for i in range(4):
                    b, free = pr.take()
                    t1 = mm(ps[b][:, :], ones, sq[:, 2 * i:2 * i + 2, :], True, True, free, t, inc=True)
                    t2 = rsqrt(flat(rn[:, 2 * i:2 * i + 2, :]), rs_t[:, i % 2, :], ps[b][:, :], 1.0, 1e-6, t1,
                               dve.last())
                    pr.rel(b, t2)
                t = stt(x, x, scale, rn, ALU.mult, ALU.mult, t2)
            meet()
            kg, ke, vt = S(4, 16, 128), S(5, 16, 128), S(6, 16, 128)
            for i in range(4):
                b, free = pr.take()
                pe.wait(free)
                for j in range(4):
                    h, m = 2 * i + j // 2, j % 2
                    t = tr(ps[b][:, j * 128:j * 128 + 128], kT[:, h, m * 128:m * 128 + 128], inc=(j == 3))
                t = afn(flat(ke[:, 4 * i:4 * i + 4, :]), ps[b][:, :], ACT.Copy, t)
                pr.rel(b, t)
                for j in range(4):
                    h, m = 2 * i + j // 2, j % 2
                    g = 4 * i + j
                    t1 = ts(dve, kg[:, g, :], ke[:, g, :], egc[:, m * 8 + h:m * 8 + h + 1], None, ALU.mult, None,
                            t)
                    ts(dve, ke[:, g, :], ke[:, g, :], een[:, m * 8 + h:m * 8 + h + 1], None, ALU.mult, None, t1)
                b, free = pr.take()
                pe.wait(free)
                for j in range(4):
                    h, m = 2 * i + j // 2, j % 2
                    t = tr(ps[b][:, j * 128:j * 128 + 128], vT[:, h, m * 128:m * 128 + 128], inc=(j == 3))
                t = afn(flat(vt[:, 4 * i:4 * i + 4, :]), ps[b][:, :], ACT.Copy, t)
                pr.rel(b, t)
            meet()
            GM, DT = S(8, 4, 4, 128), S(2, 16, 128)
            for i in range(4):
                for j in range(4):
                    h, m = 2 * i + j // 2, j % 2
                    t = ts(dve, GM[:, i, j, :], C("after"), gg[:, m, h:h + 1], None, ALU.mult, None)
                b, free = pr.take()
                pe.wait(free, t)
                for j in range(4):
                    t = mm(ps[b][:, j * 128:j * 128 + 128], GM[:, i, j, :], C("incl"), True, True, inc=(j == 3))
                d4 = DT[:, 4 * i:4 * i + 4, :]
                t = afn(flat(d4), ps[b][:, :], ACT.Exp, t)
                pr.rel(b, t)
                tt(dve, d4, d4, bc(C("incl"), 4), ALU.mult, t)
            AT, QK = S(7, 16, 128), S(8, 16, 128)
            meet()
            for i in range(4):
                b, free = pr.take()
                b2, free2 = pr.take()
                pe.wait(free, free2)
                for j in range(4):
                    h, m = 2 * i + j // 2, j % 2
                    x = kT[:, h, m * 128:m * 128 + 128]
                    mm(ps[b][:, j * 128:j * 128 + 128], x, x, True, True)
                    t = mm(ps[b2][:, j * 128:j * 128 + 128], x, qT[:, h, m * 128:m * 128 + 128], True, True,
                           inc=(j == 3))
                for j in range(4):
                    h, m = 2 * i + j // 2, j % 2
                    g = 4 * i + j
                    t1 = stt(AT[:, g, :], ps[b][:, j * 128:j * 128 + 128], be[:, m, h:h + 1], DT[:, g, :],
                             ALU.mult, ALU.mult, t)
                t2 = tt(dve, flat(QK[:, 4 * i:4 * i + 4, :]), ps[b2][:, :], flat(DT[:, 4 * i:4 * i + 4, :]),
                        ALU.mult, t)
                pr.rel(b, t1)
                pr.rel(b2, t2)
            meet()
            for i in range(4):
                b, free = pr.take()
                pe.wait(free)
                for j in range(4):
                    h, m = 2 * i + j // 2, j % 2
                    t = mm(ps[b][:, j * 128:j * 128 + 128], gg[:, m, h:h + 1].broadcast_to([128, 128]), C("incl"),
                           True, True, inc=(j == 3))
                r = rs_t[:, i % 2, :]
                t = afn(r, ps[b][:, :], ACT.Exp, t, dve.last())
                pr.rel(b, t)
                x = flat(qT[:, 2 * i:2 * i + 2, :])
                t = tt(dve, x, x, r, ALU.mult, t)
            TM, TTm, PM = S(1, 16, 128), S(2, 16, 128), wP
            meet()
            for lv in range(6):
                M = C("level")[:, lv * 128:(lv + 1) * 128]
                tp = []
                for i in range(4):
                    b, free = pr.take()
                    pe.wait(free)
                    for j in range(4):
                        g = 4 * i + j
                        t = mm(ps[b][:, j * 128:j * 128 + 128], AT[:, g, :], ident if lv == 0 else TM[:, g, :],
                               True, True, inc=(j == 3))
                    t = tt(dve, PM[:, 4 * i:4 * i + 4, :], ps[b][:, :].rearrange("p (a b) -> p a b", a=4),
                           bc(M, 4), ALU.mult, t)
                    pr.rel(b, t)
                    tp.append(t)
                for i in range(4):
                    b, free = pr.take()
                    b2, free2 = pr.take()
                    pe.wait(free, free2, tp[i])
                    for j in range(4):
                        g = 4 * i + j
                        mm(ps[b][:, j * 128:j * 128 + 128], ident if lv == 0 else TTm[:, g, :], PM[:, g, :], True,
                           True)
                        t = mm(ps[b2][:, j * 128:j * 128 + 128], PM[:, g, :], ident if lv == 0 else TTm[:, g, :],
                               True, True, inc=(j == 3))
                    for bb, X in ((b, TM), (b2, TTm)):
                        o = X[:, 4 * i:4 * i + 4, :]
                        old = bc(ident, 4) if lv == 0 else o
                        t1 = tt(dve, o, old, ps[bb][:, :].rearrange("p (a b) -> p a b", a=4), ALU.subtract, t)
                        pr.rel(bb, t1)
                pe.wait(dve.last())
            KC = S(7, 16, 128)
            meet()
            for i in range(4):
                b, free = pr.take()
                pe.wait(free)
                for j in range(4):
                    g = 4 * i + j
                    t = mm(ps[b][:, j * 128:j * 128 + 128], kg[:, g, :], TTm[:, g, :], True, True, inc=(j == 3))
                t = afn(flat(KC[:, 4 * i:4 * i + 4, :]), ps[b][:, :], ACT.Copy, t, scale=-1.0)
                pr.rel(b, t)
            meet()
            st = S(1, 8, 128)
            vn = S(4, 8, 128)
            oT = PM.rearrange("p a b -> p (a b)").rearrange("p (a b) -> p a b", b=256)
            for c in range(4):
                m, off = c // 2, (c % 2) * 64
                vb = []
                for i in range(2):
                    b, free = pr.take()
                    pe.wait(free, dve.last())
                    for j in range(4):
                        h = 4 * i + j
                        o = ps[b][off:off + 64, j * 128:j * 128 + 128]
                        t = mm(o, TTm[:, 2 * h + m, off:off + 64], vt[:, 2 * h + m, :], True, c == 0, inc=True)
                        if c:
                            t = mm(o, KC[:, 2 * h + m, off:off + 64], st[:, h, :], False, True, inc=True)
                    t = tt(dve, vn[off:off + 64, 4 * i:4 * i + 4, :],
                           ps[b][off:off + 64, :].rearrange("p (a b) -> p a b", a=4),
                           inner(be[off:off + 64, m, 4 * i:4 * i + 4], 128), ALU.mult, t)
                    pr.rel(b, t)
                    vb.append(t)
                b, free = pr.take()
                pe.wait(free, vb)
                for h in range(8):
                    o = ps[b][:, h * 64:h * 64 + 64]
                    t = mm(o, vn[off:off + 64, h, :], QK[off:off + 64, 2 * h + m, off:off + 64], True, c == 0,
                           inc=True)
                    if c:
                        t = mm(o, st[:, h, :], qT[:, h, c * 64:c * 64 + 64], False, True, inc=True)
                t_o = afn(oT[:, :, c * 64:c * 64 + 64], ps[b][:, :].rearrange("p (h i) -> p h i", h=8), ACT.Copy, t)
                pr.rel(b, t_o)
                if c < 3:
                    for i in range(2):
                        b, free = pr.take()
                        pe.wait(free)
                        for j in range(4):
                            h = 4 * i + j
                            t = mm(ps[b][:, j * 128:j * 128 + 128], ke[off:off + 64, 2 * h + m, :],
                                   vn[off:off + 64, h, :], True, True, inc=(j == 3))
                        for j in range(4):
                            h = 4 * i + j
                            u = ps[b][:, j * 128:j * 128 + 128]
                            if c == 0:
                                t1 = copy(st[:, h, :], u, t)
                            else:
                                t1 = stt(st[:, h, :], st[:, h, :], DL[:, c * 8 + h:c * 8 + h + 1], u, ALU.mult,
                                         ALU.add, t)
                        pr.rel(b, t1)
            mix = S(0, 8, 256)
            meet()
            t = gated_norm(oT, gate, mix, 8, cv1("odn"), t_o)
            meet()
            return out_proj(A["od_w_out"][0], mix, t)

        wP = sb("wP", [128, 16, 128])

        def rms_mod(src, base, gi, tok, dst, mcols=None):
            u, sq = S(8, 8, 256), S(7, 8, 256)
            t = afn(sq, src, ACT.Square, tok)
            b, t = col_sum(sq, 8, None, t)
            t = rsqrt(rs_t[:, 0, 0:256], rs_t[:, 1, 0:256], ps[b][:, 0:256], 1.0 / D, 1e-6, t)
            pr.rel(b, t)
            t = tt(dve, u, src, bc(rs_t[:, 0, 0:256], 8), ALU.mult, t, tok)
            for j in range(8):
                if mcols is None:
                    sc, sh = mc(base, 1, j), mc(base, 0, j)
                else:
                    sc, sh = mcols[:, 1, j:j + 1], mcols[:, 0, j:j + 1]
                t1 = ts(dve, u[:, j, :], u[:, j, :], vc(gi, j), sc, ALU.mult, ALU.mult, t, t_sm)
                t2 = ts(dve, dst[:, j, :], u[:, j, :], sh, None, ALU.add, None, t1)
            return t2

        s_cx = sem("s_cx")

        def attn_layer(t_x):
            w = A["ev_w_in_2"][0]
            free = meet()
            cin = S(6, 2, 1024)
            t = dma(pool, cin, A["ctx_2"][0].rearrange("(t p) n -> p t n", p=128), s_cx, *free)
            cT, hc = S(5, 8, 256), S(4, 8, 256)
            t = to_features(cin, cT, t)
            t_c = rms_mod(cT, 12, 8, t, hc, modc)
            meet()
            t_h = rms_mod(xT[:, :, :], 12, 8, t_x, hT)
            meet()

            def flat(v):
                return v.rearrange("p a b -> p (a b)")

            q = S(0, 8, 256)
            kk = S(1, 8, 256)
            v = S(2, 4, 256)
            av, ag = S(2, 8, 256)[:, 4:6, :], S(2, 8, 256)[:, 6:8, :]
            bg = S(3, 8, 256)

            def to(dst):
                return lambda p, t: afn(flat(dst), p[:, :], ACT.Copy, t)

            proj_f(w, 0, 256, hT, to(av), t_h)
            proj_f(w, 256, 256, hT, to(ag), t_h)
            for i in range(3):
                proj_f(w, 512 + 256 * i, 256, hT, to(q[:, 2 * i:2 * i + 2, :]), t_h)
            for c0, dst in ((1280, kk), (1536, None)):
                u = cols(w, c0, 256)
                for src, o in ((hc, 0), (hT, 1)):
                    b, free = pr.take()
                    pe.wait(u.tok, free, t_h, t_c)
                    for m in range(2):
                        for k in range(8):
                            a1 = u.v[:, k, m * 128:m * 128 + 128] if dst is not None else \
                                src[:, k, m * 128:m * 128 + 128]
                            a2 = src[:, k, :] if dst is not None else u.v[:, k, :]
                            t = mm(ps[b][:, m * 256:m * 256 + 256], a1, a2, k == 0, k == 7, inc=(k == 7))
                    if dst is not None:
                        t1 = copy(flat(kk[:, 2 * o:2 * o + 2, :]), ps[b][:, :], t)
                    else:
                        t1 = copy(flat(v[:, 2 * o:2 * o + 2, :]), ps[b][:, :], t)
                    pr.rel(b, t1)
                wr.rel(u.i, t)
            for i in range(3):
                proj_f(w, 1792 + 256 * i, 256, hT, to(bg[:, 2 * i:2 * i + 2, :]), t_h)
            meet()
            sq = S(7, 8, 256)
            rn = S(6, 8, 256)
            for x, n, nm in ((q, 6, "qn"), (kk, 4, "kn")):
                t = afn(sq[:, 0:n, :], x[:, 0:n, :], ACT.Square, dve.last(), pe.last())
                for i in range(n // 2):
                    b, free = pr.take()
                    t1 = mm(ps[b][:, :], ones, sq[:, 2 * i:2 * i + 2, :], True, True, free, t, inc=True)
                    t2 = rsqrt(flat(rn[:, 2 * i:2 * i + 2, :]), rs_t[:, i % 2, :], ps[b][:, :], 1.0 / 128, 1e-6,
                               t1, dve.last())
                    pr.rel(b, t2)
                t = stt(x[:, 0:n, :], x[:, 0:n, :], cv1(nm), rn[:, 0:n, :], ALU.mult, ALU.mult, t2)
            meet()
            for x, j in [(q, j) for j in range(6)] + [(kk, 2), (kk, 3)]:
                b, free = pr.take()
                t = mm(ps[b][:, 0:256], C("rot"), x[:, j, :], True, True, free, t_c2, inc=True)
                t = tt(dve, ps[b][:, 256:512], ps[b][:, 0:256], C("sinr"), ALU.mult, t)
                t1 = tt(dve, x[:, j, :], x[:, j, :], C("cosr"), ALU.mult, t)
                t = tt(dve, x[:, j, :], x[:, j, :], ps[b][:, 256:512], ALU.add, t1)
                pr.rel(b, t)
            t = None
            kr = wP[:, 0:8, :].rearrange("p a b -> p (a b)").rearrange("p (g n) -> p g n", g=2)
            for g in range(2):
                copy(kr[:, g, 0:256], kk[:, g, :], dve.last())
                t = copy(kr[:, g, 256:512], kk[:, 2 + g, :])
            mix = S(7, 8, 256)
            meet()
            P = S(4, 4, 512)
            PT = S(5, 2, 4, 256)
            scale = 128 ** -0.5
            for hp in range(3):
                for i in range(4):
                    h, qt = 2 * hp + i // 2, i % 2
                    b, free = pr.take()
                    t = mm(ps[b][:, :], q[:, h, qt * 128:qt * 128 + 128], kr[:, h // 3, :], True, True, free,
                           inc=True)
                    t = dve.do(lambda e, b=b, i=i: e.tensor_reduce(stat[:, 0, i:i + 1], ps[b][:, :], AX.X,
                                                                   ALU.max), t)
                    t = ts(dve, stat[:, 0, i:i + 1], stat[:, 0, i:i + 1], -scale, None, ALU.mult, None, t)
                    t = afn(P[:, i, :], ps[b][:, :], ACT.Exp, t, pe.last(), bias=stat[:, 0, i:i + 1], scale=scale,
                            acc=stat[:, 1, i:i + 1])
                    pr.rel(b, t)
                    t = dve.do(lambda e, i=i: e.reciprocal(stat[:, 2, i:i + 1], stat[:, 1, i:i + 1]), t)
                    tp = ts(dve, P[:, i, :], P[:, i, :], stat[:, 2, i:i + 1], None, ALU.mult, None, t)
                for i in range(2):
                    for k2 in range(2):
                        b, free = pr.take()
                        pe.wait(free, tp)
                        for kt in range(2):
                            for qt in range(2):
                                t = tr(ps[b][:, kt * 256 + qt * 128:kt * 256 + qt * 128 + 128],
                                       P[:, 2 * i + qt, (2 * k2 + kt) * 128:(2 * k2 + kt) * 128 + 128],
                                       inc=(kt == 1 and qt == 1))
                        t = copy(flat(PT[:, i, 2 * k2:2 * k2 + 2, :]), ps[b][:, :], t)
                        pr.rel(b, t)
                for i in range(2):
                    h = 2 * hp + i
                    b, free = pr.take()
                    pe.wait(free, dve.last())
                    for kt in range(4):
                        t = mm(ps[b][:, 0:256], v[:, kt, (h // 3) * 128:(h // 3) * 128 + 128], PT[:, i, kt, :],
                               kt == 0, kt == 3, inc=(kt == 3))
                    t = afn(mix[:, 2 + h, :], ps[b][:, 0:256], ACT.Copy, t)
                    pr.rel(b, t)
            meet()
            cs = S(6, 2, 272)
            dd = S(5, 2, 256)
            t = dve.do(lambda e: e.memset(cs[:, :, 0:9], 0.0))
            for j in range(2):
                t = dve.do(lambda e, j=j: e.tensor_tensor_scan(cs[:, j, 9:265], ones[:, 0:1].broadcast_to([128, 256]),
                                                               av[:, j, :], 0.0, ALU.mult, ALU.add), t)
            for j in range(2):
                t = copy(cs[:, j, 265:272], cs[:, j, 264:265].broadcast_to([128, 7]), t)
            for g, wd in enumerate((2, 4, 8, 16)):
                j, po, hw = g // 2, (g % 2) * 64, wd // 2
                t1 = tt(dve, dd[po:po + 64, j, :], cs[po:po + 64, j, 8 + hw:264 + hw],
                        cs[po:po + 64, j, 8 - hw:264 - hw], ALU.subtract, t)
            t1 = tt(dve, flat(dd), flat(dd), C("icnt"), ALU.mult, t1)
            t1 = tt(dve, dd, dd, av, ALU.subtract, t1)
            b, free = pr.take()
            pe.wait(free, t1)
            t = None
            for g in (0, 2, 1, 3):
                j, po = g // 2, (g % 2) * 64
                t = mm(ps[b][po:po + 64, j * 256:j * 256 + 256], poolw[po:po + 64, j, :], dd[po:po + 64, j, :],
                       True, True, t if g == 1 else None, inc=(g >= 2))
            for j in range(2):
                t1 = ts(dve, mix[:, j, :], ps[b][:, j * 256:j * 256 + 256], cv1("psc", j), None, ALU.mult, None, t)
            pr.rel(b, t1)
            t = afn(ag, ag, ACT.Silu)
            t = afn(bg[:, 0:6, :], bg[:, 0:6, :], ACT.Silu)
            t = tt(dve, mix[:, 0:2, :], mix[:, 0:2, :], ag, ALU.mult, t, t1)
            t = tt(dve, mix[:, 2:8, :], mix[:, 2:8, :], bg[:, 0:6, :], ALU.mult, t)
            meet()
            t_y = out_proj(A["ev_w_out_2"][0], mix, t)
            for j in range(8):
                t = stt(xT[:, j, :], Y(j), mc(12, 2, j), xT[:, j, :], ALU.mult, ALU.add, t_y)
            give_y(t)
            return t

        raw3 = misc[:, 0:2 * 516].rearrange("p (r m n) -> p r m n", r=2, m=2)
        s_w3 = sem("s_hw3")
        hd = misc[0:64, 0:1536].rearrange("p (a n) -> p a n", a=6)
        nrm = sb("nrm", [128, 2, 12])

        def sin_layer(dst, src, bi, tok):
            x, k = hd[:, 4, :], hd[:, 5, :]
            fr = colv[0:64, 2, 2:3]
            t = ts(dve, x, src, colv[0:64, 2, bi:bi + 1], fr, ALU.add, ALU.mult, tok, t_cols)
            big = 12582912.0
            t = ts(dve, k, x, 1.0 / (2 * math.pi), big, ALU.mult, ALU.add, t)
            t = ts(dve, k, k, big, None, ALU.subtract, None, t)
            c1 = 6.28125
            c2 = float(np.float32(2 * math.pi - c1))
            t = stt(x, k, -c1, x, ALU.mult, ALU.add, t)
            t = stt(x, k, -c2, x, ALU.mult, ALU.add, t)
            pi = 3.1415925
            t = ts(dve, x, x, pi, -pi, ALU.min, ALU.max, t)
            return afn(dst, x, ACT.Sin, t)

        def hyena_layer(t_x):
            w = A["od_w_in_2"][0]
            fr = meet()
            w3 = wP[0:64, :, :].rearrange("p a b -> p (a b)")
            w3b = kc_x[0:64, :, :].rearrange("p a b -> p (a b)")
            dma(pool, w3, A["hy_w3_2"][0][:, 0:2048], s_w3, *fr)
            t_w3 = dma(pool, w3b, A["hy_w3_2"][0][:, 2048:3072], s_w3, *fr)
            t_h = rms_mod(xT[:, :, :], 15, 9, t_x, hT)
            meet()

            def flat(v):
                return v.rearrange("p a b -> p (a b)")

            b, free = pr.take()
            t = mm(ps[b][0:64, 0:256], hw12[0:33, 0, :], C("emb")[0:33, :], True, True, free, t_c2, inc=True)
            t = sin_layer(hd[:, 0, :], ps[b][0:64, 0:256], 0, t)
            pr.rel(b, t)
            b, free = pr.take()
            t = mm(ps[b][0:64, 0:256], hw12[:, 1, :], hd[:, 0, :], True, True, free, t, inc=True)
            t = sin_layer(hd[:, 1, :], ps[b][0:64, 0:256], 1, t)
            pr.rel(b, t)
            hs, hdif = [S(0, 1536), S(1, 1536)], [S(2, 1536), S(3, 1536)]
            fa, fb = S(7, 1536), S(8, 1536)
            dec = C("dec")
            nb, nfree = pr.take()
            first = True
            pe.wait(nfree, t, t_w3)
            onec = one_c
            for m in range(2):
                meet()
                for o in range(2):
                    for dr in range(2):
                        dst = (fa if dr == 0 else fb)[:, o * 768:o * 768 + 768]
                        for hf in range(2):
                            c0 = o * 1536 + dr * 768 + hf * 384
                            b, free = pr.take()
                            if b == nb:
                                pr.rel(b, *free)
                                b, free = pr.take()
                            pe.wait(free)
                            lhs = hd[:, 1, m * 128:m * 128 + 128]
                            parts = [(c0, c0 + 384)] if c0 + 384 <= 2048 or c0 >= 2048 else \
                                [(c0, 2048), (2048, c0 + 384)]
                            for (a0, a1) in parts:
                                rhs = w3[:, a0:a1] if a1 <= 2048 else w3b[:, a0 - 2048:a1 - 2048]
                                t = mm(ps[b][:, a0 - c0:a1 - c0], lhs, rhs, True, True, inc=True)
                            t = tt(dve, dst[:, hf * 384:hf * 384 + 384], ps[b][:, 0:384],
                                   dec[:, m * 768 + hf * 384:m * 768 + hf * 384 + 384], ALU.mult, t, t_c2)
                            pr.rel(b, t)
                ab = S(6, 1536)
                for f, x in enumerate((fa, fb)):
                    t = afn(ab, x, ACT.Abs, dve.last(), pe.last())
                    pe.wait(t)
                    for g in range(12):
                        lst = m == 1 and f == 1 and g == 11
                        t = mm(ps[nb][:, g:g + 1], ab[:, g * 128:g * 128 + 128], onec, first and g == 0, lst,
                               inc=(g == 11), skip=True)
                    first = False
                if m == 0:
                    t = dve.do(lambda e: e.memset(fb[0:1, :], 0.0), t)
                t = tt(dve, hs[m], fa, fb, ALU.add, t)
                t = tt(dve, hdif[m], fa, fb, ALU.subtract, t)
            t = ts(dve, nrm[:, 0, :], ps[nb][:, 0:12], 1e-6, None, ALU.add, None, pe.last())
            t = dve.do(lambda e: e.reciprocal(nrm[:, 1, :], nrm[:, 0, :]), t)
            pr.rel(nb, t)
            meet()
            KR = [S(4, 1536), S(5, 1536)]
            KI = [S(6, 1536), S(7, 1536)]
            DC = C("dc").rearrange("p (a b) -> p a b", a=2)
            DS = C("ds").rearrange("p (a b) -> p a b", a=2)
            for f in range(2):
                for mat, src, dst, sc in ((DC, hs, KR, 1.0), (DS, hdif, KI, -1.0)):
                    for c in range(3):
                        b, free = pr.take()
                        pe.wait(free)
                        for m in range(2):
                            t = mm(ps[b][:, :], mat[:, m, f * 128:f * 128 + 128], src[m][:, c * 512:c * 512 + 512],
                                   m == 0, m == 1, inc=(m == 1))
                        t = afn(dst[f][:, c * 512:c * 512 + 512], ps[b][:, :], ACT.Copy, t, scale=sc)
                        pr.rel(b, t)
            meet()
            t_r3 = pool.do(lambda e: e.memset(misc[:, 0:1032], 0.0))
            z = S(0, 8, 256)
            x1, x2 = S(1, 8, 256), S(2, 8, 256)
            gt = S(3, 8, 256)
            r3 = Ring(range(2))

            def conv3(dst, j0):
                def ev(p, t):
                    r, free = r3.take()
                    t = afn(raw3[:, r, :, 1:257], p[:, :].rearrange("p (m n) -> p m n", m=2), ACT.Copy, t, t_r3,
                            free)
                    for m in range(2):
                        x = raw3[:, r, m, :]
                        j = j0 + m
                        t1 = ts(dve, dst[:, m, :], x[:, 0:256], cv1("hcw", j), cv1("hcb", j), ALU.mult, ALU.add,
                                t)
                        for k in (1, 2):
                            t1 = stt(dst[:, m, :], x[:, k:k + 256], cv1("hcw", k * 18 + j), dst[:, m, :],
                                     ALU.mult, ALU.add, t1)
                    r3.rel(r, t1)
                    return t
                return ev

            for s, dst in ((0, z), (1, x1), (2, x2)):
                for i in range(3):
                    proj_f(w, s * 768 + 256 * i, 256, hT, conv3(dst[:, 2 * i:2 * i + 2, :], s * 6 + 2 * i), t_h)
            for i in range(3):
                g = gt[:, 2 * i:2 * i + 2, :]
                proj_f(w, 2304 + 256 * i, 256, hT,
                       lambda p, t, g=g: afn(g, p[:, :].rearrange("p (m n) -> p m n", m=2), ACT.Silu, t), t_h)
            fin = z[:, 6:8, :]
            proj_f(w, 3072, 256, hT, lambda p, t: copy(flat(fin), p[:, :], t), t_h)
            g = gt[:, 6:8, :]
            proj_f(w, 3328, 256, hT, lambda p, t: afn(flat(g), p[:, :], ACT.Silu, t), t_h)
            meet()
            CT = C("dct").rearrange("p (a b) -> p a b", a=2)
            ST = C("dst").rearrange("p (a b) -> p a b", a=2)
            zt = wP[:, 0:12, :].rearrange("p a b -> p (a b)").rearrange("p (m n) -> p m n", m=2)
            ZR, ZI = S(8, 2048)[:, 0:768], S(8, 2048)[:, 768:1536]
            tmp = kc_x[:, :, :].rearrange("p a b -> p (a b)")[:, 0:768]
            YR = [hT[:, :, :].rearrange("p a b -> p (a b)")[:, 0:768],
                  hT[:, :, :].rearrange("p a b -> p (a b)")[:, 768:1536]]
            YI = [yib[:, 0, :], yib[:, 1, :]]
            for o in range(2):
                for j in range(6):
                    b, free = pr.take()
                    pe.wait(free)
                    for m in range(2):
                        t = tr(ps[b][:, m * 128:m * 128 + 128], z[:, j, m * 128:m * 128 + 128], inc=(m == 1))
                    t = copy(zt[:, :, j * 128:j * 128 + 128], ps[b][:, 0:256].rearrange("p (m n) -> p m n", m=2), t)
                    pr.rel(b, t)
                meet()
                for f in range(2):
                    for mat, dst, sc in ((DC, ZR, 1.0), (DS, ZI, -1.0)):
                        for c in range(2):
                            b, free = pr.take()
                            pe.wait(free)
                            for m in range(2):
                                t = mm(ps[b][:, 0:384], mat[:, m, f * 128:f * 128 + 128],
                                       zt[:, m, c * 384:c * 384 + 384], m == 0, m == 1, inc=(m == 1))
                            t = afn(dst[:, c * 384:c * 384 + 384], ps[b][:, 0:384], ACT.Copy, t, dve.last(),
                                    scale=sc)
                            pr.rel(b, t)
                    kr, ki = KR[f][:, o * 768:o * 768 + 768], KI[f][:, o * 768:o * 768 + 768]
                    t = tt(dve, YR[f], ZR, kr, ALU.mult, t)
                    t = tt(dve, tmp, ZI, ki, ALU.mult, t)
                    t = tt(dve, YR[f], YR[f], tmp, ALU.subtract, t)
                    t = tt(dve, YI[f], ZR, ki, ALU.mult, t)
                    t = tt(dve, tmp, ZI, kr, ALU.mult, t)
                    t = tt(dve, YI[f], YI[f], tmp, ALU.add, t)
                meet()
                gx = x1 if o == 0 else x2
                for j in range(6):
                    b, free = pr.take()
                    pe.wait(free)
                    for f in range(2):
                        mm(ps[b][:, 0:256], YR[f][:, j * 128:j * 128 + 128], CT[:, f, :], f == 0, False)
                        t = mm(ps[b][:, 0:256], YI[f][:, j * 128:j * 128 + 128], ST[:, f, :], False, f == 1,
                               inc=(f == 1))
                    r = rs_t[:, j % 2, 0:256]
                    t = afn(r, ps[b][:, 0:256], ACT.Copy, t, dve.last(), scale=nrm[:, 1, o * 6 + j:o * 6 + j + 1])
                    pr.rel(b, t)
                    t = stt(z[:, j, :], z[:, j, :], cv1("skip", o * 6 + j), r, ALU.mult, ALU.add, t)
                    t = tt(dve, z[:, j, :], z[:, j, :], gx[:, j, :], ALU.mult, t)
                meet()
            FC = C("fc").rearrange("p (a b) -> p a b", a=2)
            FS = C("fs").rearrange("p (a b) -> p a b", a=2)
            PQ = S(1, 8, 256)
            for m in range(2):
                for q, mat in ((0, FC), (1, FS)):
                    b, free = pr.take()
                    pe.wait(free)
                    for c in range(2):
                        t = mm(ps[b][:, 0:256], fin[:, c, m * 128:m * 128 + 128], mat[:, c, :], c == 0, c == 1,
                               inc=(c == 1))
                    t = afn(PQ[:, 2 * q + m, :], ps[b][:, 0:256], ACT.Copy, t, scale=1.0 if q == 0 else -1.0)
                    pr.rel(b, t)
            yt = S(2, 8, 256)
            pe.wait(t)
            for j in range(2):
                b, free = pr.take()
                pe.wait(free)
                n = 0
                for q, mat in ((0, FC), (1, FS)):
                    for m in range(2):
                        t = mm(ps[b][:, 0:256], PQ[:, 2 * q + m, j * 128:j * 128 + 128], mat[:, m, :], n == 0,
                               n == 3, inc=(n == 3))
                        n += 1
                t = afn(yt[:, j, :], ps[b][:, 0:256], ACT.Copy, t, scale=1.0 / 256)
                pr.rel(b, t)
            u = unit(A["fn_w_2"][0].rearrange("(k p) n -> p k n", p=128), 2, 256)
            for j in range(2):
                b, free = pr.take()
                pe.wait(free, u.tok, act.last())
                for c in range(2):
                    t = mm(ps[b][:, 0:256], u.v[:, c, j * 128:j * 128 + 128], yt[:, c, :], c == 0, c == 1,
                           inc=(c == 1))
                t1 = tt(dve, z[:, 6 + j, :], ps[b][:, 0:256], gt[:, 6 + j, :], ALU.mult, t)
                pr.rel(b, t1)
            wr.rel(u.i, t)
            t = tt(dve, z[:, 0:6, :], z[:, 0:6, :], gt[:, 0:6, :], ALU.mult, t1)
            meet()
            t_y = out_proj(A["od_w_out_2"][0], z, t)
            for j in range(8):
                t = stt(xT[:, j, :], Y(j), mc(15, 2, j), xT[:, j, :], ALU.mult, ALU.add, t_y)
            give_y(t)
            return t

        yib = misc[:, 0:1536].rearrange("p (a n) -> p a n", a=2)

        def whole():
            t_m = fill_to(36 - 4)
            t_h = scale_shift(hT, xT, lambda j: mc(0, 1, j), lambda j: mc(0, 0, j), t_m, t_x)
            if STOP == "h0":
                return t_h
            fill_rate[0] = R0
            t_y = even_mixer(t_h)
            fill_rate[0] = 0
            t_h = residual(0, 2, t_y, 0, 0, 0, 3)
            if STOP == "x1":
                return t_h
            t_y = moe(0, t_h)
            fill_to(12)
            t_h = residual(0, 5, t_y, 4, 0, 6, 0)
            if STOP == "x2":
                return t_h
            fill_rate[0] = R1
            t_y = delta_mixer(t_h)
            fill_rate[0] = 0
            t_h = residual(6, 2, t_y, 0, 1, 6, 3)
            if STOP == "x3":
                return t_h
            t_y = moe(1, t_h)
            t_xx = residual(6, 5, t_y, 4, 1, None, 0)
            if STOP == "x4":
                return t_xx
            fill_to(0)
            t_xx = attn_layer(t_xx)
            if STOP == "x5":
                return t_xx
            return hyena_layer(t_xx)

        t_end = whole()
        meet()
        u, sq = S(8, 8, 256), S(7, 8, 256)
        if STOP is None:
            t = afn(sq, xT[:, :, :], ACT.Square, t_end)
            b, t = col_sum(sq, 8, None, t)
            t = rsqrt(rs_t[:, 0, 0:256], rs_t[:, 1, 0:256], ps[b][:, 0:256], 1.0 / D, 1e-6, t)
            pr.rel(b, t)
            t = tt(dve, u, xT[:, :, :], bc(rs_t[:, 0, 0:256], 8), ALU.mult, t)
            for j in range(8):
                t1 = ts(dve, u[:, j, :], u[:, j, :], vc(10, j), None, ALU.mult, None, t, t_sm)
            t = t1
        else:
            t = copy(u, xT[:, :, :], t_end)
        xo = S(6, 2, 1024)
        for m in range(2):
            for k2 in range(2):
                b, free = pr.take()
                pe.wait(free, t)
                for kk in range(4):
                    tp = tr(ps[b][:, kk * 128:kk * 128 + 128], u[:, 4 * k2 + kk, m * 128:m * 128 + 128],
                            inc=(kk == 3))
                o = xo[:, m, :].rearrange("p (f k) -> p k f", k=8)[:, 4 * k2:4 * k2 + 4, :]
                t1 = copy(o, ps[b][:, :].rearrange("p (k f) -> p k f", k=4), tp)
                pr.rel(b, t1)
        s_out = sem("s_out")
        t = dma(sp, out[0].rearrange("(t p) n -> p t n", p=128), xo, s_out, t1)
        sp.wait(t)

        block = ctx.enter_context(nc.Block())

        @block.sync
        def _(e):
            sp.emit(e)

        @block.gpsimd
        def _(e):
            pool.emit(e)

        @block.scalar
        def _(e):
            act.emit(e)

        @block.vector
        def _(e):
            dve.emit(e)

        @block.tensor
        def _(e):
            pe.emit(e)


def kernel(**inputs):
    import numpy as _np
    import concourse.bacc as _bacc
    from concourse import mybir as _mybir
    from concourse.bass_utils import run_bass_kernel_spmd as _run

    nc = _bacc.Bacc("TRN2", target_bir_lowering=False, num_devices=1)
    consts, at, lo = shape_constants()
    arrays, args = {}, {}
    for name, a in list(inputs.items()) + [("consts", consts)]:
        a = _np.ascontiguousarray(a)
        arrays[f"in_{name}"] = a
        args[name] = nc.dram_tensor(f"in_{name}", a.shape, _mybir.dt.from_np(a.dtype), kind="ExternalInput").ap()
    o = nc.dram_tensor("out_0", (1, 256, 1024), _mybir.dt.float32, kind="ExternalOutput").ap()
    build(nc, args, o, at, lo)
    r = _run(nc, [arrays], core_ids=[0])
    return r.results[0]["out_0"]
```

```python
import math
from contextlib import ExitStack

import numpy as np

import concourse.bass as bass
from concourse import mybir

F32 = mybir.dt.float32
ACT = mybir.ActivationFunctionType
ALU = mybir.AluOpType
AX = mybir.AxisListType

D = 1024
T = 256
NE = 64
ALPHA = float(4 ** 0.25)
CAP = 64
R0, R1 = 3, 2


def shape_constants():
    p = np.arange(128)
    blk = {}
    blk["ident"] = np.eye(128)
    blk["flip"] = np.eye(128)[::-1]
    blk["ones"] = np.ones((128, 128))
    same = (p[:, None] // 64) == (p[None, :] // 64)
    blk["incl"] = (same & (p[:, None] <= p[None, :])).astype(float)
    blk["after"] = (same & (p[:, None] > p[None, :])).astype(float)
    blk["same"] = same.astype(float)
    blk["before"] = (p[:, None] < p[None, :]).astype(float)
    blk["pick"] = (p[:, None] % 32 == np.arange(2)[None, :]).astype(float)
    blk["iota"] = np.broadcast_to(np.arange(64), (128, 64))
    lv = []
    for b in (1, 2, 4, 8, 16, 32):
        pair = (p[:, None] // (2 * b)) == (p[None, :] // (2 * b))
        lv.append(pair & (p[:, None] % (2 * b) >= b) & (p[None, :] % (2 * b) < b))
    blk["level"] = np.stack(lv, 1).reshape(128, -1).astype(float)
    rot = np.zeros((128, 128))
    for a in range(2):
        for i in range(32):
            rot[a * 64 + 32 + i, a * 64 + i] = -1.0
            rot[a * 64 + i, a * 64 + 32 + i] = 1.0
    blk["rot"] = rot
    t = np.arange(T)
    inv = (np.float32(10000.0) ** (-np.arange(32, dtype=np.float32) / np.float32(32))).astype(np.float32)
    row = (t // 64).astype(np.float32)
    col = (t % 64).astype(np.float32)
    ang = np.stack([row[:, None] * inv, col[:, None] * inv], 1)
    ang = np.broadcast_to(ang[:, :, None, :], (T, 2, 2, 32)).reshape(T, 128).T.astype(np.float64)
    blk["cosr"] = np.cos(ang)
    blk["sinr"] = np.sin(ang)
    s = np.arange(256)
    w = (2 * s[None, :] + 1) * np.pi / 512 * s[:, None]
    for name, m in (("dc", np.cos(w)), ("ds", np.sin(w)), ("dct", np.cos(w).T / 256), ("dst", -np.sin(w).T / 256),
                    ("fc", np.cos(2 * np.pi * s[:, None] * s / 256)), ("fs", np.sin(2 * np.pi * s[:, None] * s / 256))):
        blk[name] = m.reshape(2, 128, 256).transpose(1, 0, 2).reshape(128, 512)
    ic = np.zeros((2, 128, 256))
    for g, wd in enumerate((2, 4, 8, 16)):
        cnt = np.clip(t + wd // 2, 0, T) - np.clip(t - wd // 2, 0, T)
        ic[g // 2, (g % 2) * 64:(g % 2) * 64 + 64] = 1.0 / cnt
    blk["icnt"] = ic.transpose(1, 0, 2).reshape(128, 512)
    hot = np.zeros((128, 512))
    for m in range(512):
        d = 255 - m
        if d < 0:
            hot[32, m] = 1.0
        else:
            if d < 16:
                bkt = d
            else:
                lg = np.float32(np.log(np.float32(d) / np.float32(16)))
                bkt = min(16 + int(np.float32(lg / np.float32(math.log(128.0)) * np.float32(16))), 31)
            hot[bkt, m] = 1.0
    blk["hot"] = hot
    lin = np.linspace(0.0, 1.0, T, dtype=np.float32)
    wv = (np.float32(2.0 * math.pi) * np.arange(T, dtype=np.float32)[:, None] / np.float32(T)).astype(np.float32)
    f = np.linspace(1e-4, 15, 16, dtype=np.float32)[None, :]
    fw = (f * wv).astype(np.float64)
    emb = np.concatenate([lin[:, None], np.cos(fw), -np.sin(fw)], -1)
    e = np.zeros((128, 256))
    e[:33] = emb.T
    blk["emb"] = e
    deltas = np.linspace(math.log(1e-2) / 1.5, math.log(1e-2) / 0.3, 768, dtype=np.float32)
    dec = np.exp((-lin[:, None] * np.abs(deltas)).astype(np.float64))
    blk["dec"] = dec.reshape(2, 128, 768).transpose(1, 0, 2).reshape(128, 1536)
    rs = np.ones((128, 512))
    rs[:, ::64] = 0.0
    blk["rset"] = rs
    eps = np.zeros((128, 4))
    eps[:, 0] = 1e-5
    eps[:, 1] = 1e-6
    eps[:, 2] = 1.0
    blk["eps"] = eps
    first = ("ident", "flip", "ones", "eps", "incl", "after", "same", "before", "iota", "pick", "level", "hot", "rset")
    order = list(first) + [n for n in blk if n not in first]
    at, cols, lo = {}, 0, 0
    for n in order:
        at[n] = (cols, blk[n].shape[1])
        cols += blk[n].shape[1]
        if n == first[-1]:
            lo = cols
    return np.concatenate([blk[n] for n in order], 1).astype(np.float32), at, lo


class Queue:

    def __init__(self, sem):
        self.sem, self.n, self.ops, self.seen = sem, 0, [], {}

    def wait(self, *toks):
        for t in toks:
            if t is None:
                continue
            if isinstance(t, list):
                self.wait(*t)
                continue
            s, v = t
            if self.seen.get(s.name, 0) < v:
                self.seen[s.name] = v
                self.ops.append(lambda e, s=s, v=v: e.wait_ge(s, v))

    def do(self, fn, *toks, inc=True):
        self.wait(*toks)
        if not inc:
            self.ops.append(fn)
            return None
        self.n += 1
        self.ops.append(lambda e, s=self.sem: fn(e).then_inc(s, 1))
        return (self.sem, self.n)

    def last(self):
        return (self.sem, self.n)

    def enter(self, sem):
        self.kept = (self.sem, self.n, self.ops, dict(self.seen))
        self.sem, self.n, self.ops = sem, 0, []

    def leave(self, flag):
        body = self.ops
        self.sem, self.n, self.ops, self.seen = self.kept
        self.ops.append((flag, body))

    def emit(self, e):
        for n, op in enumerate(self.ops):
            if isinstance(op, tuple):
                flag, body = op
                reg = e.alloc_register(f"flag{n}_{self.sem.name}")
                e.reg_load(reg, flag)
                with e.If_ne(reg, 0):
                    for o in body:
                        o(e)
            else:
                op(e)


class Ring:

    def __init__(self, ids):
        self.ids, self.at = list(ids), 0
        self.free = {i: [] for i in ids}

    def take(self):
        i = self.ids[self.at % len(self.ids)]
        self.at += 1
        return i, self.free[i]

    def rel(self, i, *toks):
        self.free[i] = list(toks)


def build(nc, A, out, at, lo):
    ctx = ExitStack()
    with ctx:
        def sb(name, shape, dt=F32):
            return ctx.enter_context(nc.sbuf_tensor(name, shape, dt))

        def sem(name):
            return ctx.enter_context(nc.semaphore(name))

        pe, act, dve, pool, sp = (Queue(sem("s_" + n)) for n in ("pe", "act", "dve", "pool", "sp"))
        dcount = {}

        def dma(q, dst, src, s, *toks):
            dcount[s.name] = dcount.get(s.name, 0) + 16
            q.wait(*toks)
            q.ops.append(lambda e: e.dma_start(dst, src).then_inc(s, 16))
            return (s, dcount[s.name])

        NS = 6
        wbuf = sb("wbuf", [128, NS, 2048])
        wsem = [sem(f"s_w{i}") for i in range(NS + 3)]
        wr = Ring(range(NS))
        wsec = []
        cst = sb("cst", [128, A["consts"].shape[1]])
        xT = sb("xT", [128, 8, T])
        hT = sb("hT", [128, 8, T])
        slab = sb("slab", [128, 9, 2048])
        ps = [ctx.enter_context(nc.psum_tensor(f"ps{i}", [128, 512], F32)) for i in range(8)]
        pr = Ring(range(8))

        def C(name):
            c0, n = at[name]
            return cst[:, c0:c0 + n]

        ident, flip, ones = C("ident"), C("flip"), C("ones")
        eps5, eps6 = C("eps")[:, 0:1], C("eps")[:, 1:2]
        one_c = C("eps")[:, 2:3]

        def S(i, *dims):
            v = slab[:, i, :]
            if len(dims) == 1:
                return v[:, 0:dims[0]]
            if len(dims) == 2:
                return v[:, 0:dims[0] * dims[1]].rearrange("p (a b) -> p a b", b=dims[1])
            return v[:, 0:dims[0] * dims[1] * dims[2]].rearrange("p (a b c) -> p a b c", b=dims[1], c=dims[2])

        def bc(v, n):
            return v.unsqueeze(1).broadcast_to([v.shape[0], n, v.shape[1]])

        def inner(v, n):
            return v.unsqueeze(2).broadcast_to([v.shape[0], v.shape[1], n])

        def mm(o, lhsT, rhs, start, stop, *toks, inc=False, skip=False):
            return pe.do(lambda e: e.matmul(o, lhsT, rhs, start=start, stop=stop, skip_group_check=skip),
                         *toks, inc=inc)

        def tr(o, i, *toks, inc=False):
            n = i.shape[0]
            return pe.do(lambda e: e.transpose(o, i, ident[0:n, 0:n]), *toks, inc=inc)

        def afn(o, i, fn, *toks, scale=1.0, bias=0.0, acc=None):
            return act.do(lambda e: e.activation(o, i, fn, bias=bias, scale=scale, accum_out=acc), *toks)

        def tt(q, o, a, b, op, *toks):
            return q.do(lambda e: e.tensor_tensor(o, a, b, op), *toks)

        def ts(q, o, a, s1, s2, op0, op1, *toks):
            if s2 is None:
                return q.do(lambda e: e.tensor_scalar(o, a, s1, None, op0), *toks)
            return q.do(lambda e: e.tensor_scalar(o, a, s1, s2, op0, op1), *toks)

        def stt(o, a, s, b, op0, op1, *toks):
            return dve.do(lambda e: e.scalar_tensor_tensor(o, a, s, b, op0, op1), *toks)

        def copy(o, i, *toks):
            return dve.do(lambda e: e.tensor_copy(o, i), *toks)

        fill_rate = [0]

        def meet():
            all_ = [q.last() for q in (pe, act, dve, pool)]
            fill(fill_rate[0])
            for q in (pe, act, dve, pool):
                q.wait(*all_)
            return all_

        class Unit:
            pass

        def unit(src, a, b):
            u = Unit()
            u.i, free = wr.take()
            u.v = wplace(u.i)[:, 0:a * b].rearrange("p (a b) -> p a b", b=b)
            u.tok = dma(sp, u.v, src, (wsec[-1] if wsec else wsem)[u.i], *free)
            return u

        def wplace(i):
            return wbuf[:, i, :] if i < NS else (slab[:, 7, :], slab[:, 8, :],
                                                 wP[:, :, :].rearrange("p a b -> p (a b)"))[i - NS]

        def pair_unit(g, u_, k0):
            u = Unit()
            u.i, free = wr.take()
            u.v = wplace(u.i).rearrange("p (k n) -> p k n", n=512)
            for half, w in ((0, g), (1, u_)):
                u.tok = dma(sp, u.v[:, :, half * 256:half * 256 + 256],
                            w.rearrange("(p k) n -> p k n", k=8)[:, k0:k0 + 4, :], wsem[u.i], *free)
            return u

        def cols(w, c0, n):
            return unit(w.rearrange("(p k) n -> p k n", k=8)[:, :, c0:c0 + n], 8, n)

        def rows(w, k0):
            return unit(w.rearrange("(k p) n -> p k n", p=128)[:, k0:k0 + 2, :], 2, w.shape[1])

        def proj_f(w, c0, n, rhs, evac, *ready):
            u = cols(w, c0, n)
            b, free = pr.take()
            pe.wait(u.tok, free, *ready)
            for m in range((n + 127) // 128):
                mc = min(128, n - m * 128)
                for k in range(8):
                    t = mm(ps[b][0:mc, m * 256:(m + 1) * 256], u.v[:, k, m * 128:m * 128 + mc], rhs[:, k, :],
                           k == 0, k == 7, inc=(k == 7))
            wr.rel(u.i, t)
            pr.rel(b, evac(ps[b], t))

        def proj_t(w, c0, n, lhs, evac, *ready):
            u = cols(w, c0, n)
            b, free = pr.take()
            pe.wait(u.tok, free, *ready)
            for m in range(2):
                for k in range(8):
                    t = mm(ps[b][:, m * 256:m * 256 + n], lhs[:, k, m * 128:(m + 1) * 128], u.v[:, k, :],
                           k == 0, k == 7, inc=(k == 7))
            wr.rel(u.i, t)
            pr.rel(b, evac(ps[b], t))

        YB = (4, 5, 6, 7)

        def Y(j):
            return ps[YB[j // 2]][:, (j % 2) * 256:(j % 2) * 256 + 256]

        def down(u, rhs, first, last, *ready):
            pe.wait(u.tok, *ready)
            t = None
            for kk in range(2):
                for j in range(8):
                    fin = kk == 1 and j == 7
                    t = mm(Y(j), u.v[:, kk, j::8], rhs[kk], first and kk == 0 and j % 2 == 0,
                           last and kk == 1 and j % 2 == 1, inc=fin, skip=True)
            wr.rel(u.i, t)
            return t

        def take_y():
            toks = []
            for b in YB:
                toks += pr.free[b]
            pr.ids, pr.at = [0, 1, 2, 3], 0
            return toks

        def give_y(tok):
            for b in YB:
                pr.rel(b, tok)
            pr.ids, pr.at = list(range(8)), 0

        s_in = sem("s_in")
        s_c2 = sem("s_c2")
        s_sm = sem("s_sm")
        xin = slab[:, 0:1, :].rearrange("p o n -> p (o n)").rearrange("p (t n) -> p t n", t=2)
        dma(sp, xin, A["x"][0].rearrange("(t p) n -> p t n", p=128), s_in)
        cv = sb("cv", [128, 3, 8])
        dma(sp, cv[:, 0, :], A["c"][0].rearrange("(p k) -> p k", k=8), s_in)
        dma(sp, cv[:, 1, :], A["c_2"][0].rearrange("(p k) -> p k", k=8), s_in)
        dma(sp, cv[:, 2, :], A["c_ctx_2"].rearrange("(p k) -> p k", k=8), s_in)
        t_in = dma(sp, cst[:, 0:lo], A["consts"][:, 0:lo], s_in)
        modb = sb("modb", [128, 18, 8])
        s_mb = sem("s_mb")
        for l in range(2):
            dma(act, modb[:, 6 * l:6 * l + 6, :], A["ada_b"][l].rearrange("(s p k) -> p s k", s=6, k=8), s_mb)
            t_mb = dma(act, modb[:, 12 + 3 * l:15 + 3 * l, :],
                       A["b_mod_2"][l].rearrange("(s p k) -> p s k", s=3, k=8), s_mb)
        cz = sb("cz", [128, 2, 8, 32])

        vec = sb("vec", [128, 21, 8])

        def vload(i, src, n=1):
            if n == 1:
                return dma(pool, vec[:, i, :], src.rearrange("(p k) -> p k", k=8), s_sm)
            return dma(pool, vec[:, i:i + n, :], src.rearrange("s (p k) -> p s k", k=8), s_sm)

        for i, n in enumerate(("ln_mix_g", "ln_mix_b", "ln_ffn_g", "ln_ffn_b")):
            for l in range(2):
                vload(2 * i + l, A[n][l])
        vload(8, A["norm_g_2"][0])
        vload(9, A["norm_g_2"][1])
        vload(10, A["final_g_2"])
        misc = sb("misc", [128, 2048])
        stage = misc[:, 1600:1984].rearrange("p (a b) -> p a b", a=3)
        colv = sb("colv", [128, 3, 128])
        dma(pool, stage[0:96, 0, :], A["od_conv_w"][0].rearrange("k (j p) -> (k j) p", p=128), s_sm)
        row = [0]
        place = {}

        def srow(name, src):
            n = src.shape[0]
            place[name] = row[0]
            dma(pool, stage[row[0]:row[0] + n, 1, :], src, s_sm)
            row[0] += n

        srow("hcw", A["hy_conv_w_2"][0].rearrange("k (j p) -> (k j) p", p=128))
        srow("hcb", A["hy_conv_b_2"][0].rearrange("(j p) -> j p", p=128))
        srow("skip", A["hy_skip_2"][0].rearrange("o (j p) -> (o j) p", p=128))
        srow("psc", A["pool_scale_2"][0].rearrange("(j p) -> j p", p=128))
        srow("evn", A["ev_norm"])
        srow("odn", A["od_norm"])
        srow("qn", A["q_norm_g_2"])
        srow("kn", A["k_norm_g_2"])
        srow("gkb", A["ev_gk_b"][0].rearrange("(j p) -> j p", p=128))
        nrow = row[0]
        for i, n in enumerate(("hy_b1_2", "hy_b2_2", "hy_freq_2")):
            dma(pool, stage[i:i + 1, 2, 0:64], A[n], s_sm)
        rpe33 = sb("rpe33", [33, 4])
        t_rm = pool.do(lambda e: e.memset(rpe33[:, :], -1e30))
        dma(pool, rpe33[0:32, :], A["rpe_bias"], s_sm, t_rm)
        gkw2 = sb("gkw2", [16, 256])
        dma(pool, gkw2[:, :], A["ev_gk_w2"][0], s_sm)
        poolw = sb("poolw", [128, 2, 64])
        dma(pool, poolw[:, :, :], A["pool_w_2"][0].rearrange("(t g) c d -> (g c) t d", t=2), s_sm)
        hw12 = sb("hw12", [64, 2, 64])
        dma(pool, hw12[0:33, 0, :], A["hy_w1_2"][0], s_sm)
        dma(pool, hw12[:, 1, :], A["hy_w2_2"][0], s_sm)
        rtb = sb("rtb", [128, 2, 64])
        for l in range(2):
            dma(pool, rtb[:, l, :], A["moe_router_b"][l:l + 1, :].broadcast_to([128, 64]), s_sm)
        adt = sb("adt", [128, 2, 8])
        dma(pool, adt[:, 0, :], A["od_a_log"].broadcast_to([128, 8]), s_sm)
        t_sm = dma(pool, adt[:, 1, :], A["od_dt_bias"].broadcast_to([128, 8]), s_sm)

        t_c2 = dma(pool, cst[:, lo:], A["consts"][:, lo:], s_c2)

        def vc(i, j):
            return vec[:, i, j:j + 1]

        def cv1(name, j=0):
            r = place[name] + j
            return colv[:, 1, r:r + 1]

        def small_columns():
            nonlocal t_cols
            pe.wait(t_in, t_sm)
            b, free = pr.take()
            tr(ps[b][:, 0:96], stage[0:96, 0, :])
            tr(ps[b][:, 128:128 + nrow], stage[0:nrow, 1, :])
            t = tr(ps[b][0:64, 256:259], stage[0:3, 2, 0:64], inc=True)
            copy(colv[:, 0, 0:96], ps[b][:, 0:96], t)
            copy(colv[:, 1, 0:nrow], ps[b][:, 128:128 + nrow])
            t_cols = copy(colv[0:64, 2, 0:3], ps[b][0:64, 256:259])
            pr.rel(b, t_cols)

        t_cols = None

        def to_features(src, dst, tok, a=False):
            last = None
            for k2 in range(4):
                b, free = pr.take()
                pe.wait(free, tok)
                for kk in range(2):
                    for m in range(2):
                        t = tr(ps[b][:, kk * 256 + m * 128:kk * 256 + m * 128 + 128],
                               src[:, m, 2 * k2 + kk::8], inc=(kk == 1 and m == 1))
                o = dst[:, 2 * k2:2 * k2 + 2, :].rearrange("p a b -> p (a b)")
                last = afn(o, ps[b][:, :], ACT.Copy, t) if a else copy(o, ps[b][:, :], t)
                pr.rel(b, last)
            return last


        t_z = dve.do(lambda e: e.memset(cz[:, :, :, :], 0.0))
        afn(cz[:, 0, :, 0:1], cv[:, 0, :].unsqueeze(2), ACT.Silu, t_in, t_z)
        t_ca = afn(cz[:, 1, :, 0:2].rearrange("p k s -> p s k"), cv[:, 1:3, :], ACT.Silu)
        t_x = to_features(xin, xT, t_in)
        mods = sb("mods", [128, 18, 8])
        modc = sb("modc", [128, 2, 8])
        kc_x = sb("kc_x", [128, 2, 512])
        mrow = Ring((0, 1))
        tasks = []
        later = []
        m_done = {}

        def half_section(w, s, half, base, ctx_too=False):
            def first():
                wv = w.rearrange("(p k) n -> p k n", k=8)
                us = [unit(wv[:, 4 * q:4 * q + 4, s * 1024 + half * 512:s * 1024 + half * 512 + 512], 4, 512)
                      for q in range(2)]
                b, free = pr.take()
                pe.wait(free, t_ca)
                for q in range(2):
                    pe.wait(us[q].tok)
                    for i in range(4):
                        t = mm(ps[b][32 * i:32 * i + 32, :], cz[:, 0 if base < 12 else 1, 4 * q + i, :],
                               us[q].v[:, i, :], q == 0, q == 1, inc=(i == 3), skip=True)
                    wr.rel(us[q].i, t)
                i, rfree = mrow.take()
                t = afn(kc_x[:, i, :], ps[b][:, :], ACT.Copy, t, rfree)
                pr.rel(b, t)
                return i, t

            def second(i, t):
                b, free = pr.take()
                pe.wait(free, t)
                lo_ = 64 * half
                for k in range(8):
                    t = mm(ps[b][lo_:lo_ + 64, 2 * k:2 * k + 2], kc_x[:, i, k::8], C("pick"), True, True,
                           inc=(k == 7), skip=True)
                mrow.rel(i, t)
                pv = ps[b][lo_:lo_ + 64, 0:16].rearrange("p (j v) -> p j v", v=2)
                one = 1.0 if s in (1, 4) and (base < 12 or s == 1) else 0.0
                t1 = stt(mods[lo_:lo_ + 64, base + s, :], pv[:, :, 0], one, modb[lo_:lo_ + 64, base + s, :],
                         ALU.add, ALU.add, t, t_mb)
                if ctx_too:
                    t1 = stt(modc[lo_:lo_ + 64, s, :], pv[:, :, 1], one, modb[lo_:lo_ + 64, base + s, :],
                             ALU.add, ALU.add, t)
                pr.rel(b, t1)
                m_done[base] = t1
            return first, second

        for l in range(2):
            for s_ in range(6):
                for hf in range(2):
                    tasks.append(half_section(A["ada_w"][l], s_, hf, 6 * l))
        for l in range(2):
            for s_ in range(3):
                for hf in range(2):
                    tasks.append(half_section(A["w_mod_2"][l], s_, hf, 12 + 3 * l, l == 0 and s_ < 2))
        t_left = [len(tasks)]

        def fill(n):
            for _ in range(n):
                if tasks:
                    f, g = tasks.pop(0)
                    later.append((g, f()))
                if len(later) > 1 or (later and not tasks):
                    g, x = later.pop(0)
                    g(*x)

        def fill_to(n):
            while len(tasks) > n:
                fill(1)
            while later:
                g, x = later.pop(0)
                g(*x)
            return dve.last()

        def mc(base, s, j):
            return mods[:, base + s, j:j + 1]

        def scale_shift(dst, src, g, bcol, *toks):
            for j in range(8):
                t = ts(dve, dst[:, j, :], src[:, j, :], g(j), bcol(j), ALU.mult, ALU.add, *toks)
            return t

        rs_t = sb("rs_t", [128, 2, 512])
        comb = sb("comb", [128, 4, 8])

        eps_a = {1e-5: eps5, 1e-6: eps6}
        warm = sb("warm", [1, 1])

        def rsqrt(o, src, scale, eps, toks, *also):
            tl = [afn(o_, s_, ACT.Ln, t_, *also, scale=scale, bias=eps_a[eps]) for o_, s_, t_ in zip(o, src, toks)]
            return tl, [afn(o_, o_, ACT.Exp, t_, scale=-0.5) for o_, t_ in zip(o, tl)]

        def head_norm(x, n, sq, rn, scale, *toks):
            t = []
            for i in range(n // 2):
                t.append(afn(sq[:, 2 * i:2 * i + 2, :], x[:, 2 * i:2 * i + 2, :], ACT.Square, *toks))
            bs = []
            for i in range(n // 2):
                b, free = pr.take()
                bs.append((b, mm(ps[b][:, :], ones, sq[:, 2 * i:2 * i + 2, :], True, True, free, t[i], inc=True)))
            tl, te = rsqrt([rn[:, 2 * i:2 * i + 2, :].rearrange("p a b -> p (a b)") for i in range(n // 2)],
                           [ps[b][:, :] for b, _ in bs], scale, 1e-6, [t1 for _, t1 in bs])
            for (b, _), t1 in zip(bs, tl):
                pr.rel(b, t1)
            return te

        def rstd(src, sq, eps, tok, rs=rs_t[:, 0, 0:256]):
            b, free = pr.take()
            pe.wait(free)
            for i in range(4):
                t = afn(sq[:, 2 * i:2 * i + 2, :], src[:, 2 * i:2 * i + 2, :], ACT.Square, tok[i])
                pe.wait(t)
                for k in (2 * i, 2 * i + 1):
                    t = mm(ps[b][:, 0:256], ones, sq[:, k, :], k == 0, k == 7, inc=(k == 7))
            afn(warm[:, :], ones[0:1, 0:1], ACT.Ln, act.last())
            tl, te = rsqrt([rs], [ps[b][:, 0:256]], 1.0 / D, eps, [t], dve.last())
            pr.rel(b, *tl)
            return te[0]

        def residual(base, gsec, t_y, vi, l, hbase, hsec, alpha=True, between=None):
            u, sq = S(8, 8, 256), S(7, 8, 256)
            meet()
            g0, b0, g1, b1 = (comb[:, i, :] for i in range(4))
            f = ALPHA if alpha else 1.0
            ts(dve, g0, vec[:, vi + l, :], f, None, ALU.mult, None, dve.last())
            ts(dve, b0, vec[:, vi + 2 + l, :], f, None, ALU.mult, None)
            if hbase is not None:
                tt(dve, g1, vec[:, vi + l, :], mods[:, hbase + hsec + 1, :], ALU.mult)
                t = tt(dve, b1, vec[:, vi + 2 + l, :], mods[:, hbase + hsec + 1, :], ALU.mult)
                tt(dve, b1, b1, mods[:, hbase + hsec, :], ALU.add, t)
            b, free = pr.take()
            pe.wait(free)
            for j in range(8):
                t = stt(u[:, j, :], Y(j), mc(base, gsec, j), xT[:, j, :], ALU.mult, ALU.add, t_y)
                t1 = mm(ps[b][:, 0:256], ones, u[:, j, :], j == 0, j == 7, t, inc=(j == 7))
            give_y(t)
            toks = []
            for i in range(4):
                o = u[:, 2 * i:2 * i + 2, :]
                toks.append(stt(o, bc(ps[b][:, 0:256], 2), -1.0 / D, o, ALU.mult, ALU.add, t1))
            pr.rel(b, toks[-1])
            if between is not None:
                between()
            r = rs_t[:, 0, 0:256]
            t = rstd(u, sq, 1e-5, toks)
            for i in range(4):
                o = u[:, 2 * i:2 * i + 2, :]
                t1 = tt(dve, o, o, bc(r, 2), ALU.mult, t)
                for j in (2 * i, 2 * i + 1):
                    t2 = afn(xT[:, j, :], u[:, j, :], ACT.Identity, t1, scale=g0[:, j:j + 1], bias=b0[:, j:j + 1])
                    if hbase is not None:
                        t2 = ts(dve, hT[:, j, :], u[:, j, :], g1[:, j:j + 1], b1[:, j:j + 1], ALU.mult, ALU.add, t1)
                toks[i] = t2
            return toks if hbase is None else t2

        def out_proj(w, src, *ready, between=None, each=None):
            toks = take_y()
            for q in range(4):
                u = rows(w, 2 * q)
                t = down(u, [src[:, 2 * q, :], src[:, 2 * q + 1, :]], q == 0, q == 3, toks, *ready,
                         each[q] if each is not None else None)
                if q == 1 and between is not None:
                    between()
            return t

        rtS = sb("rtS", [128, 2, 66])
        rtG = sb("rtG", [128, 2, 12])
        rt8 = sb("rt8", [128, 2, 8, 8])
        rtm = S(6, 768).rearrange("p (a m e) -> p a m e", a=6, m=2)
        wT = rs_t[0:64, 0, 0:256]
        wov = rtm[:, 5, :, :]
        hid = S(0, 8, 256).rearrange("p (h m) n -> p h m n", m=2)
        hsg = S(1, 2, 256)
        flags = sb("flags", [1, 2], mybir.dt.int32)
        t_sent = pool.do(lambda e: e.memset(rtS[:, :, :], -2e38))
        t_sent = pool.do(lambda e: e.memset(rtG[:, :, :], -2e38), t_sent)

        def route(l, t_h, between):
            b, free = pr.take()
            u = cols(A["moe_router_w"][l], 0, 64)
            pe.wait(free, t_h, u.tok)
            for m in range(2):
                for k in range(8):
                    t = mm(ps[b][:, m * 64:m * 64 + 64], hT[:, k, m * 128:(m + 1) * 128], u.v[:, k, :],
                           k == 0, k == 7, inc=(k == 7))
            wr.rel(u.i, t)
            lg = ps[b][:, 0:128].rearrange("p (m e) -> p m e", m=2)
            sc, sel, gm, wk = rtm[:, 0, :, :], rtm[:, 1, :, :], rtm[:, 2, :, 0:8], rtm[:, 3, :, :]
            t = afn(sc, lg, ACT.Exp, t, scale=-1.0)
            pr.rel(b, t)
            t = ts(dve, sc, sc, 1.0, None, ALU.add, None, t)
            t = dve.do(lambda e: e.reciprocal(sc, sc), t)
            t = tt(dve, sel, sc, bc(rtb[:, l, :], 2), ALU.add, t)
            for m in range(2):
                for g in range(8):
                    t1 = dve.do(lambda e, m=m, g=g: e.max(rt8[:, m, g, :], sel[:, m, g * 8:g * 8 + 8]), t)
            gs = rtG[:, :, 0:8]
            t = tt(dve, gs, rt8[:, :, :, 0], rt8[:, :, :, 1], ALU.add, t1, t_sent)
            for m in range(2):
                t1 = dve.do(lambda e, m=m: e.max(rt8[:, m, 0, :], gs[:, m, :]), t)
            t1 = dve.do(lambda e: e.memset(rt8[:, :, 0, 4:8], -2e38), t1)
            for m in range(2):
                t2 = dve.do(lambda e, m=m: e.match_replace(rtm[:, 4, m, 0:12], rt8[:, m, 0, :], rtG[:, m, :],
                                                           -3e38), t1)
            t = tt(dve, gm, rtm[:, 4, :, 0:8], gs, ALU.not_equal, t2)
            neg = rtm[:, 4, :, 16:24]
            t = ts(dve, neg, gm, 1e30, -1e30, ALU.mult, ALU.add, t)
            s4 = rtS[:, :, 0:64]
            for m in range(2):
                t1 = tt(dve, s4[:, m, :].rearrange("p (g e) -> p g e", e=8),
                        sel[:, m, :].rearrange("p (g e) -> p g e", e=8), inner(gm[:, m, :], 8), ALU.mult, t, t_sent)
            for m in range(2):
                t2 = tt(dve, s4[:, m, :].rearrange("p (g e) -> p g e", e=8),
                        s4[:, m, :].rearrange("p (g e) -> p g e", e=8), inner(neg[:, m, :], 8), ALU.add, t1)
            for m in range(2):
                t = dve.do(lambda e, m=m: e.max(rt8[:, m, 0, :], s4[:, m, :]), t2)
            t = dve.do(lambda e: e.memset(rt8[:, :, 0, 6:8], -2e38), t)
            wk66 = rtm[:, 3:6, :, :].rearrange("p a m e -> p (a m e)")
            for m in range(2):
                t1 = dve.do(lambda e, m=m: e.match_replace(wk66[:, 80 * m:80 * m + 66], rt8[:, m, 0, :],
                                                           rtS[:, m, :], -3e38), t)
            msk = S(6, 2048)[:, 1792:1920].rearrange("p (m e) -> p m e", m=2)
            rk = S(6, 2048)[:, 1920:2048].rearrange("p (m e) -> p m e", m=2)
            for m in range(2):
                t2 = tt(dve, msk[:, m, :], wk66[:, 80 * m:80 * m + 64], s4[:, m, :], ALU.not_equal, t1)
            t_m = t2
            t = tt(dve, sel, msk, sc, ALU.mult, t2)
            t = dve.do(lambda e: e.tensor_reduce(rt8[:, :, 1, 0:1], sel, AX.X, ALU.add), t)
            t = ts(dve, rt8[:, :, 1, 0:1], rt8[:, :, 1, 0:1], 1e-20, None, ALU.add, None, t)
            t = dve.do(lambda e: e.reciprocal(rt8[:, :, 1, 1:2], rt8[:, :, 1, 0:1]), t)
            for m in range(2):
                t1 = ts(dve, sel[:, m, :], sel[:, m, :], rt8[:, m, 1, 1:2], 2.5, ALU.mult, ALU.mult, t)
            t_w = t1
            between()
            b, free = pr.take()
            pe.wait(free, t_m)
            mm(ps[b][:, 0:64], C("before"), msk[:, 0, :], True, True)
            mm(ps[b][:, 64:128], ones, msk[:, 0, :], True, False)
            t = mm(ps[b][:, 64:128], C("before"), msk[:, 1, :], False, True, inc=True)
            t = tt(dve, rk, ps[b][:, 0:128].rearrange("p (m e) -> p m e", m=2), msk, ALU.mult, t)
            pr.rel(b, t)
            t_r = stt(rk, msk, -1.0, rk, ALU.add, ALU.add, t)
            t = dve.do(lambda e: e.tensor_reduce(rt8[:, 0, 2, 0:1], rk, AX.XY, ALU.max), t_r)
            b, free = pr.take()
            t = tr(ps[b][0:1, 0:128], rt8[:, 0, 2, 0:1], free, t, inc=True)
            t = dve.do(lambda e: e.tensor_reduce(rt8[0:1, 0, 2, 1:2], ps[b][0:1, 0:128], AX.X, ALU.max), t)
            pr.rel(b, t)
            t_f = ts(dve, flags[0:1, l:l + 1], rt8[0:1, 0, 2, 1:2], CAP - 0.5, None, ALU.is_ge, None, t)
            t = ts(dve, wov, rk, CAP - 0.5, None, ALU.is_ge, None, t_r)
            tt(dve, wov, wov, sel, ALU.mult, t, t_w)
            return sel, rk, t_w, t_r, t_f

        s_sec = [[sem(f"s_sec{l}{n}") for n in range(4)] for l in range(2)]
        w_sec = [[sem(f"s_sw{l}{n}") for n in range(NS)] for l in range(2)]

        def moe_rest(l):
            toks = [q.last() for q in (pe, act, dve, pool)]
            flag = flags[0:1, l:l + 1]
            kept = (dict(pr.free), list(pr.ids), pr.at, dict(wr.free), list(wr.ids), wr.at)
            for q, x in zip((pe, act, dve, sp), s_sec[l]):
                q.enter(x)
                q.wait(toks)
            wsec.append(w_sec[l])
            wr.ids, wr.at = list(range(NS)), 0
            for i in range(NS):
                wr.free[i] = []
            for i in range(4):
                pr.free[i] = []
            b = 0
            for m in range(2):
                t = tr(ps[b][0:64, m * 128:(m + 1) * 128], wov[:, m, :], inc=(m == 1))
            t_w = copy(wT[:, :], ps[b][0:64, 0:256], t)
            pr.rel(b, t_w)
            gu = Ring((0, 1, 2))
            gu.free[0] = [t_w]
            ws = Ring((0, 1))
            wsb = S(1, 8, 256)[:, 4:6, :]
            hr = Ring(range(4))
            sg = Ring(range(2))
            fr3 = []
            pend = None
            for e in range(NE + 1):
                if e < NE:
                    ug, uu = cols(A["moe_w_gate"][l, e], 0, 256), cols(A["moe_w_up"][l, e], 0, 256)
                    ud = rows(A["moe_w_down"][l, e], 0)
                    t_b = mm(ps[3][:, 0:256], ident[0:64, e:e + 1].broadcast_to([64, 128]), wT[:, :], True, True,
                             fr3, t_w, inc=True)
                    wi, free = ws.take()
                    wv = wsb[:, wi, :]
                    t_b = afn(wv, ps[3][:, 0:256], ACT.Copy, t_b, free)
                    fr3 = [t_b]
                    h, hfree = hr.take()
                    for m in range(2):
                        b, free = gu.take()
                        pe.wait(ug.tok, uu.tok, free)
                        for half, u in ((0, ug), (1, uu)):
                            for k in range(8):
                                t = mm(ps[b][:, half * 256:half * 256 + 256], u.v[:, k, m * 128:m * 128 + 128],
                                       hT[:, k, :], k == 0, k == 7, inc=(k == 7))
                            if m == 1:
                                wr.rel(u.i, t)
                        s, sfree = sg.take()
                        t1 = afn(hsg[:, s, :], ps[b][:, 0:256], ACT.Silu, t, sfree)
                        t2 = tt(dve, hsg[:, s, :], ps[b][:, 256:512], hsg[:, s, :], ALU.mult, t1)
                        gu.rel(b, t2)
                        t2 = tt(dve, hid[:, h, m, :], wv, hsg[:, s, :], ALU.mult, t2, t_b, hfree)
                        sg.rel(s, t2)
                    ws.rel(wi, t2)
                if pend is not None:
                    pd, ph, pt = pend
                    t = down(pd, [hid[:, ph, 0, :], hid[:, ph, 1, :]], False, False, pt)
                    hr.rel(ph, t)
                pend = (ud, h, t2)
            ends = [q.last() for q in (pe, act, dve)]
            for q in (pe, act, dve, sp):
                q.wait(ends)
            wsec.pop()
            for q in (pe, act, dve, sp):
                q.leave(flag)
            pr.free, pr.ids, pr.at, wr.free, wr.ids, wr.at = kept

        def moe(l, t_h):
            start = meet()
            us = t_ht = t_s = None
            sh = S(6, 2048)[:, 768:1792].rearrange("p (a n) -> p a n", a=4)
            htok = S(0, 2, 1024)

            def between():
                nonlocal us, t_ht, t_s
                for m in range(2):
                    for k2 in range(2):
                        b, free = pr.take()
                        pe.wait(free)
                        for k in range(4):
                            t = tr(ps[b][:, k * 128:k * 128 + 128], hT[:, 4 * k2 + k, m * 128:m * 128 + 128],
                                   inc=(k == 3))
                        t_ht = afn(htok[:, m, k2 * 512:k2 * 512 + 512], ps[b][:, :], ACT.Copy, t)
                        pr.rel(b, t_ht)
                ug, uu = cols(A["sh_w_gate"][l], 0, 256), cols(A["sh_w_up"][l], 0, 256)
                us = rows(A["sh_w_down"][l], 0)
                for m in range(2):
                    b, free = pr.take()
                    pe.wait(ug.tok, uu.tok, free)
                    for half, u in ((0, ug), (1, uu)):
                        for k in range(8):
                            t = mm(ps[b][:, half * 256:half * 256 + 256], u.v[:, k, m * 128:m * 128 + 128],
                                   hT[:, k, :], k == 0, k == 7, inc=(k == 7))
                        if m == 1:
                            wr.rel(u.i, t)
                    t1 = afn(sh[:, m, :], ps[b][:, 0:256], ACT.Silu, t)
                    t_s = tt(dve, sh[:, 2 + m, :], ps[b][:, 256:512], sh[:, m, :], ALU.mult, t1)
                    pr.rel(b, t_s)

            sel, rk, t_w, t_r, t_f = route(l, t_h, between)
            ylast = take_y()
            t = down(us, [sh[:, 2, :], sh[:, 3, :]], True, False, t_s, ylast)
            wr.ids, wr.at = [wr.ids[(wr.at + i) % NS] for i in range(NS)] + [NS, NS + 1, NS + 2], 0
            wr.at = 0
            for i in range(3):
                wr.rel(NS + i, *start)

            xg = [S(1, 8, 256), S(2, 8, 256)]
            pm = S(3, 4, 512)
            P = [pm[:, i, :].rearrange("p (m n) -> p m n", m=2) for i in range(2)]
            PW = [pm[:, 2 + i, :].rearrange("p (m n) -> p m n", m=2) for i in range(2)]
            ys = S(4, 2, 1024)
            tp = S(5, 4, 512)[:, 0:2, :]
            hh = S(5, 8, 256)[:, 4:6, :]
            sg = S(5, 8, 256)[:, 6:8, :]
            iota = C("iota")
            NG, NP = NE // 4, NE // 2
            t_P, t_PW, t_X = {}, {}, {}
            r_P, r_PW = {}, {}
            t_T, t_S, t_A = {}, {}, {}

            def places(g):
                i = g % 2
                dve.wait(r_P.get(g - 2), r_PW.get(g - 2), t_w, t_r)
                for m in range(2):
                    for j in range(4):
                        e = 4 * g + j
                        t_P[g] = ts(dve, P[i][:, m, j * 64:j * 64 + 64], iota, rk[:, m, e:e + 1],
                                    None, ALU.is_equal, None)
                for m in range(2):
                    for j in range(4):
                        e = 4 * g + j
                        t_PW[g] = ts(dve, PW[i][:, m, j * 64:j * 64 + 64], iota, rk[:, m, e:e + 1],
                                     sel[:, m, e:e + 1], ALU.is_equal, ALU.mult)

            def gather(g, half):
                i = g % 2
                pe.wait(t_P[g], t_ht)
                for k2 in range(2):
                    b, free = pr.take()
                    pe.wait(free)
                    for kk in range(2):
                        k = 4 * half + 2 * k2 + kk
                        for m in range(2):
                            t = mm(ps[b][:, kk * 256:kk * 256 + 256], htok[:, m, k * 128:k * 128 + 128],
                                   P[i][:, m, :], m == 0, m == 1, inc=(kk == 1 and m == 1))
                    k = 4 * half + 2 * k2
                    o = xg[i][:, k:k + 2, :].rearrange("p a b -> p (a b)")
                    t1 = copy(o, ps[b][:, :], t, t_A.get(2 * g - 3))
                    pr.rel(b, t1)
                t_X[(g, half)] = t1
                if half == 1:
                    r_P[g] = t

            def scatter(q):
                pe.wait(t_S[q])
                for j in range(8):
                    t = mm(Y(j), ys[:, q % 2, j::8], tp[:, q % 2, 256:512], False, q == NP - 1 and j % 2 == 1,
                           inc=(j == 7), skip=True)
                return t

            places(0)
            gather(0, 0)
            gather(0, 1)
            done = {}
            for q in range(NP):
                g, o = q // 2, (q % 2) * 128
                if q % 2 == 0 and g + 1 < NG:
                    places(g + 1)
                es = (2 * q, 2 * q + 1)
                us = {}
                for k0 in (0, 4):
                    for e in es:
                        us[(e, k0)] = pair_unit(A["moe_w_gate"][l, e], A["moe_w_up"][l, e], k0)
                ud = [rows(A["moe_w_down"][l, e], 0) for e in es]
                b, free = pr.take()
                pe.wait(free, t_X[(g, 0)], t_X[(g, 1)])
                for k in range(8):
                    k0 = k // 4 * 4
                    for i, e in enumerate(es):
                        u = us[(e, k0)]
                        if k == k0:
                            pe.wait(u.tok)
                        fin = k % 4 == 3
                        t = mm(ps[b][64 * i:64 * i + 64, :], xg[g % 2][:, k, o + 64 * i:o + 64 * i + 64],
                               u.v[:, k - k0, :], k == 0, k == 7, inc=fin, skip=True)
                        if fin:
                            wr.rel(u.i, t)
                t_A[q] = t
                t1 = afn(sg[:, q % 2, :], ps[b][:, 0:256], ACT.Silu, t)
                t1 = tt(dve, hh[:, q % 2, :], ps[b][:, 256:512], sg[:, q % 2, :], ALU.mult, t1)
                pr.rel(b, t1)
                if q:
                    done[q - 1] = scatter(q - 1)
                b, free = pr.take()
                pe.wait(free, t1, t_PW[g])
                for i in range(2):
                    tr(ps[b][:, i * 128:i * 128 + 128], hh[:, q % 2, i * 128:i * 128 + 128])
                for m in range(2):
                    t = tr(ps[b][:, 256 + m * 128:384 + m * 128], PW[g % 2][:, m, o:o + 128], inc=(m == 1))
                if q % 2 == 1:
                    r_PW[g] = t
                t_t = copy(tp[:, q % 2, :], ps[b][:, :], t, done.get(q - 2))
                pr.rel(b, t_t)
                if g + 1 < NG:
                    gather(g + 1, q % 2)
                for half in range(2):
                    b, free = pr.take()
                    pe.wait(free, t_t)
                    for kk in range(2):
                        for i in range(2):
                            pe.wait(ud[i].tok)
                            fin = kk == 1
                            t = mm(ps[b][64 * i:64 * i + 64, :],
                                   tp[:, q % 2, kk * 128 + 64 * i:kk * 128 + 64 * i + 64],
                                   ud[i].v[:, kk, half * 512:half * 512 + 512], kk == 0, kk == 1, inc=fin,
                                   skip=True)
                            if fin and half == 1:
                                wr.rel(ud[i].i, t)
                    t_S[q] = afn(ys[:, q % 2, half * 512:half * 512 + 512], ps[b][:, :], ACT.Copy, t,
                                 done.get(q - 2))
                    pr.rel(b, t_S[q])
            t = scatter(NP - 1)
            wr.ids, wr.at = list(range(NS)), 0
            sp.wait(t_f)
            moe_rest(l)
            return t

        scr = nc.dram_tensor("scr_tab", [4, 512], F32, kind="Internal")
        s_tab = sem("s_tab")
        stat = sb("stat", [128, 4, 16])

        def even_mixer(t_h):
            w = A["ev_w_in"][0]
            qk = S(0, 8, 256)
            vt = S(1, 2, 512)
            gv = S(1, 4, 512)[:, 2:4, :]
            gqk = S(2, 8, 256)
            gg = S(3, 8, 256)
            glr = gqk[:, 4, :]
            gT = S(3, 8, 256)[:, 4:6, :]
            mix = S(4, 8, 256)
            P = S(5, 8, 256)
            PT = S(6, 8, 256)

            def to(dst, scale=1.0, a=True, n=512):
                def ev(p, t):
                    if a:
                        return afn(dst, p[:, 0:n], ACT.Copy, t, scale=scale)
                    return ts(dve, dst, p[:, 0:n], scale, None, ALU.mult, None, t)
                return ev

            def flat(v):
                return v.rearrange("p a b -> p (a b)")

            b, free = pr.take()
            t = mm(ps[b][0:4, :], rpe33[:, :], C("hot")[0:33, :], True, True, free, t_sm, t_in, inc=True)
            t = copy(rs_t[0:4, 0, :], ps[b][0:4, :], t)
            pr.rel(b, t)
            t = dma(pool, scr.ap(), rs_t[0:4, 0, :], s_tab, t)
            hank = S(7, 2, 4, 256)
            for qt in range(2):
                src = bass.AP(scr, 128 * (1 - qt), [[1, 128], [512, 4], [1, 256]])
                t_hk = dma(pool, hank[:, qt, :, :], src, s_tab, t)

            for i in range(2):
                proj_f(w, 256 * i, 256, hT, to(flat(qk[:, 2 * i:2 * i + 2, :]), 128 ** -0.5, i % 2 == 0), t_h)
            for i in range(2):
                proj_f(w, 512 + 256 * i, 256, hT, to(flat(qk[:, 4 + 2 * i:6 + 2 * i, :]), 1.0, i % 2 == 0), t_h)

            def to_t(dst, i):
                def ev(p, t):
                    return copy(dst[:, :, 256 * i:256 * i + 256], p[:, :].rearrange("p (m n) -> p m n", m=2), t)
                return ev

            for i in range(2):
                proj_t(w, 1024 + 256 * i, 256, hT, to_t(vt, i), t_h)
            proj_f(w, 1536, 256, hT, to(flat(gqk[:, 0:2, :]), 0.125), t_h)
            proj_f(w, 1792, 256, hT, to(flat(gqk[:, 2:4, :]), 1.0, False), t_h)
            for i in range(2):
                proj_t(w, 2048 + 256 * i, 256, hT, to_t(gv, i), t_h)
            for i in range(2):
                proj_f(w, 2560 + 256 * i, 256, hT, to(flat(gg[:, 2 * i:2 * i + 2, :]), 1.0, i % 2 == 0), t_h)
            proj_f(w, 3072, 16, hT, lambda p, t: copy(glr[0:16, :], p[0:16, 0:256], t), t_h)
            meet()

            for q in range(8):
                h, qt = q // 2, q % 2
                b, free = pr.take()
                mm(ps[b][:, 0:256], qk[:, h, qt * 128:qt * 128 + 128], qk[:, 4 + h, :], True, False, free)
                t = mm(ps[b][:, 0:256], flip, hank[:, qt, h, :], False, True, t_hk, inc=True)
                t = dve.do(lambda e, b=b, q=q: e.tensor_reduce(stat[:, 0, q:q + 1], ps[b][:, 0:256], AX.X,
                                                               ALU.max, negate=True), t)
                t = afn(P[:, q, :], ps[b][:, 0:256], ACT.Exp, t, bias=stat[:, 0, q:q + 1],
                        acc=stat[:, 1, q:q + 1])
                pr.rel(b, t)
                t = dve.do(lambda e, q=q: e.reciprocal(stat[:, 2, q:q + 1], stat[:, 1, q:q + 1]), t)
                ts(dve, P[:, q, :], P[:, q, :], stat[:, 2, q:q + 1], None, ALU.mult, None, t)
            for h in range(4):
                b, free = pr.take()
                pe.wait(free, dve.last())
                for kt in range(2):
                    for qt in range(2):
                        t = tr(ps[b][:, kt * 256 + qt * 128:kt * 256 + qt * 128 + 128],
                               P[:, 2 * h + qt, kt * 128:kt * 128 + 128], inc=(kt == 1 and qt == 1))
                t = copy(flat(PT[:, 2 * h:2 * h + 2, :]), ps[b][:, :], t)
                pr.rel(b, t)
            for h in range(4):
                b, free = pr.take()
                pe.wait(free, dve.last())
                for kt in range(2):
                    t = mm(ps[b][:, 0:256], vt[:, kt, h * 128:h * 128 + 128], PT[:, 2 * h + kt, :], kt == 0,
                           kt == 1, inc=(kt == 1))
                t = afn(mix[:, h, :], ps[b][:, 0:256], ACT.Copy, t)
                pr.rel(b, t)

            b, free = pr.take()
            for j in range(2):
                t = mm(ps[b][:, j * 256:j * 256 + 256], gkw2[:, j * 128:j * 128 + 128], glr[0:16, :], True, True,
                       free, inc=(j == 1))
            z, ez = S(8, 8, 256)[:, 0:2, :], S(8, 8, 256)[:, 2:4, :]
            bb, e2 = S(8, 8, 256)[:, 4:6, :], S(8, 8, 256)[:, 6:8, :]
            for j in range(2):
                t1 = ts(dve, z[:, j, :], ps[b][:, j * 256:j * 256 + 256], cv1("gkb", j), None, ALU.add, None, t,
                        t_cols)
            pr.rel(b, t1)
            t = afn(ez, z, ACT.Abs, t1)
            t = afn(ez, ez, ACT.Exp, t, scale=-1.0)
            t = afn(ez, ez, ACT.Ln, t, bias=one_c)
            t = ts(dve, z, z, 0.0, None, ALU.min, None, t)
            t = tt(dve, z, z, ez, ALU.subtract, t)
            t = ts(dve, z, z, 1.0 / 16, None, ALU.mult, None, t)
            fz, fb = flat(z), flat(bb)
            t = dve.do(lambda e: e.tensor_tensor_scan(fb, C("rset"), fz, 0.0, ALU.mult, ALU.add), t)
            b4 = bb.rearrange("p j (c i) -> p (j c) i", i=64)
            e4 = e2.rearrange("p j (c i) -> p (j c) i", i=64)
            t_e = tt(dve, e4, b4[:, :, 63:64].broadcast_to([128, 8, 64]), b4, ALU.subtract, t)
            dl = stat[:, 3, 0:8]
            t = afn(dl, b4[:, :, 63], ACT.Exp, t_e)
            t = afn(z, bb, ACT.Exp, t, t_e)
            t = afn(ez, bb, ACT.Exp, t, scale=-1.0)
            t = afn(e2, e2, ACT.Exp, t, t_e)
            qe, ke, kn = S(7, 8, 256)[:, 0:2, :], S(7, 8, 256)[:, 2:4, :], S(7, 8, 256)[:, 4:6, :]
            knt = S(7, 8, 256)[:, 6:8, :]
            meet()
            tt(dve, qe, gqk[:, 0:2, :], z, ALU.mult)
            tt(dve, ke, gqk[:, 2:4, :], ez, ALU.mult)
            t = tt(dve, kn, gqk[:, 2:4, :], e2, ALU.mult)
            b, free = pr.take()
            pe.wait(free, t)
            for m in range(2):
                for j in range(2):
                    t = tr(ps[b][:, m * 256 + j * 128:m * 256 + j * 128 + 128], kn[:, j, m * 128:m * 128 + 128],
                           inc=(m == 1 and j == 1))
            t = copy(flat(knt), ps[b][:, :], t)
            pr.rel(b, t)
            aT = S(6, 8, 128)
            for m in range(2):
                b, free = pr.take()
                pe.wait(free, dve.last())
                for h in (0, 2, 1, 3):
                    po, j = (h % 2) * 64, h // 2
                    t = mm(ps[b][:, h * 128:h * 128 + 128], ke[po:po + 64, j, m * 128:m * 128 + 128],
                           qe[po:po + 64, j, m * 128:m * 128 + 128], True, True, t if h == 1 else None,
                           inc=(h >= 2))
                meet()
                t = tt(dve, aT[:, 4 * m:4 * m + 4, :], ps[b][:, :].rearrange("p (h i) -> p h i", h=4),
                       bc(C("incl"), 4), ALU.mult, t)
                pr.rel(b, t)
            st = S(5, 8, 128)[:, 0:2, :]
            oT = S(5, 8, 256)[:, 4:8, :]
            meet()
            t_st = t_i = None
            for c in range(4):
                m, off = c // 2, (c % 2) * 64
                bo, free = pr.take()
                pe.wait(free)
                for h in range(4):
                    t_i = mm(ps[bo][:, h * 64:h * 64 + 64], gv[off:off + 64, m, h * 128:h * 128 + 128],
                             aT[off:off + 64, 4 * m + h, off:off + 64], h == 0, c == 0, inc=(h == 3), skip=True)
                if c < 3:
                    bu, free = pr.take()
                    pe.wait(free)
                    for h in range(4):
                        po, j = (h % 2) * 64, h // 2
                        tu = mm(ps[bu][po:po + 64, j * 128:j * 128 + 128],
                                knt[off:off + 64, m, h * 64:h * 64 + 64], gv[off:off + 64, m, h * 128:h * 128 + 128],
                                True, True, inc=(h == 3))
                if c:
                    pe.wait(t_st)
                    for h in (0, 2, 1, 3):
                        po, j = (h % 2) * 64, h // 2
                        t_i = mm(ps[bo][:, h * 64:h * 64 + 64], st[po:po + 64, j, :],
                                 qe[po:po + 64, j, c * 64:c * 64 + 64], False, True, t_i if h < 2 else None,
                                 inc=(h >= 2), skip=True)
                t_o = afn(oT[:, :, c * 64:c * 64 + 64], ps[bo][:, 0:256].rearrange("p (h i) -> p h i", h=4),
                          ACT.Copy, t_i)
                pr.rel(bo, t_o)
                if c < 3:
                    for j in range(2):
                        u = ps[bu][:, j * 128:j * 128 + 128]
                        if c == 0:
                            t_st = copy(st[:, j, :], u, tu)
                        else:
                            t_st = stt(st[:, j, :], st[:, j, :], dl[:, j * 4 + c:j * 4 + c + 1], u, ALU.mult,
                                       ALU.add, tu, t_i)
                    pr.rel(bu, t_st)
            t = gated_norm(oT, gg, mix[:, 4:8, :], 4, cv1("evn"), t_o)
            fill(fill_rate[0])
            return out_proj(A["ev_w_out"][0], mix, each=[t_o, t_o] + t)

        def gated_norm(oT, gate, dst, n, wcol, tok):
            sq = S(8, 8, 256)
            t2 = head_norm(oT, n, sq, sq, 1.0 / 128, tok)
            ts_ = [afn(gate[:, i:i + 2, :], gate[:, i:i + 2, :], ACT.Silu, tok) for i in range(0, n, 2)]
            out_ = []
            for i in range(0, n, 2):
                t = stt(dst[:, i:i + 2, :], oT[:, i:i + 2, :], wcol, sq[:, i:i + 2, :], ALU.mult, ALU.mult,
                        t2[i // 2], t_cols)
                out_.append(tt(dve, dst[:, i:i + 2, :], dst[:, i:i + 2, :], gate[:, i:i + 2, :], ALU.mult, t,
                               ts_[i // 2]))
            return out_

        raw = misc[:, 0:3 * 518].rearrange("p (r m n) -> p r m n", r=3, m=2)
        gds = sb("gds", [128, 16, 16])
        t_raw = pool.do(lambda e: e.memset(raw[:, :, :, 0:3], 0.0))

        def delta_mixer(t_h):
            w = A["od_w_in"][0]
            qT, kT, vT, gate = S(0, 8, 256), S(1, 8, 256), S(2, 8, 256), S(3, 8, 256)
            rr = Ring(range(3))

            def flat(v):
                return v.rearrange("p a b -> p (a b)")

            ba = gds[:, 0:4, :].rearrange("p a b -> p (a b)")[:, 0:32].rearrange("p (m n) -> p m n", m=2)
            proj_t(w, 4096, 16, hT, lambda p, t: copy(ba, p[:, :].rearrange("p (m n) -> p m n", m=2)[:, :, 0:16], t),
                   t_h)
            be = gds[:, 4, :].rearrange("p (m n) -> p m n", m=2)
            gg = gds[:, 5, :].rearrange("p (m n) -> p m n", m=2)
            tz = gds[:, 6, :].rearrange("p (m n) -> p m n", m=2)
            ea = gds[:, 7, 0:8]
            t = afn(be, ba[:, :, 0:8], ACT.Exp, dve.last(), scale=-1.0)
            t = ts(dve, be, be, 1.0, None, ALU.add, None, t)
            t = dve.do(lambda e: e.reciprocal(be, be), t)
            t = tt(dve, gg, ba[:, :, 8:16], bc(adt[:, 1, :], 2), ALU.add, t)
            t = afn(tz, gg, ACT.Abs, t)
            t = afn(tz, tz, ACT.Exp, t, scale=-1.0)
            s1 = gds[:, 12, :].rearrange("p (m n) -> p m n", m=2)
            s2 = gds[:, 13, :].rearrange("p (m n) -> p m n", m=2)
            qq = gds[:, 14, :].rearrange("p (m n) -> p m n", m=2)
            t = ts(dve, s1, tz, 2.0, None, ALU.add, None, t)
            t = dve.do(lambda e: e.reciprocal(s1, s1), t)
            t = tt(dve, s1, s1, tz, ALU.mult, t)
            t = tt(dve, s2, s1, s1, ALU.mult, t)
            t = ts(dve, qq, s2, 1.0 / 15, None, ALU.mult, None, t)
            for n in (13, 11, 9, 7, 5, 3):
                t = stt(qq, qq, 1.0 / n, s2, ALU.add, ALU.mult, t)
            t = stt(qq, qq, 1.0, s1, ALU.add, ALU.mult, t)
            t = ts(dve, tz, qq, 2.0, None, ALU.mult, None, t)
            t = afn(ea, adt[:, 0, :], ACT.Exp, t)
            t = ts(dve, gg, gg, 0.0, None, ALU.max, None, t)
            t = tt(dve, gg, gg, tz, ALU.add, t)
            t = tt(dve, gg, gg, bc(ea, 2), ALU.mult, t)
            t_g = ts(dve, gg, gg, -1.0, None, ALU.mult, None, t)
            b, free = pr.take()
            pe.wait(free, t_g)
            for m in range(2):
                mm(ps[b][:, m * 8:m * 8 + 8], C("incl"), gg[:, m, :], True, True)
                mm(ps[b][:, 16 + m * 8:24 + m * 8], C("same"), gg[:, m, :], True, True)
            t = None
            for c in (0, 2, 1, 3):
                po = (c % 2) * 64
                t = mm(ps[b][:, 32 + c * 8:40 + c * 8], ones[po:po + 64, :], gg[po:po + 64, c // 2, :], True, True,
                       t if c == 1 else None, inc=(c >= 2))
            egc = gds[:, 8, :]
            een = gds[:, 9, :]
            DL = gds[:, 10:12, :].rearrange("p a b -> p (a b)")
            t1 = copy(egc, ps[b][:, 0:16], t)
            t1 = tt(dve, een, ps[b][:, 16:32], egc, ALU.subtract, t1)
            t1 = afn(egc, egc, ACT.Exp, t1)
            t1 = afn(een, een, ACT.Exp, t1)
            t1 = afn(DL, ps[b][:, 32:64], ACT.Exp, t1)
            pr.rel(b, t1)

            def conv(dst, j0):
                def ev(p, t):
                    r, free = rr.take()
                    t = afn(raw[:, r, :, 3:259], p[:, :].rearrange("p (m n) -> p m n", m=2), ACT.Copy, t, t_raw,
                            free)
                    tl = t
                    for m in range(2):
                        x = raw[:, r, m, :]
                        j = j0 + m
                        o = dst[:, m, :]
                        t1 = ts(dve, o, x[:, 0:256], colv[:, 0, j:j + 1], None, ALU.mult, None, t, t_cols)
                        for k in range(1, 4):
                            t1 = stt(o, x[:, k:k + 256], colv[:, 0, k * 24 + j:k * 24 + j + 1], o, ALU.mult,
                                     ALU.add, t1)
                    rr.rel(r, t1)
                    afn(dst, dst, ACT.Silu, t1)
                    return tl
                return ev

            for s, dst in ((0, qT), (1, kT), (2, vT)):
                for i in range(4):
                    proj_f(w, s * 1024 + 256 * i, 256, hT, conv(dst[:, 2 * i:2 * i + 2, :], s * 8 + 2 * i), t_h)
            for i in range(4):
                g = gate[:, 2 * i:2 * i + 2, :]
                proj_f(w, 3072 + 256 * i, 256, hT,
                       lambda p, t, g=g: afn(g, p[:, :].rearrange("p (m n) -> p m n", m=2), ACT.Copy, t), t_h)
            meet()
            sq, rn = S(4, 8, 256), S(5, 8, 256)
            for x, scale in ((qT, 128 ** -0.5), (kT, 1.0)):
                t2 = head_norm(x, 8, sq, rn, 1.0, dve.last(), pe.last())
                t = stt(x, x, scale, rn, ALU.mult, ALU.mult, t2)
            meet()
            kg, ke, vt = S(4, 16, 128), S(5, 16, 128), S(6, 16, 128)
            for i in range(4):
                b, free = pr.take()
                pe.wait(free)
                for j in range(4):
                    h, m = 2 * i + j // 2, j % 2
                    t = tr(ps[b][:, j * 128:j * 128 + 128], kT[:, h, m * 128:m * 128 + 128], inc=(j == 3))
                t = afn(flat(ke[:, 4 * i:4 * i + 4, :]), ps[b][:, :], ACT.Copy, t)
                pr.rel(b, t)
                for j in range(4):
                    h, m = 2 * i + j // 2, j % 2
                    g = 4 * i + j
                    t1 = ts(dve, kg[:, g, :], ke[:, g, :], egc[:, m * 8 + h:m * 8 + h + 1], None, ALU.mult, None,
                            t)
                    ts(dve, ke[:, g, :], ke[:, g, :], een[:, m * 8 + h:m * 8 + h + 1], None, ALU.mult, None, t1)
                b, free = pr.take()
                pe.wait(free)
                for j in range(4):
                    h, m = 2 * i + j // 2, j % 2
                    t = tr(ps[b][:, j * 128:j * 128 + 128], vT[:, h, m * 128:m * 128 + 128], inc=(j == 3))
                t = afn(flat(vt[:, 4 * i:4 * i + 4, :]), ps[b][:, :], ACT.Copy, t)
                pr.rel(b, t)
            meet()
            GM, DT = S(8, 4, 4, 128), S(2, 16, 128)
            for i in range(4):
                for j in range(4):
                    h, m = 2 * i + j // 2, j % 2
                    t = ts(dve, GM[:, i, j, :], C("after"), gg[:, m, h:h + 1], None, ALU.mult, None)
                b, free = pr.take()
                pe.wait(free, t)
                for j in range(4):
                    t = mm(ps[b][:, j * 128:j * 128 + 128], GM[:, i, j, :], C("incl"), True, True, inc=(j == 3))
                d4 = DT[:, 4 * i:4 * i + 4, :]
                t = afn(flat(d4), ps[b][:, :], ACT.Exp, t)
                pr.rel(b, t)
                tt(dve, d4, d4, bc(C("incl"), 4), ALU.mult, t)
            AT, QK = S(7, 16, 128), S(8, 16, 128)
            meet()
            for i in range(4):
                b, free = pr.take()
                b2, free2 = pr.take()
                pe.wait(free, free2)
                for j in range(4):
                    h, m = 2 * i + j // 2, j % 2
                    x = kT[:, h, m * 128:m * 128 + 128]
                    mm(ps[b][:, j * 128:j * 128 + 128], x, x, True, True)
                    t = mm(ps[b2][:, j * 128:j * 128 + 128], x, qT[:, h, m * 128:m * 128 + 128], True, True,
                           inc=(j == 3))
                for j in range(4):
                    h, m = 2 * i + j // 2, j % 2
                    g = 4 * i + j
                    t1 = stt(AT[:, g, :], ps[b][:, j * 128:j * 128 + 128], be[:, m, h:h + 1], DT[:, g, :],
                             ALU.mult, ALU.mult, t)
                t2 = tt(dve, flat(QK[:, 4 * i:4 * i + 4, :]), ps[b2][:, :], flat(DT[:, 4 * i:4 * i + 4, :]),
                        ALU.mult, t)
                pr.rel(b, t1)
                pr.rel(b2, t2)
            meet()
            for i in range(4):
                b, free = pr.take()
                pe.wait(free)
                for j in range(4):
                    h, m = 2 * i + j // 2, j % 2
                    t = mm(ps[b][:, j * 128:j * 128 + 128], gg[:, m, h:h + 1].broadcast_to([128, 128]), C("incl"),
                           True, True, inc=(j == 3))
                r = rs_t[:, i % 2, :]
                t = afn(r, ps[b][:, :], ACT.Exp, t, dve.last())
                pr.rel(b, t)
                x = flat(qT[:, 2 * i:2 * i + 2, :])
                t = tt(dve, x, x, r, ALU.mult, t)
            TM, TTm, PM = S(1, 16, 128), S(2, 16, 128), wP
            meet()
            for lv in range(6):
                M = C("level")[:, lv * 128:(lv + 1) * 128]
                tp = []
                for i in range(4):
                    b, free = pr.take()
                    pe.wait(free)
                    for j in range(4):
                        g = 4 * i + j
                        t = mm(ps[b][:, j * 128:j * 128 + 128], AT[:, g, :], ident if lv == 0 else TM[:, g, :],
                               True, True, inc=(j == 3))
                    t = tt(dve, PM[:, 4 * i:4 * i + 4, :], ps[b][:, :].rearrange("p (a b) -> p a b", a=4),
                           bc(M, 4), ALU.mult, t)
                    pr.rel(b, t)
                    tp.append(t)
                for i in range(4):
                    b, free = pr.take()
                    b2, free2 = pr.take()
                    pe.wait(free, free2, tp[i])
                    for j in range(4):
                        g = 4 * i + j
                        mm(ps[b][:, j * 128:j * 128 + 128], ident if lv == 0 else TTm[:, g, :], PM[:, g, :], True,
                           True)
                        t = mm(ps[b2][:, j * 128:j * 128 + 128], PM[:, g, :], ident if lv == 0 else TTm[:, g, :],
                               True, True, inc=(j == 3))
                    for bb, X in ((b, TM), (b2, TTm)):
                        o = X[:, 4 * i:4 * i + 4, :]
                        old = bc(ident, 4) if lv == 0 else o
                        t1 = tt(dve, o, old, ps[bb][:, :].rearrange("p (a b) -> p a b", a=4), ALU.subtract, t)
                        pr.rel(bb, t1)
                pe.wait(dve.last())
            KC = S(7, 16, 128)
            meet()
            for i in range(4):
                b, free = pr.take()
                pe.wait(free)
                for j in range(4):
                    g = 4 * i + j
                    t = mm(ps[b][:, j * 128:j * 128 + 128], kg[:, g, :], TTm[:, g, :], True, True, inc=(j == 3))
                t = afn(flat(KC[:, 4 * i:4 * i + 4, :]), ps[b][:, :], ACT.Copy, t, scale=-1.0)
                pr.rel(b, t)
            meet()
            st = S(1, 8, 128)
            vn = S(4, 8, 128)
            oT = PM.rearrange("p a b -> p (a b)").rearrange("p (a b) -> p a b", b=256)
            def values(c):
                m, off = c // 2, (c % 2) * 64
                vb = []
                for i in range(2):
                    b, free = pr.take()
                    pe.wait(free)
                    for j in range(4):
                        h = 4 * i + j
                        t = mm(ps[b][off:off + 64, j * 128:j * 128 + 128], TTm[:, 2 * h + m, off:off + 64],
                               vt[:, 2 * h + m, :], j == 0, c == 0 and j == 3, inc=(j == 3), skip=True)
                    vb.append((b, t))
                return vb

            vb = values(0)
            t_st = t_q = None
            for c in range(4):
                m, off = c // 2, (c % 2) * 64
                t_vn = []
                for i in range(2):
                    b, t = vb[i]
                    if c:
                        pe.wait(t_st)
                        for j in range(4):
                            h = 4 * i + j
                            t = mm(ps[b][off:off + 64, j * 128:j * 128 + 128], KC[:, 2 * h + m, off:off + 64],
                                   st[:, h, :], False, j == 3, inc=(j == 3), skip=True)
                    t = tt(dve, vn[off:off + 64, 4 * i:4 * i + 4, :],
                           ps[b][off:off + 64, :].rearrange("p (a b) -> p a b", a=4),
                           inner(be[off:off + 64, m, 4 * i:4 * i + 4], 128), ALU.mult, t)
                    pr.rel(b, t)
                    t_vn.append(t)
                bo, free = pr.take()
                pe.wait(free)
                if c:
                    for h in range(8):
                        t_q = mm(ps[bo][:, h * 64:h * 64 + 64], st[:, h, :], qT[:, h, c * 64:c * 64 + 64], h == 0,
                                 False, inc=(h == 7), skip=True)
                if c < 3:
                    bu = []
                    for i in range(2):
                        b, free = pr.take()
                        pe.wait(free, t_vn[i])
                        for j in range(4):
                            h = 4 * i + j
                            t = mm(ps[b][:, j * 128:j * 128 + 128], ke[off:off + 64, 2 * h + m, :],
                                   vn[off:off + 64, h, :], True, True, inc=(j == 3))
                        bu.append((b, t))
                    for i, (b, t) in enumerate(bu):
                        for j in range(4):
                            h = 4 * i + j
                            u = ps[b][:, j * 128:j * 128 + 128]
                            if c == 0:
                                t1 = copy(st[:, h, :], u, t)
                            else:
                                t1 = stt(st[:, h, :], st[:, h, :], DL[:, c * 8 + h:c * 8 + h + 1], u, ALU.mult,
                                         ALU.add, t, t_q)
                        pr.rel(b, t1)
                    t_st = t1
                pe.wait(t_vn)
                for h in range(8):
                    t = mm(ps[bo][:, h * 64:h * 64 + 64], vn[off:off + 64, h, :],
                           QK[off:off + 64, 2 * h + m, off:off + 64], c == 0 and h == 0, h == 7, inc=(h == 7),
                           skip=True)
                t_o = afn(oT[:, :, c * 64:c * 64 + 64], ps[bo][:, :].rearrange("p (h i) -> p h i", h=8), ACT.Copy, t)
                pr.rel(bo, t_o)
                if c < 3:
                    vb = values(c + 1)
            mix = S(0, 8, 256)
            meet()
            t = gated_norm(oT, gate, mix, 8, cv1("odn"), t_o)
            fill(fill_rate[0])
            return out_proj(A["od_w_out"][0], mix, each=t)

        wP = sb("wP", [128, 16, 128])

        def rms_mod(src, base, gi, toks, dst, mcols=None, u=None, sq=None):
            u = S(8, 8, 256) if u is None else u
            sq = S(7, 8, 256) if sq is None else sq
            w = 0 if mcols is None else 1
            g1, rs = comb[:, 2 + w, :], rs_t[:, w, 0:256]
            sc, sh = (mods[:, base + 1, :], mods[:, base, :]) if mcols is None else (mcols[:, 1, :], mcols[:, 0, :])
            t_c = tt(dve, g1, vec[:, gi, :], sc, ALU.mult, dve.last(), t_sm)
            t = rstd(src, sq, 1e-6, toks, rs)
            for i in range(4):
                o = u[:, 2 * i:2 * i + 2, :]
                t1 = tt(dve, o, src[:, 2 * i:2 * i + 2, :], bc(rs, 2), ALU.mult, t, toks[i])
                for j in (2 * i, 2 * i + 1):
                    t2 = ts(dve, dst[:, j, :], u[:, j, :], g1[:, j:j + 1], sh[:, j:j + 1], ALU.mult, ALU.add, t1, t_c)
            return t2

        s_cx = sem("s_cx")

        def attn_layer(t_y):
            w = A["ev_w_in_2"][0]
            free = meet()
            cin = S(6, 2, 1024)
            t_cin = dma(sp, cin, A["ctx_2"][0].rearrange("(t p) n -> p t n", p=128), s_cx, *free)
            cT, hc = S(5, 8, 256), S(4, 8, 256)
            t_ct = None

            def between():
                nonlocal t_ct
                t_ct = to_features(cin, cT, t_cin, True)

            t_x = residual(6, 5, t_y, 4, 1, None, 0, False, between)
            fill_to(0)
            t_h = rms_mod(xT[:, :, :], 12, 8, t_x, hT)
            t_c = rms_mod(cT, 12, 8, [t_ct] * 4, hc, modc, cT, S(6, 8, 256))

            def flat(v):
                return v.rearrange("p a b -> p (a b)")

            q = S(0, 8, 256)
            kk = S(1, 8, 256)
            v = S(2, 4, 256)
            av, ag = S(2, 8, 256)[:, 4:6, :], S(2, 8, 256)[:, 6:8, :]
            bg = S(3, 8, 256)

            def to(dst):
                return lambda p, t: afn(flat(dst), p[:, :], ACT.Copy, t)

            proj_f(w, 0, 256, hT, to(av), t_h)
            proj_f(w, 256, 256, hT, to(ag), t_h)
            for i in range(3):
                proj_f(w, 512 + 256 * i, 256, hT, to(q[:, 2 * i:2 * i + 2, :]), t_h)
            for c0, dst in ((1280, kk), (1536, None)):
                u = cols(w, c0, 256)
                for src, o in ((hc, 0), (hT, 1)):
                    b, free = pr.take()
                    pe.wait(u.tok, free, t_h, t_c)
                    for m in range(2):
                        for k in range(8):
                            a1 = u.v[:, k, m * 128:m * 128 + 128] if dst is not None else \
                                src[:, k, m * 128:m * 128 + 128]
                            a2 = src[:, k, :] if dst is not None else u.v[:, k, :]
                            t = mm(ps[b][:, m * 256:m * 256 + 256], a1, a2, k == 0, k == 7, inc=(k == 7))
                    if dst is not None:
                        t1 = copy(flat(kk[:, 2 * o:2 * o + 2, :]), ps[b][:, :], t)
                    else:
                        t1 = copy(flat(v[:, 2 * o:2 * o + 2, :]), ps[b][:, :], t)
                    pr.rel(b, t1)
                wr.rel(u.i, t)
            for i in range(3):
                proj_f(w, 1792 + 256 * i, 256, hT, to(bg[:, 2 * i:2 * i + 2, :]), t_h)
            meet()
            sq = S(7, 8, 256)
            rn = S(6, 8, 256)
            for x, n, nm in ((q, 6, "qn"), (kk, 4, "kn")):
                t2 = head_norm(x, n, sq, rn, 1.0 / 128, dve.last(), pe.last())
                t = stt(x[:, 0:n, :], x[:, 0:n, :], cv1(nm), rn[:, 0:n, :], ALU.mult, ALU.mult, t2)
            meet()
            for x, j in [(q, j) for j in range(6)] + [(kk, 2), (kk, 3)]:
                b, free = pr.take()
                t = mm(ps[b][:, 0:256], C("rot"), x[:, j, :], True, True, free, t_c2, inc=True)
                t = tt(dve, ps[b][:, 256:512], ps[b][:, 0:256], C("sinr"), ALU.mult, t)
                t1 = tt(dve, x[:, j, :], x[:, j, :], C("cosr"), ALU.mult, t)
                t = tt(dve, x[:, j, :], x[:, j, :], ps[b][:, 256:512], ALU.add, t1)
                pr.rel(b, t)
            t = None
            kr = wP[:, 0:8, :].rearrange("p a b -> p (a b)").rearrange("p (g n) -> p g n", g=2)
            for g in range(2):
                copy(kr[:, g, 0:256], kk[:, g, :], dve.last())
                t = copy(kr[:, g, 256:512], kk[:, 2 + g, :])
            mix = S(7, 8, 256)
            meet()
            PP = [S(4, 4, 512), S(8, 4, 512)]
            PT = S(5, 2, 4, 256)
            scale = 128 ** -0.5
            t_p, r_p = {}, {}

            def scores(hp):
                P = PP[hp % 2]
                for i in range(4):
                    h, qt = 2 * hp + i // 2, i % 2
                    s0, s1, s2 = (stat[:, a, 4 * hp + i:4 * hp + i + 1] for a in range(3))
                    b, free = pr.take()
                    t = mm(ps[b][:, :], q[:, h, qt * 128:qt * 128 + 128], kr[:, h // 3, :], True, True, free,
                           inc=True)
                    t = dve.do(lambda e, b=b, s0=s0: e.tensor_reduce(s0, ps[b][:, :], AX.X, ALU.max), t)
                    t = ts(dve, s0, s0, -scale, None, ALU.mult, None, t)
                    t = afn(P[:, i, :], ps[b][:, :], ACT.Exp, t, r_p.get(hp - 2), bias=s0, scale=scale, acc=s1)
                    pr.rel(b, t)
                    t = dve.do(lambda e, s1=s1, s2=s2: e.reciprocal(s2, s1), t)
                    t_p[hp] = ts(dve, P[:, i, :], P[:, i, :], s2, None, ALU.mult, None, t)

            t_av = None

            def weigh(hp):
                nonlocal t_av
                P = PP[hp % 2]
                for i in range(2):
                    for k2 in range(2):
                        b, free = pr.take()
                        pe.wait(free, t_p[hp])
                        for kt in range(2):
                            for qt in range(2):
                                t = tr(ps[b][:, kt * 256 + qt * 128:kt * 256 + qt * 128 + 128],
                                       P[:, 2 * i + qt, (2 * k2 + kt) * 128:(2 * k2 + kt) * 128 + 128],
                                       inc=(kt == 1 and qt == 1))
                        r_p[hp] = t
                        t_c = copy(flat(PT[:, i, 2 * k2:2 * k2 + 2, :]), ps[b][:, :], t, t_av)
                        pr.rel(b, t_c)
                for i in range(2):
                    h = 2 * hp + i
                    b, free = pr.take()
                    pe.wait(free, t_c)
                    for kt in range(4):
                        t = mm(ps[b][:, 0:256], v[:, kt, (h // 3) * 128:(h // 3) * 128 + 128], PT[:, i, kt, :],
                               kt == 0, kt == 3, inc=(kt == 3))
                    t_av = t
                    t = afn(mix[:, 2 + h, :], ps[b][:, 0:256], ACT.Copy, t)
                    pr.rel(b, t)

            scores(0)
            afn(ag, ag, ACT.Silu)
            t_sl = afn(bg[:, 0:6, :], bg[:, 0:6, :], ACT.Silu)
            scores(1)
            weigh(0)
            scores(2)
            weigh(1)
            weigh(2)
            meet()
            cs = S(6, 2, 272)
            dd = S(5, 2, 256)
            t = dve.do(lambda e: e.memset(cs[:, :, 0:9], 0.0))
            for j in range(2):
                t = dve.do(lambda e, j=j: e.tensor_tensor_scan(cs[:, j, 9:265], ones[:, 0:1].broadcast_to([128, 256]),
                                                               av[:, j, :], 0.0, ALU.mult, ALU.add), t)
            for j in range(2):
                t = copy(cs[:, j, 265:272], cs[:, j, 264:265].broadcast_to([128, 7]), t)
            for g, wd in enumerate((2, 4, 8, 16)):
                j, po, hw = g // 2, (g % 2) * 64, wd // 2
                t1 = tt(dve, dd[po:po + 64, j, :], cs[po:po + 64, j, 8 + hw:264 + hw],
                        cs[po:po + 64, j, 8 - hw:264 - hw], ALU.subtract, t)
            t1 = tt(dve, flat(dd), flat(dd), C("icnt"), ALU.mult, t1)
            t1 = tt(dve, dd, dd, av, ALU.subtract, t1)
            b, free = pr.take()
            pe.wait(free, t1)
            t = None
            for g in (0, 2, 1, 3):
                j, po = g // 2, (g % 2) * 64
                t = mm(ps[b][po:po + 64, j * 256:j * 256 + 256], poolw[po:po + 64, j, :], dd[po:po + 64, j, :],
                       True, True, t if g == 1 else None, inc=(g >= 2))
            for j in range(2):
                t1 = ts(dve, mix[:, j, :], ps[b][:, j * 256:j * 256 + 256], cv1("psc", j), None, ALU.mult, None, t)
            pr.rel(b, t1)
            each = [tt(dve, mix[:, 0:2, :], mix[:, 0:2, :], ag, ALU.mult, t_sl, t1)]
            each += [tt(dve, mix[:, 2 + i:4 + i, :], mix[:, 2 + i:4 + i, :], bg[:, i:i + 2, :], ALU.mult, t_sl)
                     for i in (0, 2, 4)]
            hidden = hidden_1()

            def between():
                nonlocal hidden
                hidden = (hidden_2(hidden[0]),) + hidden[1:]

            t_y = out_proj(A["ev_w_out_2"][0], mix, between=between, each=each)
            for j in range(8):
                t = stt(xT[:, j, :], Y(j), mc(12, 2, j), xT[:, j, :], ALU.mult, ALU.add, t_y)
            give_y(t)
            return t, hidden

        raw3 = misc[:, 0:2 * 516].rearrange("p (r m n) -> p r m n", r=2, m=2)
        s_w3 = sem("s_hw3")
        hd = misc[0:64, 0:1536].rearrange("p (a n) -> p a n", a=6)
        nrm = sb("nrm", [128, 2, 12])

        def sin_layer(dst, src, bi, tok):
            x, k = hd[:, 4, :], hd[:, 5, :]
            fr = colv[0:64, 2, 2:3]
            t = ts(dve, x, src, colv[0:64, 2, bi:bi + 1], fr, ALU.add, ALU.mult, tok, t_cols)
            big = 12582912.0
            t = ts(dve, k, x, 1.0 / (2 * math.pi), big, ALU.mult, ALU.add, t)
            t = ts(dve, k, k, big, None, ALU.subtract, None, t)
            c1 = 6.28125
            c2 = float(np.float32(2 * math.pi - c1))
            t = stt(x, k, -c1, x, ALU.mult, ALU.add, t)
            t = stt(x, k, -c2, x, ALU.mult, ALU.add, t)
            pi = 3.1415925
            t = ts(dve, x, x, pi, -pi, ALU.min, ALU.max, t)
            return afn(dst, x, ACT.Sin, t)

        def hidden_1():
            fr = [q.last() for q in (pe, act, dve)]
            w3 = wP[0:64, :, :].rearrange("p a b -> p (a b)")
            w3b = kc_x[0:64, :, :].rearrange("p a b -> p (a b)")
            dma(pool, w3, A["hy_w3_2"][0][:, 0:2048], s_w3, *fr)
            t_w3 = dma(pool, w3b, A["hy_w3_2"][0][:, 2048:3072], s_w3, *fr)
            b, free = pr.take()
            t = mm(ps[b][0:64, 0:256], hw12[0:33, 0, :], C("emb")[0:33, :], True, True, free, t_c2, inc=True)
            t = sin_layer(hd[:, 0, :], ps[b][0:64, 0:256], 0, t)
            pr.rel(b, t)
            return t, w3, w3b, t_w3

        def hidden_2(t):
            b, free = pr.take()
            t = mm(ps[b][0:64, 0:256], hw12[:, 1, :], hd[:, 0, :], True, True, free, t, inc=True)
            t = sin_layer(hd[:, 1, :], ps[b][0:64, 0:256], 1, t)
            pr.rel(b, t)
            return t

        def hyena_layer(t_x, hidden):
            w = A["od_w_in_2"][0]

            def flat(v):
                return v.rearrange("p a b -> p (a b)")

            meet()
            t, w3, w3b, t_w3 = hidden
            hs, hdif = [S(0, 1536), S(1, 1536)], [S(2, 1536), S(3, 1536)]
            fas, fbs = [S(7, 1536), S(4, 1536)], [S(8, 1536), S(5, 1536)]
            dec = C("dec")
            pe.wait(t, t_w3)
            wi, wfree = wr.take()
            ab = [wplace(wi)[:, 0:1536], S(6, 1536)]
            act.wait(wfree)
            t_ab = t_add = None
            first = True
            for m in range(2):
                fa, fb = fas[m], fbs[m]
                tf = [None, None]
                for dr in range(2):
                    for o in range(2):
                        dst = (fa if dr == 0 else fb)[:, o * 768:o * 768 + 768]
                        for hf in range(2):
                            c0 = o * 1536 + dr * 768 + hf * 384
                            b, free = pr.take()
                            pe.wait(free)
                            lhs = hd[:, 1, m * 128:m * 128 + 128]
                            parts = [(c0, c0 + 384)] if c0 + 384 <= 2048 or c0 >= 2048 else \
                                [(c0, 2048), (2048, c0 + 384)]
                            for (a0, a1) in parts:
                                rhs = w3[:, a0:a1] if a1 <= 2048 else w3b[:, a0 - 2048:a1 - 2048]
                                t = mm(ps[b][:, a0 - c0:a1 - c0], lhs, rhs, True, True, inc=True)
                            t = tt(dve, dst[:, hf * 384:hf * 384 + 384], ps[b][:, 0:384],
                                   dec[:, m * 768 + hf * 384:m * 768 + hf * 384 + 384], ALU.mult, t, t_c2)
                            pr.rel(b, t)
                    tf[dr] = t
                for f, x in enumerate((fa, fb)):
                    t_ab = afn(ab[0 if first else 1], x, ACT.Abs, tf[f], t_add)
                    if not first:
                        t_add = tt(pool, ab[0], ab[0], ab[1], ALU.add, t_ab)
                    first = False
                if m == 0:
                    t = dve.do(lambda e, fb=fb: e.memset(fb[0:1, :], 0.0), t_ab)
                tt(dve, hs[m], fa, fb, ALU.add, t)
                t = tt(dve, hdif[m], fa, fb, ALU.subtract, t)
                if m == 0:
                    t_h = rms_mod(xT[:, :, :], 15, 9, [t_x] * 4, hT, None, hT, hT)
            t_d = t
            KR = [S(4, 1536), S(5, 1536)]
            KI = [S(6, 1536), S(7, 1536)]
            DC = C("dc").rearrange("p (a b) -> p a b", a=2)
            DS = C("ds").rearrange("p (a b) -> p a b", a=2)
            for f in range(2):
                for mat, src, dst, sc in ((DC, hs, KR, 1.0), (DS, hdif, KI, -1.0)):
                    for c in range(3):
                        b, free = pr.take()
                        pe.wait(free, t_d)
                        for m in range(2):
                            t = mm(ps[b][:, :], mat[:, m, f * 128:f * 128 + 128], src[m][:, c * 512:c * 512 + 512],
                                   m == 0, m == 1, inc=(m == 1))
                        t = afn(dst[f][:, c * 512:c * 512 + 512], ps[b][:, :], ACT.Copy, t, t_d, t_add, scale=sc)
                        pr.rel(b, t)
            nb, nfree = pr.take()
            pe.wait(nfree, t_add)
            for g in range(12):
                t = mm(ps[nb][:, g:g + 1], ab[0][:, g * 128:g * 128 + 128], one_c, True, True, inc=(g == 11))
            wr.rel(wi, t)
            t = ts(dve, nrm[:, 0, :], ps[nb][:, 0:12], 1e-6, None, ALU.add, None, t)
            t = dve.do(lambda e: e.reciprocal(nrm[:, 1, :], nrm[:, 0, :]), t)
            pr.rel(nb, t)
            meet()
            t_r3 = pool.do(lambda e: e.memset(misc[:, 0:1032], 0.0))
            z = S(0, 8, 256)
            x1, x2 = S(1, 8, 256), S(2, 8, 256)
            gt = S(3, 8, 256)
            r3 = Ring(range(2))

            def conv3(dst, j0):
                def ev(p, t):
                    r, free = r3.take()
                    t = afn(raw3[:, r, :, 1:257], p[:, :].rearrange("p (m n) -> p m n", m=2), ACT.Copy, t, t_r3,
                            free)
                    for m in range(2):
                        x = raw3[:, r, m, :]
                        j = j0 + m
                        t1 = ts(dve, dst[:, m, :], x[:, 0:256], cv1("hcw", j), cv1("hcb", j), ALU.mult, ALU.add,
                                t)
                        for k in (1, 2):
                            t1 = stt(dst[:, m, :], x[:, k:k + 256], cv1("hcw", k * 18 + j), dst[:, m, :],
                                     ALU.mult, ALU.add, t1)
                    r3.rel(r, t1)
                    return t
                return ev

            for s, dst in ((0, z), (1, x1), (2, x2)):
                for i in range(3):
                    proj_f(w, s * 768 + 256 * i, 256, hT, conv3(dst[:, 2 * i:2 * i + 2, :], s * 6 + 2 * i), t_h)
            for i in range(3):
                g = gt[:, 2 * i:2 * i + 2, :]
                proj_f(w, 2304 + 256 * i, 256, hT,
                       lambda p, t, g=g: afn(g, p[:, :].rearrange("p (m n) -> p m n", m=2), ACT.Silu, t), t_h)
            fin = z[:, 6:8, :]
            proj_f(w, 3072, 256, hT, lambda p, t: copy(flat(fin), p[:, :], t), t_h)
            g = gt[:, 6:8, :]
            proj_f(w, 3328, 256, hT, lambda p, t: afn(flat(g), p[:, :], ACT.Silu, t), t_h)
            meet()
            CT = C("dct").rearrange("p (a b) -> p a b", a=2)
            ST = C("dst").rearrange("p (a b) -> p a b", a=2)
            zt = wP[:, 0:12, :].rearrange("p a b -> p (a b)").rearrange("p (m n) -> p m n", m=2)
            wi, wfree = wr.take()
            act.wait(wfree)
            ZZ = [S(8, 2048), wplace(wi)]
            tmp = kc_x[:, :, :].rearrange("p a b -> p (a b)")[:, 0:768]
            tmp2 = rs_t[:, :, :].rearrange("p a b -> p (a b)")[:, 0:768]
            t2r = misc[:, 1536:2048].rearrange("p (a b) -> p a b", a=2)
            YR = [hT[:, :, :].rearrange("p a b -> p (a b)")[:, 0:768],
                  hT[:, :, :].rearrange("p a b -> p (a b)")[:, 768:1536]]
            YI = [yib[:, 0, :], yib[:, 1, :]]
            t_z = [None] * 6
            t_zt = t_inv = None
            t_pr = [None, None]
            t_r = [None, None]
            t_l1 = t_l2 = None
            for o in range(2):
                for j in range(6):
                    b, free = pr.take()
                    pe.wait(free, t_z[j])
                    for m in range(2):
                        t = tr(ps[b][:, m * 128:m * 128 + 128], z[:, j, m * 128:m * 128 + 128], inc=(m == 1))
                    t = copy(zt[:, :, j * 128:j * 128 + 128], ps[b][:, 0:256].rearrange("p (m n) -> p m n", m=2), t,
                             t_zt)
                    pr.rel(b, t)
                pe.wait(t)
                for f in range(2):
                    ZR, ZI = ZZ[f][:, 0:768], ZZ[f][:, 768:1536]
                    for mat, dst, sc in ((DC, ZR, 1.0), (DS, ZI, -1.0)):
                        for c in range(2):
                            b, free = pr.take()
                            pe.wait(free)
                            for m in range(2):
                                t = mm(ps[b][:, 0:384], mat[:, m, f * 128:f * 128 + 128],
                                       zt[:, m, c * 384:c * 384 + 384], m == 0, m == 1, inc=(m == 1))
                            t_zt = t
                            t = afn(dst[:, c * 384:c * 384 + 384], ps[b][:, 0:384], ACT.Copy, t, t_pr[f], scale=sc)
                            pr.rel(b, t)
                    kr, ki = KR[f][:, o * 768:o * 768 + 768], KI[f][:, o * 768:o * 768 + 768]
                    t_zf = t
                    t = tt(dve, YR[f], ZR, kr, ALU.mult, t_zf, t_inv)
                    t = tt(dve, tmp, ZI, ki, ALU.mult, t_zf, t_l1)
                    t1 = tt(dve, YR[f], YR[f], tmp, ALU.subtract, t)
                    t = tt(pool, YI[f], ZR, ki, ALU.mult, t_zf, t_inv)
                    t = tt(pool, tmp2, ZI, kr, ALU.mult, t_zf, t_l2)
                    t2 = tt(pool, YI[f], YI[f], tmp2, ALU.add, t)
                    t_l1, t_l2 = t1, t2
                    t_pr[f] = [t1, t2]
                gx = x1 if o == 0 else x2
                bs = [pr.take() for _ in range(6)]
                for f in range(2):
                    pe.wait(t_pr[f])
                    for j in range(6):
                        b, free = bs[j]
                        if f == 0:
                            pe.wait(free)
                        mm(ps[b][:, 0:256], YR[f][:, j * 128:j * 128 + 128], CT[:, f, :], f == 0, False)
                        t = mm(ps[b][:, 0:256], YI[f][:, j * 128:j * 128 + 128], ST[:, f, :], False, f == 1,
                               inc=(f == 1))
                        if f == 1:
                            r = t2r[:, j % 2, :]
                            t_inv = t
                            t = afn(r, ps[b][:, 0:256], ACT.Copy, t, t_r[j % 2],
                                    scale=nrm[:, 1, o * 6 + j:o * 6 + j + 1])
                            pr.rel(b, t)
                            t = stt(z[:, j, :], z[:, j, :], cv1("skip", o * 6 + j), r, ALU.mult, ALU.add, t)
                            t_r[j % 2] = t
                            t_z[j] = tt(dve, z[:, j, :], z[:, j, :], gx[:, j, :], ALU.mult, t)
            wr.rel(wi, *t_pr[1])
            meet()
            t_g = tt(dve, z[:, 0:6, :], z[:, 0:6, :], gt[:, 0:6, :], ALU.mult)
            FC = C("fc").rearrange("p (a b) -> p a b", a=2)
            FS = C("fs").rearrange("p (a b) -> p a b", a=2)
            PQ = S(1, 8, 256)
            for m in range(2):
                for q, mat in ((0, FC), (1, FS)):
                    b, free = pr.take()
                    pe.wait(free)
                    for c in range(2):
                        t = mm(ps[b][:, 0:256], fin[:, c, m * 128:m * 128 + 128], mat[:, c, :], c == 0, c == 1,
                               inc=(c == 1))
                    t = afn(PQ[:, 2 * q + m, :], ps[b][:, 0:256], ACT.Copy, t, scale=1.0 if q == 0 else -1.0)
                    pr.rel(b, t)
            yt = S(2, 8, 256)
            pe.wait(t)
            for j in range(2):
                b, free = pr.take()
                pe.wait(free)
                n = 0
                for q, mat in ((0, FC), (1, FS)):
                    for m in range(2):
                        t = mm(ps[b][:, 0:256], PQ[:, 2 * q + m, j * 128:j * 128 + 128], mat[:, m, :], n == 0,
                               n == 3, inc=(n == 3))
                        n += 1
                t = afn(yt[:, j, :], ps[b][:, 0:256], ACT.Copy, t, scale=1.0 / 256)
                pr.rel(b, t)
            u = unit(A["fn_w_2"][0].rearrange("(k p) n -> p k n", p=128), 2, 256)
            for j in range(2):
                b, free = pr.take()
                pe.wait(free, u.tok, act.last())
                for c in range(2):
                    t = mm(ps[b][:, 0:256], u.v[:, c, j * 128:j * 128 + 128], yt[:, c, :], c == 0, c == 1,
                           inc=(c == 1))
                t1 = tt(dve, z[:, 6 + j, :], ps[b][:, 0:256], gt[:, 6 + j, :], ALU.mult, t)
                pr.rel(b, t1)
            wr.rel(u.i, t)
            t_y = out_proj(A["od_w_out_2"][0], z, each=[t_g, t_g, t_g, t1])
            for j in range(8):
                t = stt(xT[:, j, :], Y(j), mc(15, 2, j), xT[:, j, :], ALU.mult, ALU.add, t_y)
            give_y(t)
            return t

        yib = misc[:, 0:1536].rearrange("p (a n) -> p a n", a=2)

        def whole():
            t_m = fill_to(36 - 4)
            t_h = scale_shift(hT, xT, lambda j: mc(0, 1, j), lambda j: mc(0, 0, j), t_m, t_x)
            t_x0 = ts(dve, xT[:, :, :], xT[:, :, :], ALPHA, None, ALU.mult, None, t_h)
            small_columns()
            fill_rate[0] = R0
            t_y = even_mixer(t_h)
            fill_rate[0] = 0
            t_h = residual(0, 2, t_y, 0, 0, 0, 3)
            t_y = moe(0, t_h)
            fill_to(14)
            t_h = residual(0, 5, t_y, 4, 0, 6, 0)
            fill_rate[0] = R1
            t_y = delta_mixer(t_h)
            fill_rate[0] = 0
            t_h = residual(6, 2, t_y, 0, 1, 6, 3)
            t_y = moe(1, t_h)
            t_xx = attn_layer(t_y)
            t_xx, hidden = t_xx
            return hyena_layer(t_xx, hidden)

        t_end = whole()
        meet()
        u, sq = S(8, 8, 256), S(7, 8, 256)
        t = rstd(xT, sq, 1e-6, [t_end] * 4)
        for i in range(4):
            o = u[:, 2 * i:2 * i + 2, :]
            t1 = tt(dve, o, xT[:, 2 * i:2 * i + 2, :], bc(rs_t[:, 0, 0:256], 2), ALU.mult, t)
            for j in (2 * i, 2 * i + 1):
                t2 = ts(dve, u[:, j, :], u[:, j, :], vc(10, j), None, ALU.mult, None, t1, t_sm)
        t = t2
        xo = S(6, 2, 1024)
        for m in range(2):
            for k2 in range(2):
                b, free = pr.take()
                pe.wait(free, t)
                for kk in range(4):
                    tp = tr(ps[b][:, kk * 128:kk * 128 + 128], u[:, 4 * k2 + kk, m * 128:m * 128 + 128],
                            inc=(kk == 3))
                o = xo[:, m, :].rearrange("p (f k) -> p k f", k=8)[:, 4 * k2:4 * k2 + 4, :]
                t1 = copy(o, ps[b][:, :].rearrange("p (k f) -> p k f", k=4), tp)
                pr.rel(b, t1)
        s_out = sem("s_out")
        t = dma(sp, out[0].rearrange("(t p) n -> p t n", p=128), xo, s_out, t1)
        sp.wait(t)

        block = ctx.enter_context(nc.Block())

        @block.sync
        def _(e):
            sp.emit(e)

        @block.gpsimd
        def _(e):
            pool.emit(e)

        @block.scalar
        def _(e):
            act.emit(e)

        @block.vector
        def _(e):
            dve.emit(e)

        @block.tensor
        def _(e):
            pe.emit(e)


def kernel(**inputs):
    import numpy as _np
    import concourse.bacc as _bacc
    from concourse import mybir as _mybir
    from concourse.bass_utils import run_bass_kernel_spmd as _run

    nc = _bacc.Bacc("TRN2", target_bir_lowering=False, num_devices=1)
    consts, at, lo = shape_constants()
    arrays, args = {}, {}
    for name, a in list(inputs.items()) + [("consts", consts)]:
        a = _np.ascontiguousarray(a)
        arrays[f"in_{name}"] = a
        args[name] = nc.dram_tensor(f"in_{name}", a.shape, _mybir.dt.from_np(a.dtype), kind="ExternalInput").ap()
    o = nc.dram_tensor("out_0", (1, 256, 1024), _mybir.dt.float32, kind="ExternalOutput").ap()
    build(nc, args, o, at, lo)
    r = _run(nc, [arrays], core_ids=[0])
    return r.results[0]["out_0"]
```
